# Optimizing a Trainium2 kernel written in Bass

```python
import jax, jax.numpy as jnp
from jax import lax
import numpy as np

D_MODEL = 1024
BATCH = 1
SEQ = 1024
DEPTH = 1

MLA_HEADS = 8
MLA_Q_RANK = 384
MLA_KV_RANK = 256
MLA_NOPE = 128
MLA_ROPE = 64
MLA_V = 128
MLA_WIDTH = MLA_HEADS * MLA_V
RET_HEADS = 4
RET_QK = 256
RET_V = 512
RET_WIDTH = RET_HEADS * RET_V
RET_CHUNK = 128
ATTN_BLOCK = 128
ROPE_THETA = 10000.0
EPS = 1e-6
IN_SIZES = (MLA_Q_RANK, MLA_KV_RANK, MLA_ROPE, MLA_WIDTH,
            RET_HEADS * RET_QK, RET_HEADS * RET_QK, RET_WIDTH, RET_WIDTH,
            D_MODEL, D_MODEL)
IN_TOTAL = 384 + 256 + 64 + 1024 + 1024 + 1024 + 2048 + 2048 + 1024 + 1024

kernel_name = "hybrid_mla_retention_gated_block"

def _split_points():
    pts, acc = [], 0
    for s in IN_SIZES[:-1]:
        acc += s
        pts.append(acc)
    return pts

def rmsnorm(x, g):
    xf = x.astype(jnp.float32)
    r = xf * lax.rsqrt(jnp.mean(xf * xf, axis=-1, keepdims=True) + EPS)
    return (r * g.astype(jnp.float32)).astype(x.dtype)

def rotary(x, positions):
    d = x.shape[-1]
    inv_freq = ROPE_THETA ** (-jnp.arange(0, d, 2, dtype=jnp.float32) / d)
    ang = positions.astype(jnp.float32)[..., None] * inv_freq
    cos = jnp.cos(ang)[:, :, None, :]
    sin = jnp.sin(ang)[:, :, None, :]
    xf = x.astype(jnp.float32)
    x1, x2 = xf[..., : d // 2], xf[..., d // 2:]
    out = jnp.concatenate([x1 * cos - x2 * sin, x2 * cos + x1 * sin], axis=-1)
    return out.astype(x.dtype)

def causal_block_attention(q, k, v):
    B, S, H, Dh = q.shape
    nb = S // ATTN_BLOCK
    scale = Dh ** -0.5
    qb = q.reshape(B, nb, ATTN_BLOCK, H, Dh).transpose(1, 0, 3, 2, 4)
    k_idx = jnp.arange(S)

    def one_block(args):
        qi, i = args
        s = jnp.einsum('bhqd,bkhd->bhqk', qi, k, preferred_element_type=jnp.float32) * scale
        q_idx = i * ATTN_BLOCK + jnp.arange(ATTN_BLOCK)
        mask = k_idx[None, :] <= q_idx[:, None]
        s = jnp.where(mask[None, None], s, -1e30)
        p = jax.nn.softmax(s, axis=-1).astype(v.dtype)
        return jnp.einsum('bhqk,bkhd->bqhd', p, v)

    out = lax.map(one_block, (qb, jnp.arange(nb)))
    return out.transpose(1, 0, 2, 3, 4).reshape(B, S, H, v.shape[-1])

def mla_branch(c_q, c_kv, k_pe, positions, g_q, w_q_up, g_kv, w_kv_up):
    B, S, _ = c_q.shape
    q = (rmsnorm(c_q, g_q) @ w_q_up).reshape(B, S, MLA_HEADS, MLA_NOPE + MLA_ROPE)
    q = jnp.concatenate([q[..., :MLA_NOPE], rotary(q[..., MLA_NOPE:], positions)], axis=-1)
    kv = (rmsnorm(c_kv, g_kv) @ w_kv_up).reshape(B, S, MLA_HEADS, MLA_NOPE + MLA_V)
    k_nope, v = kv[..., :MLA_NOPE], kv[..., MLA_NOPE:]
    k_rope = rotary(k_pe[:, :, None, :], positions)
    k = jnp.concatenate([k_nope, jnp.broadcast_to(k_rope, (B, S, MLA_HEADS, MLA_ROPE))], axis=-1)
    return causal_block_attention(q, k, v).reshape(B, S, MLA_WIDTH)

def retention_branch(q, k, v, positions, g_ret):
    B, S, _ = q.shape
    H, C = RET_HEADS, RET_CHUNK
    n = S // C
    q = rotary(q.reshape(B, S, H, RET_QK), positions)
    k = rotary(k.reshape(B, S, H, RET_QK), positions) * (RET_QK ** -0.5)
    v = v.reshape(B, S, H, RET_V)
    log_gamma = jnp.log1p(-jnp.exp2(-5.0 - jnp.arange(H, dtype=jnp.float32)))
    idx = jnp.arange(C, dtype=jnp.float32)
    diff = idx[:, None] - idx[None, :]
    decay_in = jnp.where(diff >= 0, jnp.exp(log_gamma[:, None, None] * jnp.maximum(diff, 0.0)), 0.0)
    xi = jnp.exp(log_gamma[:, None] * (idx + 1.0))
    zeta = jnp.exp(log_gamma[:, None] * (C - 1.0 - idx))
    gamma_c = jnp.exp(log_gamma * C)

    def to_chunks(t):
        return t.reshape(B, n, C, H, t.shape[-1]).transpose(1, 0, 3, 2, 4).astype(jnp.float32)

    def step(R, chunk):
        qc, kc, vc = chunk
        inner = jnp.einsum('bhqk,bhkd->bhqd', jnp.einsum('bhqd,bhkd->bhqk', qc, kc) * decay_in[None], vc)
        cross = jnp.einsum('bhqd,bhde->bhqe', qc, R) * xi[None, :, :, None]
        R = R * gamma_c[None, :, None, None] + jnp.einsum('bhkd,bhke->bhde', kc * zeta[None, :, :, None], vc)
        return R, inner + cross

    R0 = jnp.zeros((B, H, RET_QK, RET_V), jnp.float32)
    _, out = lax.scan(step, R0, (to_chunks(q), to_chunks(k), to_chunks(v)))
    out = out.transpose(1, 0, 3, 2, 4).reshape(B, S, H, RET_V)
    mu = jnp.mean(out, axis=-1, keepdims=True)
    var = jnp.mean(jnp.square(out - mu), axis=-1, keepdims=True)
    out = ((out - mu) * lax.rsqrt(var + EPS)).reshape(B, S, RET_WIDTH) * g_ret.astype(jnp.float32)
    return out.astype(q.dtype)

def setup_inputs(seed: int = 0) -> dict:
    key = jax.random.key(seed)
    ks = jax.random.split(key, 17)
    f32 = jnp.float32

    def w(k, shape, fan_in):
        return jax.random.normal(k, shape, f32) * (fan_in ** -0.5)

    def gain(k, shape):
        return 1.0 + 0.02 * jax.random.normal(k, shape, f32)

    x = jax.random.normal(ks[0], (BATCH, SEQ, D_MODEL), f32)
    c = jax.random.normal(ks[1], (BATCH, D_MODEL), f32)
    positions = (jnp.arange(SEQ, dtype=jnp.int32)[None, :]
                 + jax.random.randint(ks[2], (BATCH, 1), 0, 1024, dtype=jnp.int32))
    return {
        "x": x,
        "c": c,
        "positions": positions,
        "w_ada": w(ks[3], (DEPTH, D_MODEL, 3 * D_MODEL), D_MODEL),
        "b_ada": 0.02 * jax.random.normal(ks[4], (DEPTH, 3 * D_MODEL), f32),
        "g_pre": gain(ks[5], (DEPTH, D_MODEL)),
        "w_in": w(ks[6], (DEPTH, D_MODEL, IN_TOTAL), D_MODEL),
        "g_q": gain(ks[7], (DEPTH, MLA_Q_RANK)),
        "w_q_up": w(ks[8], (DEPTH, MLA_Q_RANK, MLA_HEADS * (MLA_NOPE + MLA_ROPE)), MLA_Q_RANK),
        "g_kv": gain(ks[9], (DEPTH, MLA_KV_RANK)),
        "w_kv_up": w(ks[10], (DEPTH, MLA_KV_RANK, MLA_HEADS * (MLA_NOPE + MLA_V)), MLA_KV_RANK),
        "g_ret": gain(ks[11], (DEPTH, RET_WIDTH)),
        "w_proj_mla": w(ks[12], (DEPTH, MLA_WIDTH, D_MODEL), MLA_WIDTH),
        "w_proj_ret": w(ks[13], (DEPTH, RET_WIDTH, D_MODEL), RET_WIDTH),
        "w_out": w(ks[14], (DEPTH, D_MODEL, D_MODEL), D_MODEL),
        "g_final": gain(ks[15], (D_MODEL,)),
    }

def reference(x, c, positions, w_ada, b_ada, g_pre, w_in, g_q, w_q_up, g_kv, w_kv_up,
              g_ret, w_proj_mla, w_proj_ret, w_out, g_final):
    pts = _split_points()
    for l in range(DEPTH):
        mod = jax.nn.silu(c) @ w_ada[l] + b_ada[l]
        shift, scale, gate = jnp.split(mod[:, None, :], 3, axis=-1)
        h = rmsnorm(x, g_pre[l]) * (1.0 + scale) + shift
        proj = h @ w_in[l]
        (c_q, c_kv, k_pe, gate_mla, q_ret, k_ret, v_ret, gate_ret,
         merge_mla, merge_ret) = jnp.split(proj, pts, axis=-1)
        y_mla = mla_branch(c_q, c_kv, k_pe, positions, g_q[l], w_q_up[l], g_kv[l], w_kv_up[l])
        y_mla = y_mla * jax.nn.silu(gate_mla)
        y_ret = retention_branch(q_ret, k_ret, v_ret, positions, g_ret[l]) * jax.nn.silu(gate_ret)
        merged = (jax.nn.sigmoid(merge_mla) * (y_mla @ w_proj_mla[l])
                  + jax.nn.sigmoid(merge_ret) * (y_ret @ w_proj_ret[l]))
        x = x + gate * (merged @ w_out[l])
    return rmsnorm(x, g_final)


_drawn_inputs = setup_inputs


def setup_inputs(seed=0):
    import zlib

    import numpy as np

    out = dict(_drawn_inputs(seed))
    spreads = {}
    factors = {'b_ada': 2.751, 'g_pre': 4.631, 'g_q': 8.0, 'g_kv': 8.0, 'g_ret': 8.0, 'g_final': 2.849}
    for name, (base, spread) in spreads.items():
        noise = np.random.default_rng([zlib.crc32(name.encode()), seed]).standard_normal(out[name].shape)
        drawn = base * np.exp(spread * noise) if base else spread * noise
        out[name] = __import__('jax').numpy.asarray(drawn.astype(out[name].dtype))
    for name, factor in factors.items():
        out[name] = (out[name] * factor).astype(out[name].dtype)
    return out
```

```python
from contextlib import ExitStack

import numpy as np
import concourse.bass as bass
from concourse import mybir

F32 = mybir.dt.float32
F32R = mybir.dt.float32r
I32 = mybir.dt.int32
ALU = mybir.AluOpType
ACT = mybir.ActivationFunctionType
AX = mybir.AxisListType

P = 128
S = 1024
D = 1024
KD = D // P
NT = S // P
HALF = 512
EPS = 1e-6
Q_RANK, KV_RANK, ROPE = 384, 256, 64
KQ, KKV = Q_RANK // P, KV_RANK // P
H_MLA, NOPE, V_MLA = 8, 128, 128
SCALE = float(NOPE + ROPE) ** -0.5
H_RET, RET_QK, RET_V = 4, 256, 512
GATE_MLA, Q_RET, K_RET, GATE_RET, MERGE_MLA, MERGE_RET = 0, 8, 16, 24, 40, 48
ACT_TILES = 56
MASKED = -1e30
TURN_1 = 6.28125
TURN_2 = float(np.float32(2 * np.pi - TURN_1))
TURN_3 = float(2 * np.pi - TURN_1 - TURN_2)
ROUNDER = 12582912.0
PI_BELOW = 3.1415925
COL_C, COL_BADA, COL_GPRE, COL_GQ, COL_GKV, COL_GRET = 0, 8, 24, 32, 35, 37
N_COLS = 53
CC_FREQ_RET, CC_FREQ_MLA, CC_SIGN, CC_HALF_PI, CC_EPS = 0, 1, 2, 3, 4


def one(ap, i):
    return ap[bass.ds(i, 1)]


class ProductSemaphores:

    def __init__(self, sem):
        self.loaded = sem("product_w_loaded")
        self.hi_ready = sem("product_w_hi_ready")
        self.lo_ready = sem("product_w_lo_ready")
        self.slot_free = sem("product_w_slot_free")
        self.summed = sem("product_tile_summed")
        self.psum_free = sem("product_psum_free")
        self.stage_free = [sem("product_stage_even_free"), sem("product_stage_odd_free")]
        self.base = dict.fromkeys(("loaded", "hi", "lo", "slot", "summed", "psum", "stage"), 0)

    def past(self, **counts):
        for key, count in counts.items():
            self.base[key] += count


def transposed_product(nc, sems, weights, x_hi, x_lo, raw, w_hi, w_lo, psum, segments,
                       stage=None, dst=None, keep=None):
    groups, _, k_tiles, cols = weights.shape
    per = cols // P
    loaded, hi_ready, lo_ready, slot_free = sems.loaded, sems.hi_ready, sems.lo_ready, sems.slot_free
    summed, psum_free, stage_free = sems.summed, sems.psum_free, sems.stage_free
    base = dict(sems.base)
    with nc.Block() as block:
        @block.sync
        def _(sp):
            def load(g):
                sp.dma_start(raw[:, 0:k_tiles, 0:cols],
                             one(weights, g).rearrange("a p k n -> p (a k) n")).then_inc(loaded, 16)

            def store(g):
                if dst is None:
                    return
                for j in range(per):
                    sp.wait_ge(psum_free, g * per + (per + j + 1 + base["psum"]))
                    sp.dma_start(one(dst, g * per + j).rearrange("a p n -> p (a n)"),
                                 stage[:, j % 2, :]).then_inc(stage_free[j % 2], 16)

            if dst is not None:
                for free in stage_free:
                    sp.sem_inc(free, 16)
            load(0)
            with sp.Fori(0, groups - 1) as g:
                sp.wait_ge(lo_ready, g * per + (per + base["lo"]))
                load(g + 1)
                store(g)
            store(groups - 1)
            if dst is not None:
                for free in stage_free:
                    sp.wait_ge(free, 16 + 8 * groups * per + base["stage"])

        @block.scalar
        def _(act):
            def split(g, j):
                if j == 0:
                    act.wait_ge(loaded, g * 16 + 16 + base["loaded"])
                nc.scalar.activation(w_hi[:, 0:k_tiles, j * P:(j + 1) * P], raw[:, 0:k_tiles, j * P:(j + 1) * P],
                                     ACT.Copy).then_inc(hi_ready, 1)

            def evacuate(g, j, func):
                act.wait_ge(summed, g * per + (j + 1) + base["summed"])
                if keep is None:
                    act.wait_ge(stage_free[j % 2], g * (8 * per) + 16 * (j // 2 + 1) + base["stage"])
                    out = stage[:, j % 2, :]
                else:
                    out = keep[:, bass.ds(g * per + j, 1), :].rearrange("p a n -> p (a n)")
                nc.scalar.activation(out, psum[:, j, :], func).then_inc(psum_free, 1)

            act.sem_inc(psum_free, per)
            for j in range(per):
                split(0, j)
            first = 0
            for count, func in segments:
                last = first + count
                looped = min(last, groups - 1)
                if looped > first:
                    with act.Fori(first, looped) as g:
                        for j in range(per):
                            evacuate(g, j, func)
                            split(g + 1, j)
                if last == groups:
                    for j in range(per):
                        evacuate(groups - 1, j, func)
                first = last

        @block.vector
        def _(dve):
            with dve.Fori(0, groups) as g:
                for j in range(per):
                    dve.wait_ge(hi_ready, g * per + (j + 1) + base["hi"])
                    nc.vector.tensor_tensor(w_lo[:, 0:k_tiles, j * P:(j + 1) * P],
                                            raw[:, 0:k_tiles, j * P:(j + 1) * P],
                                            w_hi[:, 0:k_tiles, j * P:(j + 1) * P].bitcast(F32),
                                            ALU.subtract).then_inc(lo_ready, 1)

        @block.tensor
        def _(pe):
            with pe.Fori(0, groups) as g:
                for j in range(per):
                    cut = slice(j * P, (j + 1) * P)
                    pe.wait_ge(lo_ready, g * per + (j + 1) + base["lo"])
                    pe.wait_ge(psum_free, g * per + (j + 1) + base["psum"])
                    for half in range(2):
                        out = psum[:, j, half * HALF:(half + 1) * HALF]
                        tok = slice(half * HALF, (half + 1) * HALF)
                        for k in range(k_tiles):
                            nc.tensor.matmul(out, w_hi[:, k, cut], x_hi[:, k, tok], start=(k == 0), stop=False)
                            nc.tensor.matmul(out, w_hi[:, k, cut], x_lo[:, k, tok], start=False, stop=False)
                            last = nc.tensor.matmul(out, w_lo[:, k, cut], x_hi[:, k, tok],
                                                    start=False, stop=(k == k_tiles - 1))
                    last.then_inc(summed, 1)
    tiles = groups * per
    sems.past(loaded=16 * groups, hi=tiles, lo=tiles, summed=tiles, psum=per + tiles,
              stage=16 + 8 * tiles if dst is not None else 0)


def token_product(nc, sems, weights, x_hi, x_lo, raw, w_hi, w_lo, psum, stage, store):
    groups, _, k_tiles, cols = weights.shape
    loaded, hi_ready, lo_ready, slot_free = sems.loaded, sems.hi_ready, sems.lo_ready, sems.slot_free
    summed, psum_free, stage_free = sems.summed, sems.psum_free, sems.stage_free
    base = dict(sems.base)
    bank = psum[:, :, :].rearrange("p a (b n) -> p (a b) n", n=HALF)
    with nc.Block() as block:
        @block.sync
        def _(sp):
            def load(g):
                sp.dma_start(raw[:, 0:k_tiles, :],
                             one(weights, g).rearrange("a p k n -> p (a k) n")).then_inc(loaded, 16)

            def stores(g):
                for t in range(NT):
                    sp.wait_ge(psum_free, g * NT + (8 + t + 1 + base["psum"]))
                    store(sp, g, t, stage[:, t % 2, 0:HALF]).then_inc(stage_free[t % 2], 16)

            for free in stage_free:
                sp.sem_inc(free, 16)
            load(0)
            with sp.Fori(0, groups - 1) as g:
                sp.wait_ge(lo_ready, g * k_tiles + (k_tiles + base["lo"]))
                load(g + 1)
                stores(g)
            stores(groups - 1)
            for free in stage_free:
                sp.wait_ge(free, 16 + 8 * groups * NT + base["stage"])

        @block.scalar
        def _(act):
            def split(g, k, first=False):
                if k == 0:
                    act.wait_ge(loaded, g * 16 + 16 + base["loaded"])
                if not first and k < k_tiles - 1:
                    act.wait_ge(slot_free, (g - 1) * (k_tiles - 1) + (k + 1) + base["slot"])
                elif not first:
                    act.wait_ge(summed, g * NT + base["summed"])
                nc.scalar.activation(w_hi[:, k, :], raw[:, k, :], ACT.Copy).then_inc(hi_ready, 1)

            def evacuate(g, t):
                act.wait_ge(summed, g * NT + (t + 1) + base["summed"])
                act.wait_ge(stage_free[t % 2], g * (8 * NT) + 16 * (t // 2 + 1) + base["stage"])
                nc.scalar.activation(stage[:, t % 2, 0:HALF], bank[:, t, :], ACT.Copy).then_inc(psum_free, 1)

            act.sem_inc(psum_free, 8)
            for k in range(k_tiles):
                split(0, k, first=True)
            with act.Fori(0, groups - 1) as g:
                for t in range(NT - 1):
                    evacuate(g, t)
                for k in range(k_tiles):
                    split(g + 1, k)
                evacuate(g, NT - 1)
            for t in range(NT):
                evacuate(groups - 1, t)

        @block.vector
        def _(dve):
            with dve.Fori(0, groups) as g:
                for k in range(k_tiles):
                    dve.wait_ge(hi_ready, g * k_tiles + (k + 1) + base["hi"])
                    nc.vector.tensor_tensor(w_lo[:, k, :], raw[:, k, :], w_hi[:, k, :].bitcast(F32),
                                            ALU.subtract).then_inc(lo_ready, 1)

        @block.tensor
        def _(pe):
            with pe.Fori(0, groups) as g:
                for t in range(NT):
                    tok = slice(t * P, (t + 1) * P)
                    pe.wait_ge(psum_free, g * NT + (t + 1) + base["psum"])
                    for k in range(k_tiles):
                        if t == 0:
                            pe.wait_ge(lo_ready, g * k_tiles + (k + 1) + base["lo"])
                        nc.tensor.matmul(bank[:, t, :], x_hi[:, k, tok], w_hi[:, k, :], start=(k == 0), stop=False)
                        nc.tensor.matmul(bank[:, t, :], x_lo[:, k, tok], w_hi[:, k, :], start=False, stop=False)
                        last = nc.tensor.matmul(bank[:, t, :], x_hi[:, k, tok], w_lo[:, k, :],
                                                start=False, stop=(k == k_tiles - 1))
                        if t == NT - 1 and k < k_tiles - 1:
                            last.then_inc(slot_free, 1)
                    last.then_inc(summed, 1)
    sems.past(loaded=16 * groups, hi=groups * k_tiles, lo=groups * k_tiles, slot=groups * (k_tiles - 1),
              summed=groups * NT, psum=8 + groups * NT, stage=16 + 8 * groups * NT)


def condition(nc, sem, a, t, spare):
    ins_loaded = sem("vectors_loaded")
    x_loaded = [sem("x_first_loaded"), sem("x_second_loaded")]
    rows_loaded = sem("rows_loaded")
    pos_loaded = sem("positions_loaded")
    ada_loaded = [sem("ada_even_loaded"), sem("ada_odd_loaded")]
    silu_c_ready = sem("silu_c_ready")
    ada_step = sem("ada_step")
    mod_summed = sem("mod_summed")
    mod_ready = sem("mod_ready")
    squared = sem("x_squared")
    rms = sem("x_rms")
    rooted = sem("x_rooted")
    normed = sem("x_normed")
    turned = sem("x_turned")
    h_hi_ready = sem("h_hi_ready")
    h_full_ready = sem("h_full_ready")
    h_lo_ready = sem("h_lo_ready")
    table = sem("table_step")
    sines = sem("sines_ready")
    magnitude = sem("angle_magnitude")
    const_ready = sem("const_ready")
    consts_split = sem("consts_split")
    with ExitStack() as ctx:
        sb = lambda n, shape, dt=F32: ctx.enter_context(nc.sbuf_tensor(n, shape, dt))
        pb = lambda n, shape: ctx.enter_context(nc.psum_tensor(n, shape, F32))
        x_tok = sb("x_tok", [P, NT, D])
        junk = sb("junk", [P, D])
        causal_add = sb("causal_add", [P, P])
        ada = sb("ada", [P, 2, KD, HALF])
        acc = sb("ada_sum", [P, 3 * D])
        mod = sb("mod", [P, 16])
        ss = sb("x_sumsq", [P, NT])
        root = sb("x_root", [P, NT])
        rstd = sb("x_rstd", [P, NT])
        silu_c = sb("silu_c", [P, KD])
        h_full = junk[:, :].rearrange("p (a n) -> p a n", n=HALF)
        ang, mag, turns = spare[:, 0:2, :], spare[:, 2:4, :], spare[:, 4, :]
        pos_i = spare[:, 5, :].bitcast(I32)
        p_mod = pb("p_mod", [P, HALF])
        p_gate = pb("p_gate", [P, 2, HALF])
        p_x = pb("p_x", [P, 4, HALF])
        block = ctx.enter_context(nc.Block())

        @block.sync
        def _(sp):
            sp.dma_start(t["cols"][:, :], a["cols"]).then_inc(ins_loaded, 16)
            sp.dma_start(t["consts"][:, :], a["consts"]).then_inc(ins_loaded, 16)
            sp.dma_start(t["ident"][:, :], a["ident"]).then_inc(ins_loaded, 16)
            sp.dma_start(causal_add[:, :], a["causal_add"]).then_inc(ins_loaded, 16)
            sp.dma_start(t["causal_kq"][:, :], a["causal_kq"]).then_inc(ins_loaded, 16)
            sp.dma_start(pos_i, a["positions"].partition_broadcast(P)).then_inc(pos_loaded, 16)
            for n in range(6):
                if n >= 2:
                    sp.wait_ge(ada_step, KD * (n - 1))
                sp.dma_start(ada[:, n % 2, :, :], a["w_ada"][n]).then_inc(ada_loaded[n % 2], 16)
                if n in (0, 1):
                    sp.dma_start(x_tok[:, 4 * n:4 * n + 4, :],
                                 a["x"][4 * n:4 * n + 4].rearrange("t p d -> p t d")).then_inc(x_loaded[n], 16)
            sp.dma_start(t["gate"][:, :], a["b_gate"].partition_broadcast(P)).then_inc(rows_loaded, 16)
            sp.dma_start(t["g_final"][:, :], a["g_final"].partition_broadcast(P)).then_inc(rows_loaded, 16)

        @block.gpsimd
        def _(pool):
            nc.gpsimd.memset(t["ones"][:, :], 1.0).then_inc(const_ready, 1)

        @block.scalar
        def _(act):
            act.wait_ge(ins_loaded, 80)
            nc.scalar.activation(t["ident_r"][:, :], t["ident"][:, :], ACT.Copy).then_inc(consts_split, 1)
            nc.scalar.activation(t["causal_r"][:, :], causal_add[:, :], ACT.Copy).then_inc(consts_split, 1)
            nc.scalar.activation(silu_c[:, :], t["cols"][:, COL_C:COL_C + KD], ACT.Silu).then_inc(silu_c_ready, 1)
            for n in range(NT):
                act.wait_ge(x_loaded[n // 4], 16)
                if n:
                    act.wait_ge(squared, n)
                nc.scalar.activation(junk[:, :], x_tok[:, n, :], ACT.Square,
                                     accum_out=ss[:, n:n + 1]).then_inc(squared, 1)
            act.wait_ge(rms, 1)
            nc.scalar.activation(root[:, :], ss[:, :], ACT.Sqrt).then_inc(rooted, 1)
            for n, sin_out in enumerate((t["sin_ret"][:, 1, :], t["sin_mla"][:, :])):
                act.wait_ge(table, 7 * (n + 1))
                nc.scalar.activation(mag[:, n, :], ang[:, n, :], ACT.Abs).then_inc(magnitude, 1)
                nc.scalar.activation(sin_out, ang[:, n, :], ACT.Sin, scale=(
                    t["consts"][:, CC_SIGN:CC_SIGN + 1] if n else 1.0)).then_inc(sines, 1)
                act.wait_ge(magnitude, n + 1)
                nc.scalar.activation((t["cos_mla"] if n else t["cos_ret"])[:, :], mag[:, n, :], ACT.Sin, scale=-1.0,
                                     bias=t["consts"][:, CC_HALF_PI:CC_HALF_PI + 1]).then_inc(sines, 1)
            nc.scalar.activation(t["sin_ret"][:, 0, :], ang[:, 0, :], ACT.Sin, scale=-1.0).then_inc(sines, 1)
            act.wait_ge(mod_ready, 3)
            for m in range(2 * KD):
                half, k = divmod(m, KD)
                act.wait_ge(turned, m + 1)
                nc.scalar.activation(t["h_hi"][:, k, half * HALF:(half + 1) * HALF], p_x[:, m % 4, :], ACT.Identity,
                                     scale=mod[:, KD + k:KD + k + 1], bias=mod[:, k:k + 1]).then_inc(h_hi_ready, 1)

        @block.vector
        def _(dve):
            dve.wait_ge(ins_loaded, 80)
            dve.wait_ge(pos_loaded, 16)
            steps = [0]

            def chained(ins):
                steps[0] += 1
                ins.then_inc(table, 1)
                dve.wait_ge(table, steps[0])

            for n, col in enumerate((CC_FREQ_RET, CC_FREQ_MLA)):
                chained(nc.vector.tensor_scalar(ang[:, n, :], pos_i, t["consts"][:, col:col + 1], None,
                                                ALU.mult))
                chained(nc.vector.tensor_scalar(turns, ang[:, n, :], float(1 / (2 * np.pi)), ROUNDER,
                                                ALU.mult, ALU.add))
                chained(nc.vector.tensor_scalar(turns, turns, -ROUNDER, None, ALU.add))
                for part in (TURN_1, TURN_2, TURN_3):
                    chained(nc.vector.scalar_tensor_tensor(out=ang[:, n, :], in0=turns, scalar=-part,
                                                           in1=ang[:, n, :], op0=ALU.mult, op1=ALU.add))
                chained(nc.vector.tensor_scalar(ang[:, n, :], ang[:, n, :], PI_BELOW, -PI_BELOW, ALU.min, ALU.max))
            dve.wait_ge(silu_c_ready, 1)
            for n in range(6):
                dve.wait_ge(ada_loaded[n % 2], 16 * (n // 2 + 1))
                cut = slice(n * HALF, (n + 1) * HALF)
                for k in range(KD):
                    if k == 0:
                        ins = nc.vector.tensor_scalar(acc[:, cut], ada[:, n % 2, k, :], silu_c[:, 0:1], None, ALU.mult)
                    else:
                        ins = nc.vector.scalar_tensor_tensor(out=acc[:, cut], in0=ada[:, n % 2, k, :],
                                                             scalar=silu_c[:, k:k + 1], in1=acc[:, cut],
                                                             op0=ALU.mult, op1=ALU.add)
                    ins.then_inc(ada_step, 1)
                    dve.wait_ge(ada_step, n * KD + k + 1)
                if n == 0:
                    dve.wait_ge(squared, NT)
                    nc.vector.tensor_scalar(ss[:, :], ss[:, :], 1.0 / D, EPS, ALU.mult, ALU.add).then_inc(rms, 1)
                    dve.wait_ge(rooted, 1)
                    nc.vector.reciprocal(rstd[:, :], root[:, :]).then_inc(rms, 1)
                    dve.wait_ge(rms, 2)
                    for j in range(NT):
                        nc.vector.tensor_scalar(x_tok[:, j, :], x_tok[:, j, :], rstd[:, j:j + 1], None,
                                                ALU.mult).then_inc(normed, 1)
                if n == 3:
                    dve.wait_ge(mod_summed, 1)
                    nc.vector.tensor_tensor(mod[:, :], p_mod[:, 0:16], t["cols"][:, COL_BADA:COL_BADA + 16],
                                            ALU.add).then_inc(mod_ready, 1)
                    dve.wait_ge(mod_ready, 1)
                    nc.vector.tensor_scalar(mod[:, KD:], mod[:, KD:], 1.0, None, ALU.add).then_inc(mod_ready, 1)
                    dve.wait_ge(mod_ready, 2)
                    nc.vector.tensor_tensor(mod[:, KD:], mod[:, KD:], t["cols"][:, COL_GPRE:COL_GPRE + KD],
                                            ALU.mult).then_inc(mod_ready, 1)
                    dve.wait_ge(mod_ready, 3)
                    for m in range(2 * KD):
                        half, k = divmod(m, KD)
                        dve.wait_ge(turned, m + 1)
                        if m >= 2:
                            dve.wait_ge(h_lo_ready, m - 1)
                        dve.wait_ge(h_hi_ready, m + 1)
                        nc.vector.tensor_scalar(h_full[:, m % 2, :], p_x[:, m % 4, :], mod[:, KD + k:KD + k + 1],
                                                mod[:, k:k + 1], ALU.mult, ALU.add).then_inc(h_full_ready, 1)
                        dve.wait_ge(h_full_ready, m + 1)
                        cols = slice(half * HALF, (half + 1) * HALF)
                        nc.vector.tensor_tensor(t["h_lo"][:, k, cols], h_full[:, m % 2, :],
                                                t["h_hi"][:, k, cols].bitcast(F32), ALU.subtract).then_inc(h_lo_ready, 1)
            dve.wait_ge(rows_loaded, 32)
            dve.wait_ge(mod_summed, 2)
            nc.vector.tensor_tensor(t["gate"][:, :], t["gate"][:, :], p_gate[:, :, :].rearrange("p a n -> p (a n)"),
                                    ALU.add).then_inc(mod_ready, 1)

        @block.tensor
        def _(pe):
            pe.wait_ge(normed, NT)
            pe.wait_ge(const_ready, 1)

            def turn(m):
                half, k = divmod(m, KD)
                if m >= 4:
                    pe.wait_ge(h_lo_ready, m - 3)
                for j in range(4):
                    last = nc.tensor.transpose(p_x[:, m % 4, j * P:(j + 1) * P],
                                               x_tok[:, 4 * half + j, k * P:(k + 1) * P], t["ident"][:, :])
                last.then_inc(turned, 1)

            for m in range(4):
                turn(m)
            pe.wait_ge(ada_step, 4 * KD)
            for n in range(16):
                last = nc.tensor.matmul(p_mod[:, n:n + 1], acc[:, n * P:(n + 1) * P], t["ones"][:, 0:1],
                                        start=True, stop=True)
            last.then_inc(mod_summed, 1)
            for m in range(4, 2 * KD):
                turn(m)
            pe.wait_ge(ada_step, 6 * KD)
            for half in range(2):
                last = nc.tensor.matmul(p_gate[:, half, :], t["ones"][:, :],
                                        acc[:, 2 * D + half * HALF:2 * D + (half + 1) * HALF], start=True, stop=True)
            last.then_inc(mod_summed, 1)


def normalise_latents(nc, sem, t, latent, cq_hi, cq_lo, ckv_hi, ckv_lo):
    squared = sem("latent_squared")
    summed = sem("latent_summed")
    rooted = sem("latent_rooted")
    inverted = sem("latent_inverted")
    scaled = sem("latent_scaled")
    hi_ready = sem("latent_hi_ready")
    lo_ready = sem("latent_lo_ready")
    swapped = sem("k_pe_swapped")
    roped = sem("k_pe_roped")
    with ExitStack() as ctx:
        sb = lambda n, shape, dt=F32: ctx.enter_context(nc.sbuf_tensor(n, shape, dt))
        square = sb("latent_square", [P, KQ + KKV, S])
        root = sb("latent_root", [P, 2, S])
        swap = sb("k_pe_swap", [P, S])
        rope = sb("k_pe_rope", [P, S])
        sums = ctx.enter_context(nc.psum_tensor("latent_sums", [P, 2, 2, HALF], F32))
        block = ctx.enter_context(nc.Block())
        tiles = [(0, n) for n in range(KQ)] + [(1, n) for n in range(KKV)]
        K_PE = KQ + KKV

        @block.sync
        def _(sp):
            for q in range(4):
                sp.dma_start(swap[32 * q:32 * q + 32, :],
                             latent[32 * (q ^ 1):32 * (q ^ 1) + 32, K_PE, :]).then_inc(swapped, 16)

        @block.scalar
        def _(act):
            for n in range(KQ + KKV):
                nc.scalar.activation(square[:, n, :], latent[:, n, :], ACT.Square).then_inc(squared, 1)
            for b, rank in enumerate((Q_RANK, KV_RANK)):
                act.wait_ge(summed, b + 1)
                nc.scalar.activation(root[:, b, :], sums[:, b, :, :].rearrange("p a n -> p (a n)"), ACT.Sqrt,
                                     scale=1.0 / rank, bias=t["consts"][:, CC_EPS:CC_EPS + 1]).then_inc(rooted, 1)
            for i, (b, n) in enumerate(tiles):
                act.wait_ge(scaled, i + 1)
                gain = t["cols"][:, COL_GQ + i:COL_GQ + i + 1]
                hi = ckv_hi if b else cq_hi
                nc.scalar.activation(hi[:, n, :], latent[:, i, :], ACT.Copy, scale=gain).then_inc(hi_ready, 1)
            act.wait_ge(roped, 3)
            nc.scalar.activation(t["k_rope_hi"][:, :], rope[:, :], ACT.Copy).then_inc(hi_ready, 1)

        @block.tensor
        def _(pe):
            for b, (first, last) in enumerate(((0, KQ), (KQ, KQ + KKV))):
                pe.wait_ge(squared, last)
                for half in range(2):
                    for n in range(first, last):
                        ins = nc.tensor.matmul(sums[:, b, half, :], t["ones"][:, :],
                                               square[:, n, half * HALF:(half + 1) * HALF],
                                               start=(n == first), stop=(n == last - 1))
                ins.then_inc(summed, 1)

        @block.vector
        def _(dve):
            dve.wait_ge(swapped, 64)
            nc.vector.tensor_tensor(rope[:, :], latent[:, K_PE, :], t["cos_mla"][:, :], ALU.mult).then_inc(roped, 1)
            nc.vector.tensor_tensor(swap[:, :], swap[:, :], t["sin_mla"][:, :], ALU.mult).then_inc(roped, 1)
            dve.wait_ge(roped, 2)
            nc.vector.tensor_tensor(rope[:, :], rope[:, :], swap[:, :], ALU.add).then_inc(roped, 1)
            for b in range(2):
                dve.wait_ge(rooted, b + 1)
                nc.vector.reciprocal(root[:, b, :], root[:, b, :]).then_inc(inverted, 1)
            dve.wait_ge(inverted, 2)
            for i, (b, n) in enumerate(tiles):
                nc.vector.tensor_tensor(latent[:, i, :], latent[:, i, :], root[:, b, :], ALU.mult).then_inc(scaled, 1)
            for i, (b, n) in enumerate(tiles):
                dve.wait_ge(hi_ready, i + 1)
                gain = t["cols"][:, COL_GQ + i:COL_GQ + i + 1]
                hi, lo = (ckv_hi, ckv_lo) if b else (cq_hi, cq_lo)
                nc.vector.scalar_tensor_tensor(out=lo[:, n, :], in0=latent[:, i, :], scalar=gain,
                                               in1=hi[:, n, :].bitcast(F32), op0=ALU.mult,
                                               op1=ALU.subtract).then_inc(lo_ready, 1)
            dve.wait_ge(hi_ready, len(tiles) + 1)
            nc.vector.tensor_tensor(t["k_rope_lo"][:, :], rope[:, :], t["k_rope_hi"][:, :].bitcast(F32),
                                    ALU.subtract).then_inc(lo_ready, 1)


def attention(nc, sem, a, t, q_t, q_rope_t, k_t, v_tok, act_t, y_t):
    loaded = sem("head_loaded")
    gate_loaded = [sem("gate_even_loaded"), sem("gate_odd_loaded")]
    roped = sem("q_rope_step")
    hi_ready = sem("head_hi_ready")
    lo_ready = sem("head_lo_ready")
    score_done = sem("score_done")
    max_done = sem("max_done")
    neg_done = sem("neg_max_done")
    exp_done = sem("exp_done")
    recip_done = sem("recip_done")
    prob_done = sem("prob_done")
    turned = sem("prob_turned")
    pt_hi_ready = sem("pt_hi_ready")
    pt_lo_ready = sem("pt_lo_ready")
    pv_done = sem("pv_done")
    y_done = sem("y_done")
    stored = [sem("y_even_stored"), sem("y_odd_stored")]
    LOADS = 9
    CHUNKS = [1, 1, 1, 1, 2, 2, 2, 2]
    BEFORE = [sum(CHUNKS[:i]) for i in range(NT + 1)]
    PAIRS = NT // 2
    with ExitStack() as ctx:
        sb = lambda n, shape, dt=F32: ctx.enter_context(nc.sbuf_tensor(n, shape, dt))
        pb = lambda n, shape: ctx.enter_context(nc.psum_tensor(n, shape, F32))
        q_raw, k_raw = sb("q_raw", [P, S]), sb("k_raw", [P, S])
        v_raw = sb("v_raw", [P, NT, V_MLA])
        r_raw, r_swap, r_sum = sb("r_raw", [P, S]), sb("r_swap", [P, S]), sb("r_sum", [P, S])
        gate = sb("head_gate", [P, 2, S])
        q_hi, q_lo = sb("q_hi", [P, 2, S], F32R), sb("q_lo", [P, 2, S], F32R)
        k_hi, k_lo = sb("k_hi", [P, 2, S], F32R), sb("k_lo", [P, 2, S], F32R)
        v_hi, v_lo = sb("v_hi", [P, 2, NT, V_MLA], F32R), sb("v_lo", [P, 2, NT, V_MLA], F32R)
        q_rope = sb("q_rope", [P, 2, S], F32R)
        prob = sb("prob", [P, 2, S])
        pt_hi, pt_lo = sb("pt_hi", [P, 2, NT, 256], F32R), sb("pt_lo", [P, 2, NT, 256], F32R)
        y = sb("y_head", [P, 2, S])
        row_max, neg_max = sb("row_max", [P, 2]), sb("neg_max", [P, 2])
        row_sum, recip = sb("row_sum", [P, 2]), sb("recip", [P, 2])
        p_s = pb("p_scores", [P, 2, S])
        p_t = pb("p_turned", [P, 2, HALF])
        p_y = pb("p_y", [P, 2, HALF])
        block = ctx.enter_context(nc.Block())

        ROUNDS = H_MLA // 2

        def rounds(engine, body):
            with engine.Fori(0, ROUNDS - 1) as it:
                body(it, False)
            body(ROUNDS - 1, True)

        @block.sync
        def _(sp):
            with sp.Fori(0, ROUNDS) as it:
                for s in range(2):
                    h = it * 2 + s

                    def head(ap, rows=slice(None)):
                        return one(ap, h).rearrange("a p n -> p (a n)")[rows]

                    sp.wait_ge(lo_ready, it * 8 + 4 * (s + 1))
                    sp.dma_start(q_raw[:, :], head(q_t)).then_inc(loaded, 16)
                    sp.dma_start(k_raw[:, :], head(k_t)).then_inc(loaded, 16)
                    sp.dma_start(v_raw[:, :, :], one(v_tok, h).rearrange("a p t n -> p (a t) n")).then_inc(loaded, 16)
                    for rep in range(2):
                        sp.dma_start(r_raw[64 * rep:64 * rep + 64, :], head(q_rope_t)).then_inc(loaded, 16)
                        for part in range(2):
                            row, src = 64 * rep + 32 * part, 32 * (1 - part)
                            sp.dma_start(r_swap[row:row + 32, :], head(q_rope_t, slice(src, src + 32)))\
                                .then_inc(loaded, 16)
                    sp.wait_ge(y_done, it * 8 + 4 * (s + 1))
                    sp.dma_start(gate[:, s, :], head(act_t)).then_inc(gate_loaded[s], 16)

        @block.gpsimd
        def _(pool):
            def rotate(it, s):
                pool.wait_ge(loaded, it * (2 * 16 * LOADS) + 16 * LOADS * (s + 1))
                nc.gpsimd.tensor_tensor(r_raw[:, :], r_raw[:, :], t["cos_mla"][:, :], ALU.mult).then_inc(roped, 1)
                nc.gpsimd.tensor_tensor(r_swap[:, :], r_swap[:, :], t["sin_mla"][:, :], ALU.mult).then_inc(roped, 1)
                pool.wait_ge(roped, it * 6 + (3 * s + 2))
                pool.wait_ge(lo_ready, it * 8 + 4 * (s + 1))
                nc.gpsimd.tensor_tensor(r_sum[:, :], r_raw[:, :], r_swap[:, :], ALU.add).then_inc(roped, 1)

            with pool.Fori(0, ROUNDS) as it:
                for s in range(2):
                    rotate(it, s)

        def prepare_hi(act, it, s, part):
            if part == 0:
                act.wait_ge(loaded, it * (2 * 16 * LOADS) + 16 * LOADS * (s + 1))
                act.wait_ge(pv_done, it * 8 + 4 * (s + 1))
            src, out = [(q_raw[:, :], q_hi[:, s, :]), (k_raw[:, :], k_hi[:, s, :]),
                        (v_raw[:, :, :], v_hi[:, s, :, :]), (r_sum[:, :], q_rope[:, s, :])][part]
            if part == 3:
                act.wait_ge(roped, it * 6 + 3 * (s + 1))
            nc.scalar.activation(out, src, ACT.Copy).then_inc(hi_ready, 1)

        def prepare_lo(dve, it, s, part):
            dve.wait_ge(hi_ready, it * 8 + (4 * s + part + 1))
            low = slice(64, 128)
            src, hi, out = [
                (q_raw[:, :], q_hi[:, s, :], q_lo[:, s, :]), (k_raw[:, :], k_hi[:, s, :], k_lo[:, s, :]),
                (v_raw[:, :, :], v_hi[:, s, :, :], v_lo[:, s, :, :]),
                (r_sum[low, :], q_rope[low, s, :], q_rope[low, s, :])][part]
            nc.vector.tensor_tensor(out, src, hi.bitcast(F32), ALU.subtract).then_inc(lo_ready, 1)

        STEPS = 2 * NT
        CH = 2 * BEFORE[NT]

        def chunks(m):
            i = m % NT
            return [(BEFORE[i] + (m // NT) * BEFORE[NT] + c, 4 * c, min(4, i + 1 - 4 * c)) for c in range(CHUNKS[i])]

        @block.scalar
        def _(act):
            for part in range(4):
                prepare_hi(act, 0, 0, part)

            def body(it, is_last):
                for m in range(STEPS + 2):
                    if m < STEPS:
                        width = (m % NT + 1) * P
                        act.wait_ge(neg_done, it * STEPS + (m + 1))
                        if m >= 2:
                            act.wait_ge(turned, it * CH + (chunks(m - 2)[-1][0] + 1))
                        nc.scalar.activation(prob[:, m % 2, 0:width], p_s[:, m % 2, 0:width], ACT.Exp,
                                             bias=neg_max[:, m % 2:m % 2 + 1], scale=SCALE,
                                             accum_out=row_sum[:, m % 2:m % 2 + 1]).then_inc(exp_done, 1)
                    if m >= 2:
                        pair = (m - 2) // 2
                        off = (m % 2) * P
                        for c, j, count in chunks(m - 2):
                            act.wait_ge(turned, it * CH + (c + 1))
                            if pair >= 2:
                                act.wait_ge(pv_done, it * 8 + (2 * PAIRS + pair - 1))
                            nc.scalar.activation(pt_hi[:, pair % 2, j:j + count, off:off + P],
                                                 p_t[:, c % 2, 0:count * P].rearrange("p (j n) -> p j n", n=P),
                                                 ACT.Copy).then_inc(pt_hi_ready, 1)
                    if 4 <= m % NT < 8 and m < STEPS and not (is_last and m >= NT):
                        prepare_hi(act, it + m // NT, 1 - m // NT, m % NT - 4)
                    if m in (NT + 4, STEPS + 1):
                        s = 0 if m == NT + 4 else 1
                        act.wait_ge(y_done, it * 8 + (2 * PAIRS + PAIRS * (s + 1)))
                        act.dma_start(one(y_t, it * 2 + s).rearrange("a p n -> p (a n)"), y[:, s, :])\
                            .then_inc(stored[s], 16)

            for free in stored:
                act.sem_inc(free, 16)
            rounds(act, body)
            for free in stored:
                act.wait_ge(free, 16 + 8 * H_MLA)

        @block.vector
        def _(dve):
            dve.sem_inc(lo_ready, 4)
            dve.sem_inc(y_done, 2 * PAIRS)
            for part in range(4):
                prepare_lo(dve, 0, 0, part)

            def body(it, is_last):
                for m in range(STEPS + 4):
                    if m < STEPS:
                        one_slot = slice(m % 2, m % 2 + 1)
                        dve.wait_ge(score_done, it * STEPS + (m + 1))
                        nc.vector.reduce_max(row_max[:, one_slot], p_s[:, m % 2, 0:(m % NT + 1) * P], AX.X)\
                            .then_inc(max_done, 1)
                        dve.wait_ge(max_done, it * STEPS + (m + 1))
                        nc.vector.tensor_scalar(neg_max[:, one_slot], row_max[:, one_slot], -SCALE, None,
                                                ALU.mult).then_inc(neg_done, 1)
                    if 1 <= m <= STEPS:
                        b = m - 1
                        one_slot = slice(b % 2, b % 2 + 1)
                        width = (b % NT + 1) * P
                        dve.wait_ge(exp_done, it * STEPS + (b + 1))
                        nc.vector.reciprocal(recip[:, one_slot], row_sum[:, one_slot]).then_inc(recip_done, 1)
                        dve.wait_ge(recip_done, it * STEPS + (b + 1))
                        nc.vector.tensor_scalar(prob[:, b % 2, 0:width], prob[:, b % 2, 0:width], recip[:, one_slot],
                                                None, ALU.mult).then_inc(prob_done, 1)
                    if 2 <= m <= STEPS + 1:
                        pair = (m - 2) // 2
                        off = (m % 2) * P
                        for c, j, count in chunks(m - 2):
                            dve.wait_ge(pt_hi_ready, it * CH + (c + 1))
                            nc.vector.tensor_tensor(pt_lo[:, pair % 2, j:j + count, off:off + P],
                                                    p_t[:, c % 2, 0:count * P].rearrange("p (j n) -> p j n", n=P),
                                                    pt_hi[:, pair % 2, j:j + count, off:off + P].bitcast(F32),
                                                    ALU.subtract).then_inc(pt_lo_ready, 1)
                    if m >= 4 and m % 2 == 0:
                        pair = (m - 4) // 2
                        s, p = divmod(pair, PAIRS)
                        dve.wait_ge(pv_done, it * 8 + (2 * PAIRS + pair + 1))
                        if p == 0:
                            dve.wait_ge(stored[s], it * 16 + 16)
                            dve.wait_ge(gate_loaded[s], it * 16 + 16)
                        cut = slice(256 * p, 256 * p + 256)
                        nc.vector.tensor_tensor(y[:, s, cut], p_y[:, pair % 2, 0:256], gate[:, s, cut], ALU.mult)\
                            .then_inc(y_done, 1)
                    if 4 <= m % NT < 8 and m < STEPS and not (is_last and m >= NT):
                        prepare_lo(dve, it + m // NT, 1 - m // NT, m % NT - 4)

            rounds(dve, body)

        @block.tensor
        def _(pe):
            def scores(it, m):
                s, i = divmod(m, NT)
                if i == 0:
                    pe.wait_ge(lo_ready, it * 8 + (4 + 4 * (s + 1)))
                if m >= 2:
                    pe.wait_ge(exp_done, it * STEPS + (m - 1))
                q = slice(i * P, (i + 1) * P)
                for c in range(0, (i + 1) * P, HALF):
                    k = slice(c, min(c + HALF, (i + 1) * P))
                    out = p_s[:, m % 2, k]
                    diagonal = k.stop == (i + 1) * P
                    nc.tensor.matmul(out, q_hi[:, s, q], k_hi[:, s, k], start=True, stop=False)
                    nc.tensor.matmul(out, q_hi[:, s, q], k_lo[:, s, k], start=False, stop=False)
                    nc.tensor.matmul(out, q_lo[:, s, q], k_hi[:, s, k], start=False, stop=False)
                    nc.tensor.matmul(out, q_rope[:, s, q], t["k_rope_hi"][:, k], start=False, stop=False)
                    last = nc.tensor.matmul(out, q_rope[:, s, q], t["k_rope_lo"][:, k], start=False, stop=not diagonal)
                    if diagonal:
                        last = nc.tensor.matmul(p_s[:, m % 2, q], t["ident_r"][:, :], t["causal_r"][:, :],
                                                start=False, stop=True)
                last.then_inc(score_done, 1)

            def turn(it, m):
                pe.wait_ge(prob_done, it * STEPS + (m + 1))
                for c, j, count in chunks(m):
                    if c >= 2:
                        pe.wait_ge(pt_lo_ready, it * CH + (c - 1))
                    for b in range(count):
                        last = nc.tensor.transpose(p_t[:, c % 2, b * P:(b + 1) * P],
                                                   prob[:, m % 2, (j + b) * P:(j + b + 1) * P], t["ident"][:, :])
                    last.then_inc(turned, 1)

            def values(it, pair):
                s, p = divmod(pair, PAIRS)
                pe.wait_ge(pt_lo_ready, it * CH + (chunks(2 * pair + 1)[-1][0] + 1))
                if pair >= 2:
                    pe.wait_ge(y_done, it * 8 + (2 * PAIRS + pair - 1))
                for j in range(2 * p + 2):
                    cols = slice(P if j == 2 * p + 1 else 0, 256)
                    out = p_y[:, pair % 2, cols]
                    nc.tensor.matmul(out, v_hi[:, s, j, :], pt_hi[:, pair % 2, j, cols], start=(j == 0), stop=False)
                    nc.tensor.matmul(out, v_hi[:, s, j, :], pt_lo[:, pair % 2, j, cols], start=False, stop=False)
                    last = nc.tensor.matmul(out, v_lo[:, s, j, :], pt_hi[:, pair % 2, j, cols], start=False,
                                            stop=(j == 2 * p + 1))
                last.then_inc(pv_done, 1)

            def body(it, is_last):
                for m in range(STEPS + 4):
                    if m < STEPS:
                        scores(it, m)
                    if m >= 4 and m % 2 == 0:
                        values(it, (m - 4) // 2)
                    if 1 <= m <= STEPS:
                        turn(it, m - 1)

            pe.sem_inc(pv_done, 2 * PAIRS)
            rounds(pe, body)


def retention(nc, sem, a, t, act_t, v_tok, y_t):
    loaded = [sem("chunk_loaded_%d" % r) for r in range(4)]
    v_loaded = [sem("chunk_v_loaded_%d" % r) for r in range(4)]
    gate_loaded = [sem("chunk_gate_loaded_%d" % r) for r in range(4)]
    rotated = sem("chunk_rotated")
    added = sem("chunk_rope_added")
    decayed = sem("chunk_decayed")
    qk_hi_ready = sem("qk_hi_ready")
    qk_lo_ready = sem("qk_lo_ready")
    v_hi_ready = sem("v_hi_ready")
    v_lo_ready = sem("v_lo_ready")
    k_turned = sem("k_turned")
    k_hi_ready = sem("k_tok_hi_ready")
    k_lo_ready = sem("k_tok_lo_ready")
    inner_done = sem("inner_scores_done")
    masked = sem("inner_scores_masked")
    i_hi_ready = sem("inner_hi_ready")
    i_lo_ready = sem("inner_lo_ready")
    out_done = sem("out_done")
    state_done = sem("state_done")
    r_hi_ready = sem("state_hi_ready")
    r_lo_ready = sem("state_lo_ready")
    stats_done = sem("stats_done")
    rooted = sem("out_rooted")
    normed = sem("out_normed")
    out_turned = sem("out_turned")
    y_done = sem("chunk_y_done")
    stored = [sem("chunk_y_even_stored"), sem("chunk_y_odd_stored")]
    RING = 4
    with ExitStack() as ctx:
        sb = lambda n, shape, dt=F32: ctx.enter_context(nc.sbuf_tensor(n, shape, dt))
        pb = lambda n, shape: ctx.enter_context(nc.psum_tensor(n, shape, F32))
        x = sb("qk_raw", [P, RING, 2, 2, P])
        decay = sb("decay", [P, RING, 2, P])
        v_raw = sb("v_chunk", [P, RING, RET_V])
        gate = sb("gate_chunk", [P, RING, 4, P])
        rot = sb("rot", [P, 2, 2, 2, P])
        cross = sb("rot_cross", [P, 2, 2, 2, P])
        qk_hi, qk_lo = sb("qk_hi", [P, 2, 2, 2, P], F32R), sb("qk_lo", [P, 2, 2, 2, P], F32R)
        v_hi, v_lo = sb("vr_hi", [P, 2, RET_V], F32R), sb("vr_lo", [P, 2, RET_V], F32R)
        k_hi, k_lo = sb("k_tok_hi", [P, 2, RET_QK], F32R), sb("k_tok_lo", [P, 2, RET_QK], F32R)
        inner = sb("inner", [P, 2, P])
        i_hi, i_lo = sb("inner_hi", [P, 2, P], F32R), sb("inner_lo", [P, 2, P], F32R)
        r_hi, r_lo = sb("state_hi", [P, 2, RET_V], F32R), sb("state_lo", [P, 2, RET_V], F32R)
        out_n = sb("out_n", [P, 2, RET_V])
        y = sb("y_chunk", [P, 2, 4, P])
        stats, mean_var = sb("stats", [P, 2, 6]), sb("mean_var", [P, 2, 2])
        root, rstd, shift = sb("root_r", [P, 2]), sb("rstd_r", [P, 2]), sb("shift_r", [P, 2])
        carrier = sb("carrier", [P, 1])
        p_k = pb("p_k_tok", [P, HALF])
        p_i = pb("p_inner", [P, HALF])
        p_o = pb("p_out", [P, 2, HALF])
        p_r = pb("p_state", [P, 2, HALF])
        p_y = pb("p_y_turned", [P, 2, HALF])
        block = ctx.enter_context(nc.Block())
        C = NT

        def two_tiles(tile, h, m):
            return act_t[bass.ds(h * 2 + tile, 2)].rearrange("a p n -> p a n")[:, :, m * P:(m + 1) * P]

        @block.sync
        def _(sp):
            def load(h, m):
                r = m % RING
                sp.dma_start(x[:, r, 0, :, :], two_tiles(Q_RET, h, m)).then_inc(loaded[r], 16)
                sp.dma_start(x[:, r, 1, :, :], two_tiles(K_RET, h, m)).then_inc(loaded[r], 16)
                sp.dma_start(decay[:, r, :, :], one(a["decay"], h)[:, :, m * P:(m + 1) * P]
                             .rearrange("a b n -> (a b) n").partition_broadcast(P)).then_inc(loaded[r], 16)
                sp.dma_start(v_raw[:, r, :], one(v_tok, h).rearrange("a p t n -> p (a t) n")[:, m, :])\
                    .then_inc(v_loaded[r], 16)
                sp.dma_start(gate[:, r, :, :], act_t[bass.ds(h * 4 + GATE_RET, 4)]
                             .rearrange("a p n -> p a n")[:, :, m * P:(m + 1) * P]).then_inc(gate_loaded[r], 16)

            def body(h, is_last):
                for m in range(C):
                    sp.wait_ge(y_done, h * C + (m + 1))
                    sp.dma_start(y_t[bass.ds(h * 4, 4)].rearrange("a p n -> p a n")[:, :, m * P:(m + 1) * P],
                                 y[:, m % 2, :, :]).then_inc(stored[m % 2], 16)
                    if m + RING < C:
                        load(h, m + RING)
                    elif not is_last:
                        load(h + 1, m + RING - C)

            for free in stored:
                sp.sem_inc(free, 16)
            for m in range(RING):
                load(0, m)
            with sp.Fori(0, H_RET - 1) as h:
                body(h, False)
            body(H_RET - 1, True)
            for free in stored:
                sp.wait_ge(free, 16 + 8 * H_RET * C)

        @block.gpsimd
        def _(pool):
            with pool.Fori(0, H_RET) as h:
                for m in range(C):
                    r, s = m % RING, m % 2
                    tok = slice(m * P, (m + 1) * P)
                    pool.wait_ge(loaded[r], h * (48 * C // RING) + 48 * (m // RING + 1))
                    pool.wait_ge(k_turned, h * C + (m + 1))
                    nc.gpsimd.tensor_tensor(
                        rot[:, s, :, :, :].rearrange("p a b n -> p (a b) n"), x[:, r, :, :, :].rearrange("p a b n -> p (a b) n"),
                        t["cos_ret"][:, tok].unsqueeze(1).broadcast_to([P, 4, P]), ALU.mult).then_inc(rotated, 1)
                    for b in range(2):
                        nc.gpsimd.tensor_tensor(
                            cross[:, s, :, b, :], x[:, r, :, 1 - b, :],
                            t["sin_ret"][:, b, tok].unsqueeze(1).broadcast_to([P, 2, P]), ALU.mult).then_inc(rotated, 1)
                    pool.wait_ge(v_hi_ready, h * C + (m + 1))
                    nc.gpsimd.tensor_tensor(v_lo[:, s, :], v_raw[:, r, :], v_hi[:, s, :].bitcast(F32),
                                            ALU.subtract).then_inc(v_lo_ready, 1)

        @block.scalar
        def _(act):
            with act.Fori(0, H_RET) as h:
                for m in range(-2, C):
                    c, s = m + 1, (m + 1) % 2
                    if 0 <= c < C:
                        act.wait_ge(k_turned, h * C + (2 + c + 1))
                        nc.scalar.activation(k_hi[:, s, :], p_k[:, 0:RET_QK], ACT.Copy).then_inc(k_hi_ready, 1)
                        act.wait_ge(masked, h * C + (c + 1))
                        nc.scalar.activation(i_hi[:, s, :], inner[:, s, :], ACT.Copy).then_inc(i_hi_ready, 1)
                    c, s = m + 2, m % 2
                    if c < C:
                        act.wait_ge(v_loaded[c % RING], h * (16 * C // RING) + 16 * (c // RING + 1))
                        if c >= 2:
                            act.wait_ge(state_done, h * (C - 1) + (c - 1))
                        nc.scalar.activation(v_hi[:, s, :], v_raw[:, c % RING, :], ACT.Copy).then_inc(v_hi_ready, 1)
                        act.wait_ge(decayed, h * C + (c + 1))
                        nc.scalar.activation(qk_hi[:, s, :, :, :], rot[:, s, :, :, :], ACT.Copy).then_inc(qk_hi_ready, 1)
                    if m >= 0:
                        s = m % 2
                        if m < C - 1:
                            act.wait_ge(state_done, h * (C - 1) + (m + 1))
                            for b in range(2):
                                nc.scalar.activation(r_hi[:, b, :], p_r[:, b, :], ACT.Copy).then_inc(r_hi_ready, 1)
                        act.wait_ge(stats_done, h * (4 * C) + (4 * m + 2))
                        nc.scalar.activation(root[:, s:s + 1], mean_var[:, s, 1:2], ACT.Sqrt,
                                             bias=t["consts"][:, CC_EPS:CC_EPS + 1]).then_inc(rooted, 1)
                        act.wait_ge(stats_done, h * (4 * C) + (4 * m + 4))
                        nc.scalar.activation(out_n[:, s, :], p_o[:, s, :], ACT.Identity, scale=rstd[:, s:s + 1],
                                             bias=shift[:, s:s + 1]).then_inc(normed, 1)

        @block.vector
        def _(dve):
            with dve.Fori(0, H_RET) as h:
                for m in range(-2, C + 1):
                    c, s = m + 1, (m + 1) % 2
                    if 0 <= c < C:
                        dve.wait_ge(k_hi_ready, h * C + (c + 1))
                        nc.vector.tensor_tensor(k_lo[:, s, :], p_k[:, 0:RET_QK], k_hi[:, s, :].bitcast(F32),
                                                ALU.subtract).then_inc(k_lo_ready, 1)
                        dve.wait_ge(inner_done, h * C + (c + 1))
                        nc.vector.tensor_tensor(inner[:, s, :], p_i[:, 0:P], t["causal_kq"][:, :], ALU.mult)\
                            .then_inc(masked, 1)
                        dve.wait_ge(i_hi_ready, h * C + (c + 1))
                        nc.vector.tensor_tensor(i_lo[:, s, :], inner[:, s, :], i_hi[:, s, :].bitcast(F32),
                                                ALU.subtract).then_inc(i_lo_ready, 1)
                    c, s = m + 2, m % 2
                    if c < C:
                        dve.wait_ge(rotated, h * (3 * C) + 3 * (c + 1))
                        nc.vector.tensor_tensor(rot[:, s, :, :, :], rot[:, s, :, :, :], cross[:, s, :, :, :], ALU.add)\
                            .then_inc(added, 1)
                        dve.wait_ge(added, h * C + (c + 1))
                        nc.vector.tensor_tensor(rot[:, s, :, :, :], rot[:, s, :, :, :],
                                                decay[:, c % RING, :, :].unsqueeze(2).broadcast_to([P, 2, 2, P]),
                                                ALU.mult).then_inc(decayed, 1)
                        dve.wait_ge(qk_hi_ready, h * C + (c + 1))
                        nc.vector.tensor_tensor(qk_lo[:, s, :, :, :], rot[:, s, :, :, :],
                                                qk_hi[:, s, :, :, :].bitcast(F32), ALU.subtract).then_inc(qk_lo_ready, 1)
                    if 0 <= m < C:
                        s = m % 2
                        cut = slice(s, s + 1)
                        dve.wait_ge(out_done, h * C + (m + 1))
                        nc.vector.bn_stats(stats[:, s, :], p_o[:, s, :]).then_inc(stats_done, 1)
                        dve.wait_ge(stats_done, h * (4 * C) + (4 * m + 1))
                        nc.vector.memset(carrier[:, :], 0.0)
                        nc.vector.bn_aggr(mean_var[:, s, :], stats[:, s, :]).then_inc(stats_done, 1)
                        if m < C - 1:
                            for b in range(2):
                                dve.wait_ge(r_hi_ready, h * (2 * (C - 1)) + (2 * m + b + 1))
                                nc.vector.tensor_tensor(r_lo[:, b, :], p_r[:, b, :], r_hi[:, b, :].bitcast(F32),
                                                        ALU.subtract).then_inc(r_lo_ready, 1)
                        dve.wait_ge(rooted, h * C + (m + 1))
                        nc.vector.reciprocal(rstd[:, cut], root[:, cut]).then_inc(stats_done, 1)
                        dve.wait_ge(stats_done, h * (4 * C) + (4 * m + 3))
                        nc.vector.tensor_scalar(shift[:, cut], mean_var[:, s, 0:1], -1.0, rstd[:, cut],
                                                ALU.mult, ALU.mult).then_inc(stats_done, 1)
                    if m >= 1:
                        c, s = m - 1, (m - 1) % 2
                        dve.wait_ge(out_turned, h * C + (c + 1))
                        dve.wait_ge(gate_loaded[c % RING], h * (16 * C // RING) + 16 * (c // RING + 1))
                        dve.wait_ge(stored[s], h * (8 * C) + 16 * (c // 2 + 1))
                        nc.vector.tensor_tensor(y[:, s, :, :], p_y[:, s, :].rearrange("p (a n) -> p a n", n=P),
                                                gate[:, c % RING, :, :], ALU.mult).then_inc(y_done, 1)

        @block.tensor
        def _(pe):
            pe.sem_inc(k_turned, 2)
            with pe.Fori(0, H_RET) as h:
                for m in range(-1, C + 1):
                    c, s = m + 1, (m + 1) % 2
                    if c < C:
                        pe.wait_ge(qk_lo_ready, h * C + (c + 1))
                        if c:
                            pe.wait_ge(k_lo_ready, h * C + c)
                        for b in range(2):
                            last = nc.tensor.transpose(p_k[:, b * P:(b + 1) * P], rot[:, s, 1, b, :], t["ident"][:, :])
                        last.then_inc(k_turned, 1)
                        if c:
                            pe.wait_ge(masked, h * C + c)
                        for b in range(2):
                            out = p_i[:, 0:P]
                            nc.tensor.matmul(out, qk_hi[:, s, 1, b, :], qk_hi[:, s, 0, b, :], start=(b == 0), stop=False)
                            nc.tensor.matmul(out, qk_hi[:, s, 1, b, :], qk_lo[:, s, 0, b, :], start=False, stop=False)
                            last = nc.tensor.matmul(out, qk_lo[:, s, 1, b, :], qk_hi[:, s, 0, b, :], start=False,
                                                    stop=(b == 1))
                        last.then_inc(inner_done, 1)
                    if 0 <= m < C:
                        s = m % 2
                        pe.wait_ge(v_lo_ready, h * C + (m + 1))
                        pe.wait_ge(i_lo_ready, h * C + (m + 1))
                        if m >= 2:
                            pe.wait_ge(normed, h * C + (m - 1))
                        out = p_o[:, s, :]
                        nc.tensor.matmul(out, i_hi[:, s, :], v_hi[:, s, :], start=True, stop=False)
                        nc.tensor.matmul(out, i_hi[:, s, :], v_lo[:, s, :], start=False, stop=False)
                        last = nc.tensor.matmul(out, i_lo[:, s, :], v_hi[:, s, :], start=False, stop=(m == 0))
                        if m:
                            for b in range(2):
                                pe.wait_ge(r_lo_ready, h * (2 * (C - 1)) + (2 * (m - 1) + b + 1))
                                nc.tensor.matmul(out, qk_hi[:, s, 0, b, :], r_hi[:, b, :], start=False, stop=False)
                                nc.tensor.matmul(out, qk_hi[:, s, 0, b, :], r_lo[:, b, :], start=False, stop=False)
                                last = nc.tensor.matmul(out, qk_lo[:, s, 0, b, :], r_hi[:, b, :], start=False,
                                                        stop=(b == 1))
                        last.then_inc(out_done, 1)
                    if 0 <= m < C - 1:
                        pe.wait_ge(k_lo_ready, h * C + (m + 1))
                        for b in range(2):
                            cut = slice(b * P, (b + 1) * P)
                            out = p_r[:, b, :]
                            nc.tensor.matmul(out, k_hi[:, s, cut], v_hi[:, s, :], start=(m == 0), stop=False,
                                             skip_group_check=True)
                            nc.tensor.matmul(out, k_hi[:, s, cut], v_lo[:, s, :], start=False, stop=False,
                                             skip_group_check=True)
                            last = nc.tensor.matmul(out, k_lo[:, s, cut], v_hi[:, s, :], start=False, stop=True,
                                                    skip_group_check=True)
                        last.then_inc(state_done, 1)
                    if m >= 1:
                        s = (m - 1) % 2
                        pe.wait_ge(normed, h * C + m)
                        if m >= 3:
                            pe.wait_ge(y_done, h * C + (m - 2))
                        for b in range(4):
                            last = nc.tensor.transpose(p_y[:, s, b * P:(b + 1) * P], out_n[:, s, b * P:(b + 1) * P],
                                                       t["ident"][:, :])
                        last.then_inc(out_turned, 1)


def merge(nc, sem, a, t, weights, y_mla, y_ret, act_t, merged):
    y_loaded = [sem("y_even_loaded"), sem("y_odd_loaded")]
    y_hi_ready = sem("y_hi_ready")
    y_lo_ready = sem("y_lo_ready")
    loaded = sem("proj_w_loaded")
    hi_ready = sem("proj_w_hi_ready")
    lo_ready = sem("proj_w_lo_ready")
    summed = sem("proj_summed")
    gate_loaded = [sem("merge_gate_even_loaded"), sem("merge_gate_odd_loaded")]
    step = sem("merge_step")
    psum_free = sem("proj_psum_free")
    SETS, RING, PAIRS = 3, 12, KD // 2
    with ExitStack() as ctx:
        sb = lambda n, shape, dt=F32: ctx.enter_context(nc.sbuf_tensor(n, shape, dt))
        y_raw = sb("y_raw", [P, 2, S])
        y_hi, y_lo = sb("y_hi", [P, RING, S], F32R), sb("y_lo", [P, RING, S], F32R)
        raw = sb("proj_raw", [P, KD, 2 * P])
        w_hi, w_lo = sb("proj_hi", [P, KD, 2 * P], F32R), sb("proj_lo", [P, KD, 2 * P], F32R)
        gate = sb("merge_gate", [P, 2, S])
        part = sb("merge_part", [P, 2, S])
        psum = ctx.enter_context(nc.psum_tensor("p_proj", [P, 4, S], F32))
        block = ctx.enter_context(nc.Block())

        def gain(i):
            return t["cols"][:, COL_GRET + i:COL_GRET + i + 1] if i < 2 * KD else None

        @block.gpsimd
        def _(pool):
            for i in range(SETS * KD):
                if i >= 2:
                    pool.wait_ge(y_lo_ready, i - 1)
                src = y_ret[i] if i < 2 * KD else y_mla[i - 2 * KD]
                pool.dma_start(y_raw[:, i % 2, :], src).then_inc(y_loaded[i % 2], 16)

        @block.sync
        def _(sp):
            sp.dma_start(raw[:, :, :], weights[0]).then_inc(loaded, 16)
            for z in range(SETS):
                def body(g, is_last):
                    if z:
                        for j in range(2):
                            sp.wait_ge(psum_free, g * 2 + (z * KD + j + 1))
                            sp.dma_start(gate[:, j, :], one(act_t, g * 2 + (j + (MERGE_RET if z == 1 else MERGE_MLA)))
                                         .rearrange("a p n -> p (a n)")).then_inc(gate_loaded[j], 16)
                    if not is_last or z < SETS - 1:
                        sp.wait_ge(lo_ready, g * 2 + (2 * PAIRS * z + 2))
                        sp.dma_start(raw[:, :, :], one(weights, g + (z * PAIRS + 1))
                                     .rearrange("a p k n -> p (a k) n")).then_inc(loaded, 16)

                with sp.Fori(0, PAIRS - 1) as g:
                    body(g, False)
                body(PAIRS - 1, True)

        @block.scalar
        def _(act):
            def split_y(i):
                act.wait_ge(y_loaded[i % 2], 16 * (i // 2 + 1))
                scale = gain(i)
                nc.scalar.activation(y_hi[:, i % RING, :], y_raw[:, i % 2, :], ACT.Copy,
                                     scale=1.0 if scale is None else scale).then_inc(y_hi_ready, 1)

            def split_w(z, g, j, first=False):
                if not first:
                    act.wait_ge(summed, g * 2 + (z * KD + j + 1))
                    if j == 0:
                        act.wait_ge(loaded, g * 16 + 16 * (z * PAIRS + 2))
                cut = slice(j * P, (j + 1) * P)
                nc.scalar.activation(w_hi[:, :, cut], raw[:, :, cut], ACT.Copy).then_inc(hi_ready, 1)

            act.wait_ge(loaded, 16)
            split_w(0, 0, 0, first=True)
            for k in range(KD):
                split_y(k)
            split_w(0, 0, 1, first=True)
            for z in range(SETS):
                with act.Fori(0, PAIRS - 1) as g:
                    for j in range(2):
                        split_w(z, g, j)
                if z < SETS - 1:
                    for k in range(4):
                        split_y((z + 1) * KD + k)
                    for j in range(2):
                        split_w(z, PAIRS - 1, j)
                    for k in range(4, KD):
                        split_y((z + 1) * KD + k)

        @block.vector
        def _(dve):
            def low_y(i):
                dve.wait_ge(y_hi_ready, i + 1)
                slot = i % RING
                if gain(i) is None:
                    ins = nc.vector.tensor_tensor(y_lo[:, slot, :], y_raw[:, i % 2, :],
                                                  y_hi[:, slot, :].bitcast(F32), ALU.subtract)
                else:
                    ins = nc.vector.scalar_tensor_tensor(out=y_lo[:, slot, :], in0=y_raw[:, i % 2, :], scalar=gain(i),
                                                         in1=y_hi[:, slot, :].bitcast(F32), op0=ALU.mult,
                                                         op1=ALU.subtract)
                ins.then_inc(y_lo_ready, 1)

            def low_w(z, g, j, ahead=1):
                dve.wait_ge(hi_ready, g * 2 + (2 * PAIRS * z + 2 * ahead + j + 1))
                cut = slice(j * P, (j + 1) * P)
                nc.vector.tensor_tensor(w_lo[:, :, cut], raw[:, :, cut], w_hi[:, :, cut].bitcast(F32),
                                        ALU.subtract).then_inc(lo_ready, 1)

            def evacuate(z, g, j):
                out = merged[:, bass.ds(g * 2 + j, 1), :].rearrange("p a n -> p (a n)")
                dve.wait_ge(summed, g * 2 + (z * KD + j + 1))
                if z == 0:
                    nc.vector.tensor_copy(out, psum[:, j, :]).then_inc(psum_free, 1)
                    return
                dve.wait_ge(gate_loaded[j], g * 16 + 16 * ((z - 1) * PAIRS + 1))
                if z == 1:
                    nc.vector.tensor_tensor(part[:, j, :], psum[:, j, :], out, ALU.add).then_inc(step, 1)
                    dve.wait_ge(step, g * 2 + ((z - 1) * KD + j + 1))
                    nc.vector.tensor_tensor(out, part[:, j, :], gate[:, j, :], ALU.mult).then_inc(psum_free, 1)
                else:
                    nc.vector.tensor_tensor(part[:, j, :], psum[:, j, :], gate[:, j, :], ALU.mult).then_inc(step, 1)
                    dve.wait_ge(step, g * 2 + ((z - 1) * KD + j + 1))
                    nc.vector.tensor_tensor(out, part[:, j, :], out, ALU.add).then_inc(psum_free, 1)

            dve.sem_inc(psum_free, 2)
            low_w(0, 0, 0, ahead=0)
            for k in range(KD):
                low_y(k)
            low_w(0, 0, 1, ahead=0)
            for z in range(SETS):
                with dve.Fori(0, PAIRS - 1) as g:
                    for j in range(2):
                        evacuate(z, g, j)
                        low_w(z, g, j)
                if z < SETS - 1:
                    for k in range(4):
                        low_y((z + 1) * KD + k)
                for j in range(2):
                    evacuate(z, PAIRS - 1, j)
                    if z < SETS - 1:
                        low_w(z, PAIRS - 1, j)
                if z < SETS - 1:
                    for k in range(4, KD):
                        low_y((z + 1) * KD + k)

        @block.tensor
        def _(pe):
            def tile(z, g, j, first=False):
                cut = slice(j * P, (j + 1) * P)
                pe.wait_ge(lo_ready, g * 2 + (2 * PAIRS * z + j + 1))
                pe.wait_ge(psum_free, g * 2 + (z * KD + j + 1))
                for half in range(2):
                    out = psum[:, j, half * HALF:(half + 1) * HALF]
                    tok = slice(half * HALF, (half + 1) * HALF)
                    for k in range(KD):
                        slot = (z * KD + k) % RING
                        if first and half == 0:
                            pe.wait_ge(y_lo_ready, z * KD + k + 1)
                        nc.tensor.matmul(out, w_hi[:, k, cut], y_hi[:, slot, tok], start=(k == 0), stop=False)
                        nc.tensor.matmul(out, w_hi[:, k, cut], y_lo[:, slot, tok], start=False, stop=False)
                        last = nc.tensor.matmul(out, w_lo[:, k, cut], y_hi[:, slot, tok], start=False,
                                                stop=(k == KD - 1))
                last.then_inc(summed, 1)

            for z in range(SETS):
                for j in range(2):
                    tile(z, 0, j, first=(j == 0))
                with pe.Fori(1, PAIRS) as g:
                    for j in range(2):
                        tile(z, g, j)


def output(nc, sem, a, t, w_out, merged, out):
    w_loaded = [sem("out_w_even_loaded"), sem("out_w_odd_loaded")]
    x_loaded = [sem("residual_even_loaded"), sem("residual_odd_loaded")]
    m_hi_ready = sem("merged_hi_ready")
    m_lo_ready = sem("merged_lo_ready")
    w_hi_ready = sem("out_w_hi_ready")
    w_lo_ready = sem("out_w_lo_ready")
    summed = sem("out_summed")
    gated = sem("out_gated")
    added = sem("out_added")
    squared = sem("out_squared")
    meaned = sem("out_meaned")
    rooted = sem("out_root_ready")
    inverted = sem("out_inverted")
    finished = sem("out_finished")
    stored = [sem("out_even_stored"), sem("out_odd_stored")]
    with ExitStack() as ctx:
        sb = lambda n, shape, dt=F32: ctx.enter_context(nc.sbuf_tensor(n, shape, dt))
        m_hi, m_lo = sb("m_hi", [P, KD, S], F32R), sb("m_lo", [P, KD, S], F32R)
        w_raw = sb("out_raw", [P, 2, D])
        w_hi, w_lo = sb("out_hi", [P, KD, D], F32R), sb("out_lo", [P, KD, D], F32R)
        x = sb("residual", [P, 2, D])
        y = sb("out_y", [P, 2, D])
        ss, root, rstd = sb("out_ss", [P, 2]), sb("out_root", [P, 2]), sb("out_rstd", [P, 2])
        psum = ctx.enter_context(nc.psum_tensor("p_final", [P, 4, D], F32))
        block = ctx.enter_context(nc.Block())

        @block.sync
        def _(sp):
            for k in range(KD):
                if k >= 2:
                    sp.wait_ge(w_lo_ready, k - 1)
                sp.dma_start(w_raw[:, k % 2, :], w_out[k]).then_inc(w_loaded[k % 2], 16)
            for n in range(NT):
                if n >= 2:
                    sp.wait_ge(stored[n % 2], 16 * (n // 2))
                sp.dma_start(x[:, n % 2, :], a["x"][n]).then_inc(x_loaded[n % 2], 16)

        @block.gpsimd
        def _(pool):
            for n in range(NT):
                pool.wait_ge(finished, n + 1)
                pool.dma_start(out[n * P:(n + 1) * P, :], x[:, n % 2, :]).then_inc(stored[n % 2], 16)
            for done in stored:
                pool.wait_ge(done, 8 * NT)

        @block.scalar
        def _(act):
            for k in range(KD):
                nc.scalar.activation(m_hi[:, k, :], merged[:, k, :], ACT.Copy).then_inc(m_hi_ready, 1)
                act.wait_ge(w_loaded[k % 2], 16 * (k // 2 + 1))
                nc.scalar.activation(w_hi[:, k, :], w_raw[:, k % 2, :], ACT.Copy).then_inc(w_hi_ready, 1)
            for n in range(NT):
                s = n % 2
                act.wait_ge(added, n + 1)
                nc.scalar.activation(psum[:, n % 4, :], y[:, s, :], ACT.Square, accum_out=ss[:, s:s + 1])\
                    .then_inc(squared, 1)
                act.wait_ge(meaned, n + 1)
                nc.scalar.activation(root[:, s:s + 1], ss[:, s:s + 1], ACT.Sqrt).then_inc(rooted, 1)

        @block.vector
        def _(dve):
            for k in range(KD):
                dve.wait_ge(m_hi_ready, k + 1)
                nc.vector.tensor_tensor(m_lo[:, k, :], merged[:, k, :], m_hi[:, k, :].bitcast(F32),
                                        ALU.subtract).then_inc(m_lo_ready, 1)
                dve.wait_ge(w_hi_ready, k + 1)
                nc.vector.tensor_tensor(w_lo[:, k, :], w_raw[:, k % 2, :], w_hi[:, k, :].bitcast(F32),
                                        ALU.subtract).then_inc(w_lo_ready, 1)
            for n in range(NT):
                s = n % 2
                dve.wait_ge(summed, n + 1)
                nc.vector.tensor_tensor(y[:, s, :], psum[:, n % 4, :], t["gate"][:, :], ALU.mult).then_inc(gated, 1)
                dve.wait_ge(gated, n + 1)
                dve.wait_ge(x_loaded[s], 16 * (n // 2 + 1))
                nc.vector.tensor_tensor(y[:, s, :], y[:, s, :], x[:, s, :], ALU.add).then_inc(added, 1)
                dve.wait_ge(squared, n + 1)
                nc.vector.tensor_scalar(ss[:, s:s + 1], ss[:, s:s + 1], 1.0 / D, EPS, ALU.mult, ALU.add)\
                    .then_inc(meaned, 1)
                dve.wait_ge(rooted, n + 1)
                nc.vector.reciprocal(rstd[:, s:s + 1], root[:, s:s + 1]).then_inc(inverted, 1)
                dve.wait_ge(inverted, n + 1)
                nc.vector.scalar_tensor_tensor(out=x[:, s, :], in0=y[:, s, :], scalar=rstd[:, s:s + 1],
                                               in1=t["g_final"][:, :], op0=ALU.mult, op1=ALU.mult).then_inc(finished, 1)

        @block.tensor
        def _(pe):
            for n in range(NT):
                tok = slice(n * P, (n + 1) * P)
                if n >= 4:
                    pe.wait_ge(rooted, n - 3)
                for half in range(2):
                    cut = slice(half * HALF, (half + 1) * HALF)
                    for k in range(KD):
                        if n == 0 and half == 0:
                            pe.wait_ge(m_lo_ready, k + 1)
                            pe.wait_ge(w_lo_ready, k + 1)
                        res = psum[:, n % 4, cut]
                        nc.tensor.matmul(res, m_hi[:, k, tok], w_hi[:, k, cut], start=(k == 0), stop=False)
                        nc.tensor.matmul(res, m_hi[:, k, tok], w_lo[:, k, cut], start=False, stop=False)
                        last = nc.tensor.matmul(res, m_lo[:, k, tok], w_hi[:, k, cut], start=False, stop=(k == KD - 1))
                last.then_inc(summed, 1)


def build(nc, a, out):
    with ExitStack() as ctx:
        def sem(name):
            return ctx.enter_context(nc.semaphore(name))

        def sb(name, shape, dt=F32, where=ctx):
            return where.enter_context(nc.sbuf_tensor(name, shape, dt))

        def scratch(name, shape):
            return nc.dram_tensor(name, shape, F32, kind="Internal").ap()

        products = ProductSemaphores(sem)
        act_t = scratch("act_t", (ACT_TILES, P, S))
        v_ret = scratch("v_ret", (H_RET, P, NT, RET_V))
        q_t = scratch("q_t", (12, P, S))
        k_t = scratch("k_t", (H_MLA, P, S))
        v_mla = scratch("v_mla", (H_MLA, P, NT, V_MLA))
        y_mla = scratch("y_mla", (H_MLA, P, S))
        y_ret = scratch("y_ret", (H_RET * 4, P, S))

        t = {
            "cols": sb("cols", [P, N_COLS]), "consts": sb("consts", [P, 8]), "ones": sb("ones", [P, P]),
            "ident": sb("ident", [P, P]), "ident_r": sb("ident_r", [P, P], F32R),
            "causal_r": sb("causal_r", [P, P], F32R), "causal_kq": sb("causal_kq", [P, P]),
            "gate": sb("gate", [P, D]), "g_final": sb("g_final", [P, D]),
        }
        with ExitStack() as tables:
            t["cos_ret"] = sb("cos_ret", [P, S], where=tables)
            t["sin_ret"] = sb("sin_ret", [P, 2, S], where=tables)
            t["cos_mla"] = sb("cos_mla", [P, S], where=tables)
            t["sin_mla"] = sb("sin_mla", [P, S], where=tables)
            t["k_rope_hi"] = sb("k_rope_hi", [P, S], F32R, where=tables)
            t["k_rope_lo"] = sb("k_rope_lo", [P, S], F32R, where=tables)
            with ExitStack() as latents:
                latent = sb("latent", [P, 6, S], where=latents)
                with ExitStack() as hidden:
                    t["h_hi"] = sb("h_hi", [P, KD, S], F32R, where=hidden)
                    t["h_lo"] = sb("h_lo", [P, KD, S], F32R, where=hidden)
                    condition(nc, sem, a, t, latent)
                    with ExitStack() as w:
                        raw = sb("w_raw", [P, KD, HALF], where=w)
                        w_hi, w_lo = sb("w_hi", [P, KD, HALF], F32R, w), sb("w_lo", [P, KD, HALF], F32R, w)
                        stage = sb("stage", [P, 2, S], where=w)
                        psum = w.enter_context(nc.psum_tensor("p_tiles", [P, 4, S], F32))
                        common = (t["h_hi"], t["h_lo"], raw, w_hi, w_lo, psum)
                        transposed_product(nc, products, a["w_latent"], *common, [(2, ACT.Copy)], keep=latent)
                        transposed_product(nc, products, a["w_act"], *common,
                                           [(2, ACT.Silu), (4, ACT.Copy), (4, ACT.Silu), (4, ACT.Sigmoid)],
                                           stage=stage, dst=act_t)
                        token_product(nc, products, a["w_v"], *common, stage,
                                      lambda e, g, tile, src: e.dma_start(
                                          one(v_ret, g).rearrange("a p t n -> p (a t) n")[:, tile, :], src))
                with ExitStack() as up:
                    cq_hi, cq_lo = sb("cq_hi", [P, KQ, S], F32R, up), sb("cq_lo", [P, KQ, S], F32R, up)
                    ckv_hi, ckv_lo = sb("ckv_hi", [P, KKV, S], F32R, up), sb("ckv_lo", [P, KKV, S], F32R, up)
                    normalise_latents(nc, sem, t, latent, cq_hi, cq_lo, ckv_hi, ckv_lo)
                    raw = sb("up_raw", [P, KQ, HALF], where=up)
                    w_hi, w_lo = sb("up_hi", [P, KQ, HALF], F32R, up), sb("up_lo", [P, KQ, HALF], F32R, up)
                    stage = sb("up_stage", [P, 2, S], where=up)
                    psum = up.enter_context(nc.psum_tensor("p_up", [P, 4, S], F32))
                    transposed_product(nc, products, a["w_q_up"], cq_hi, cq_lo, raw, w_hi, w_lo, psum,
                                       [(3, ACT.Copy)], stage=stage, dst=q_t)
                    transposed_product(nc, products, a["w_k_up"], ckv_hi, ckv_lo, raw, w_hi, w_lo, psum,
                                       [(2, ACT.Copy)], stage=stage, dst=k_t)
                    token_product(nc, products, a["w_v_up"], ckv_hi, ckv_lo, raw, w_hi, w_lo, psum, stage,
                                  lambda e, g, tile, src: e.dma_start(
                                      v_mla[bass.ds(g * 4, 4)].rearrange("h p t n -> p h t n")[:, :, tile, :],
                                      src.rearrange("p (h n) -> p h n", h=4)))
            q_rope_t = q_t[8:12].rearrange("a (b p) n -> (a b) p n", b=2)
            attention(nc, sem, a, t, q_t, q_rope_t, k_t, v_mla, act_t, y_mla)
            retention(nc, sem, a, t, act_t, v_ret, y_ret)
        merged = sb("merged", [P, KD, S])
        merge(nc, sem, a, t, a["w_proj"], y_mla, y_ret, act_t, merged)
        output(nc, sem, a, t, a["w_out"], merged, out)


def shape_constants():
    consts = np.zeros((P, 8), np.float32)
    f = np.arange(P)
    consts[:, CC_FREQ_RET] = 10000.0 ** (-(2.0 * f) / RET_QK)
    consts[:, CC_FREQ_MLA] = 10000.0 ** (-(2.0 * (f % 32)) / ROPE)
    consts[:, CC_SIGN] = np.where(f % 64 < 32, -1.0, 1.0)
    consts[:, CC_HALF_PI] = np.pi / 2
    consts[:, CC_EPS] = EPS
    log_gamma = np.log1p(-np.exp2(-5.0 - np.arange(H_RET)))[:, None]
    token = np.arange(S)[None, :] + 1.0
    decay = np.stack([np.exp(log_gamma * token), np.exp(-log_gamma * token) * RET_QK ** -0.5], axis=1)
    later = f[None, :] > f[:, None]
    return {
        "consts": consts, "decay": decay.astype(np.float32), "ident": np.eye(P, dtype=np.float32),
        "causal_add": np.where(later, MASKED, 0.0).astype(np.float32),
        "causal_kq": (f[:, None] <= f[None, :]).astype(np.float32),
    }


def kernel(**inputs):
    import concourse.bacc as bacc
    from concourse.bass_utils import run_bass_kernel_spmd

    def groups(w, cols):
        k, n = w.shape
        return np.ascontiguousarray(w.reshape(k // P, P, n // cols, cols).transpose(2, 1, 0, 3))

    def columns(v):
        return v.reshape(-1, P).T

    w_in = inputs["w_in"][0]
    w_q = inputs["w_q_up"][0].reshape(Q_RANK, H_MLA, NOPE + ROPE)
    w_kv = inputs["w_kv_up"][0].reshape(KV_RANK, H_MLA, NOPE + V_MLA)
    b_ada = inputs["b_ada"][0]
    w_ret = inputs["w_proj_ret"][0]
    k_pe = w_in[:, 640:704]
    arrays = {
        "x": inputs["x"][0].reshape(NT, P, D),
        "positions": inputs["positions"][0],
        "cols": np.ascontiguousarray(np.concatenate([
            columns(inputs["c"][0]), columns(b_ada[:2 * D]), columns(inputs["g_pre"][0]), columns(inputs["g_q"][0]),
            columns(inputs["g_kv"][0]), columns(inputs["g_ret"][0])], axis=1)),
        "b_gate": b_ada[2 * D:],
        "g_final": inputs["g_final"],
        "w_ada": groups(inputs["w_ada"][0], HALF),
        "w_latent": groups(np.concatenate([w_in[:, :640], k_pe, k_pe], axis=1), 3 * P),
        "w_act": groups(np.concatenate([w_in[:, 704:3776], w_in[:, 5824:]], axis=1), HALF),
        "w_v": groups(w_in[:, 3776:5824], HALF),
        "w_q_up": groups(np.concatenate([w_q[:, :, :NOPE].reshape(Q_RANK, -1), w_q[:, :, NOPE:].reshape(Q_RANK, -1)],
                                        axis=1), HALF),
        "w_k_up": groups(w_kv[:, :, :NOPE].reshape(KV_RANK, -1), HALF),
        "w_v_up": groups(w_kv[:, :, NOPE:].reshape(KV_RANK, -1), HALF),
        "w_proj": np.concatenate([groups(w_ret[:D], 2 * P), groups(w_ret[D:], 2 * P),
                                  groups(inputs["w_proj_mla"][0], 2 * P)]),
        "w_out": inputs["w_out"][0].reshape(KD, P, D),
    }
    nc = bacc.Bacc("TRN2", target_bir_lowering=False, num_devices=1)
    aps = {}
    for name, value in arrays.items():
        value = arrays[name] = np.ascontiguousarray(value)
        aps[name] = nc.dram_tensor("in_" + name, value.shape, mybir.dt.from_np(value.dtype), kind="ExternalInput").ap()
    for name, value in shape_constants().items():
        made = nc.inline_tensor(value, name="const_" + name)
        aps[name] = made.ap() if not isinstance(made, bass.AP) else made
    out = nc.dram_tensor("out", (S, D), F32, kind="ExternalOutput").ap()
    build(nc, aps, out)
    result = run_bass_kernel_spmd(nc, [{"in_" + k: v for k, v in arrays.items()}], core_ids=[0])
    return result.results[0]["out"].reshape(1, S, D)
```

```python
from contextlib import ExitStack

import numpy as np
import concourse.bass as bass
from concourse import mybir

F32 = mybir.dt.float32
F32R = mybir.dt.float32r
I32 = mybir.dt.int32
ALU = mybir.AluOpType
ACT = mybir.ActivationFunctionType
AX = mybir.AxisListType

P = 128
S = 1024
D = 1024
KD = D // P
NT = S // P
HALF = 512
EPS = 1e-6
Q_RANK, KV_RANK, ROPE = 384, 256, 64
KQ, KKV = Q_RANK // P, KV_RANK // P
H_MLA, NOPE, V_MLA = 8, 128, 128
SCALE = float(NOPE + ROPE) ** -0.5
H_RET, RET_QK, RET_V = 4, 256, 512
GATE_MLA, Q_RET, K_RET, GATE_RET, MERGE_MLA, MERGE_RET = 0, 8, 16, 24, 40, 48
ACT_TILES = 56
MASKED = -1e30
TURN_1 = 6.28125
TURN_2 = float(np.float32(2 * np.pi - TURN_1))
TURN_3 = float(2 * np.pi - TURN_1 - TURN_2)
ROUNDER = 12582912.0
PI_BELOW = 3.1415925
COL_C, COL_BADA, COL_GPRE, COL_GQ, COL_GKV, COL_GRET = 0, 8, 24, 32, 35, 37
N_COLS = 53
CC_FREQ_RET, CC_FREQ_MLA, CC_SIGN, CC_HALF_PI, CC_EPS = 0, 1, 2, 3, 4


def one(ap, i):
    return ap[bass.ds(i, 1)]


def pipelined(engine, step, rounds, size, drain):
    def body(it, first, last):
        for m in range(size):
            step(it, m, lambda b: b >= 0 or not first, last)

    body(0, True, False)
    with engine.Fori(1, rounds - 1) as it:
        body(it, False, False)
    body(rounds - 1, False, True)
    for m in range(size, size + drain):
        step(rounds - 1, m, lambda b: b < size, True)


def lag(it, m, size):
    return (it, m) if m >= 0 else (it - 1, m + size)


class ProductSemaphores:

    def __init__(self, sem):
        self.loaded = sem("product_w_loaded")
        self.hi_ready = sem("product_w_hi_ready")
        self.lo_ready = sem("product_w_lo_ready")
        self.slot_free = sem("product_w_slot_free")
        self.summed = sem("product_tile_summed")
        self.psum_free = sem("product_psum_free")
        self.stage_free = [sem("product_stage_even_free"), sem("product_stage_odd_free")]
        self.base = dict.fromkeys(("loaded", "hi", "lo", "slot", "summed", "psum", "stage"), 0)

    def past(self, **counts):
        for key, count in counts.items():
            self.base[key] += count


def transposed_product(nc, sems, weights, x_hi, x_lo, raw, w_hi, w_lo, psum, segments,
                       stage=None, dst=None, keep=None):
    groups, _, k_tiles, cols = weights.shape
    per = cols // P
    loaded, hi_ready, lo_ready, slot_free = sems.loaded, sems.hi_ready, sems.lo_ready, sems.slot_free
    summed, psum_free, stage_free = sems.summed, sems.psum_free, sems.stage_free
    base = dict(sems.base)
    with nc.Block() as block:
        @block.sync
        def _(sp):
            def load(g):
                sp.dma_start(raw[:, 0:k_tiles, 0:cols],
                             one(weights, g).rearrange("a p k n -> p (a k) n")).then_inc(loaded, 16)

            def store(g):
                if dst is None:
                    return
                for j in range(per):
                    sp.wait_ge(psum_free, g * per + (per + j + 1 + base["psum"]))
                    sp.dma_start(one(dst, g * per + j).rearrange("a p n -> p (a n)"),
                                 stage[:, j % 2, :]).then_inc(stage_free[j % 2], 16)

            if dst is not None:
                for free in stage_free:
                    sp.sem_inc(free, 16)
            load(0)
            with sp.Fori(0, groups - 1) as g:
                sp.wait_ge(lo_ready, g * per + (per + base["lo"]))
                load(g + 1)
                store(g)
            store(groups - 1)
            if dst is not None:
                for free in stage_free:
                    sp.wait_ge(free, 16 + 8 * groups * per + base["stage"])

        @block.scalar
        def _(act):
            def split(g, j):
                if j == 0:
                    act.wait_ge(loaded, g * 16 + 16 + base["loaded"])
                nc.scalar.activation(w_hi[:, 0:k_tiles, j * P:(j + 1) * P], raw[:, 0:k_tiles, j * P:(j + 1) * P],
                                     ACT.Copy).then_inc(hi_ready, 1)

            def evacuate(g, j, func):
                act.wait_ge(summed, g * per + (j + 1) + base["summed"])
                if keep is None:
                    act.wait_ge(stage_free[j % 2], g * (8 * per) + 16 * (j // 2 + 1) + base["stage"])
                    out = stage[:, j % 2, :]
                else:
                    out = keep[:, bass.ds(g * per + j, 1), :].rearrange("p a n -> p (a n)")
                nc.scalar.activation(out, psum[:, j, :], func).then_inc(psum_free, 1)

            act.sem_inc(psum_free, per)
            for j in range(per):
                split(0, j)
            first = 0
            for count, func in segments:
                last = first + count
                looped = min(last, groups - 1)
                if looped > first:
                    with act.Fori(first, looped) as g:
                        for j in range(per):
                            evacuate(g, j, func)
                            split(g + 1, j)
                if last == groups:
                    for j in range(per):
                        evacuate(groups - 1, j, func)
                first = last

        @block.vector
        def _(dve):
            with dve.Fori(0, groups) as g:
                for j in range(per):
                    dve.wait_ge(hi_ready, g * per + (j + 1) + base["hi"])
                    nc.vector.tensor_tensor(w_lo[:, 0:k_tiles, j * P:(j + 1) * P],
                                            raw[:, 0:k_tiles, j * P:(j + 1) * P],
                                            w_hi[:, 0:k_tiles, j * P:(j + 1) * P].bitcast(F32),
                                            ALU.subtract).then_inc(lo_ready, 1)

        @block.tensor
        def _(pe):
            with pe.Fori(0, groups) as g:
                for j in range(per):
                    cut = slice(j * P, (j + 1) * P)
                    pe.wait_ge(lo_ready, g * per + (j + 1) + base["lo"])
                    pe.wait_ge(psum_free, g * per + (j + 1) + base["psum"])
                    for half in range(2):
                        out = psum[:, j, half * HALF:(half + 1) * HALF]
                        tok = slice(half * HALF, (half + 1) * HALF)
                        for k in range(k_tiles):
                            nc.tensor.matmul(out, w_hi[:, k, cut], x_hi[:, k, tok], start=(k == 0), stop=False)
                            nc.tensor.matmul(out, w_hi[:, k, cut], x_lo[:, k, tok], start=False, stop=False)
                            last = nc.tensor.matmul(out, w_lo[:, k, cut], x_hi[:, k, tok],
                                                    start=False, stop=(k == k_tiles - 1))
                    last.then_inc(summed, 1)
    tiles = groups * per
    sems.past(loaded=16 * groups, hi=tiles, lo=tiles, summed=tiles, psum=per + tiles,
              stage=16 + 8 * tiles if dst is not None else 0)


def token_product(nc, sems, weights, x_hi, x_lo, raw, w_hi, w_lo, psum, stage, store):
    groups, _, k_tiles, cols = weights.shape
    loaded, hi_ready, lo_ready, slot_free = sems.loaded, sems.hi_ready, sems.lo_ready, sems.slot_free
    summed, psum_free, stage_free = sems.summed, sems.psum_free, sems.stage_free
    base = dict(sems.base)
    bank = psum[:, :, :].rearrange("p a (b n) -> p (a b) n", n=HALF)
    with nc.Block() as block:
        @block.sync
        def _(sp):
            def load(g):
                sp.dma_start(raw[:, 0:k_tiles, :],
                             one(weights, g).rearrange("a p k n -> p (a k) n")).then_inc(loaded, 16)

            def stores(g):
                for t in range(NT):
                    sp.wait_ge(psum_free, g * NT + (8 + t + 1 + base["psum"]))
                    store(sp, g, t, stage[:, t % 2, 0:HALF]).then_inc(stage_free[t % 2], 16)

            for free in stage_free:
                sp.sem_inc(free, 16)
            load(0)
            with sp.Fori(0, groups - 1) as g:
                sp.wait_ge(lo_ready, g * k_tiles + (k_tiles + base["lo"]))
                load(g + 1)
                stores(g)
            stores(groups - 1)
            for free in stage_free:
                sp.wait_ge(free, 16 + 8 * groups * NT + base["stage"])

        @block.scalar
        def _(act):
            def split(g, k, first=False):
                if k == 0:
                    act.wait_ge(loaded, g * 16 + 16 + base["loaded"])
                if not first and k < k_tiles - 1:
                    act.wait_ge(slot_free, (g - 1) * (k_tiles - 1) + (k + 1) + base["slot"])
                elif not first:
                    act.wait_ge(summed, g * NT + base["summed"])
                nc.scalar.activation(w_hi[:, k, :], raw[:, k, :], ACT.Copy).then_inc(hi_ready, 1)

            def evacuate(g, t):
                act.wait_ge(summed, g * NT + (t + 1) + base["summed"])
                act.wait_ge(stage_free[t % 2], g * (8 * NT) + 16 * (t // 2 + 1) + base["stage"])
                nc.scalar.activation(stage[:, t % 2, 0:HALF], bank[:, t, :], ACT.Copy).then_inc(psum_free, 1)

            act.sem_inc(psum_free, 8)
            for k in range(k_tiles):
                split(0, k, first=True)
            with act.Fori(0, groups - 1) as g:
                for t in range(NT - 1):
                    evacuate(g, t)
                for k in range(k_tiles):
                    split(g + 1, k)
                evacuate(g, NT - 1)
            for t in range(NT):
                evacuate(groups - 1, t)

        @block.vector
        def _(dve):
            with dve.Fori(0, groups) as g:
                for k in range(k_tiles):
                    dve.wait_ge(hi_ready, g * k_tiles + (k + 1) + base["hi"])
                    nc.vector.tensor_tensor(w_lo[:, k, :], raw[:, k, :], w_hi[:, k, :].bitcast(F32),
                                            ALU.subtract).then_inc(lo_ready, 1)

        @block.tensor
        def _(pe):
            with pe.Fori(0, groups) as g:
                for t in range(NT):
                    tok = slice(t * P, (t + 1) * P)
                    pe.wait_ge(psum_free, g * NT + (t + 1) + base["psum"])
                    for k in range(k_tiles):
                        if t == 0:
                            pe.wait_ge(lo_ready, g * k_tiles + (k + 1) + base["lo"])
                        nc.tensor.matmul(bank[:, t, :], x_hi[:, k, tok], w_hi[:, k, :], start=(k == 0), stop=False)
                        nc.tensor.matmul(bank[:, t, :], x_lo[:, k, tok], w_hi[:, k, :], start=False, stop=False)
                        last = nc.tensor.matmul(bank[:, t, :], x_hi[:, k, tok], w_lo[:, k, :],
                                                start=False, stop=(k == k_tiles - 1))
                        if t == NT - 1 and k < k_tiles - 1:
                            last.then_inc(slot_free, 1)
                    last.then_inc(summed, 1)
    sems.past(loaded=16 * groups, hi=groups * k_tiles, lo=groups * k_tiles, slot=groups * (k_tiles - 1),
              summed=groups * NT, psum=8 + groups * NT, stage=16 + 8 * groups * NT)


def condition(nc, sem, a, t, spare):
    ins_loaded = sem("vectors_loaded")
    x_loaded = [sem("x_first_loaded"), sem("x_second_loaded")]
    rows_loaded = sem("rows_loaded")
    pos_loaded = sem("positions_loaded")
    ada_loaded = [sem("ada_even_loaded"), sem("ada_odd_loaded")]
    silu_c_ready = sem("silu_c_ready")
    ada_step = sem("ada_step")
    mod_summed = sem("mod_summed")
    mod_ready = sem("mod_ready")
    squared = sem("x_squared")
    rms = sem("x_rms")
    rooted = sem("x_rooted")
    normed = sem("x_normed")
    turned = sem("x_turned")
    h_hi_ready = sem("h_hi_ready")
    h_full_ready = sem("h_full_ready")
    h_lo_ready = sem("h_lo_ready")
    table = sem("table_step")
    sines = sem("sines_ready")
    magnitude = sem("angle_magnitude")
    const_ready = sem("const_ready")
    consts_split = sem("consts_split")
    with ExitStack() as ctx:
        sb = lambda n, shape, dt=F32: ctx.enter_context(nc.sbuf_tensor(n, shape, dt))
        pb = lambda n, shape: ctx.enter_context(nc.psum_tensor(n, shape, F32))
        x_tok = sb("x_tok", [P, NT, D])
        junk = sb("junk", [P, D])
        causal_add = sb("causal_add", [P, P])
        ada = sb("ada", [P, 2, KD, HALF])
        acc = sb("ada_sum", [P, 3 * D])
        mod = sb("mod", [P, 16])
        ss = sb("x_sumsq", [P, NT])
        root = sb("x_root", [P, NT])
        rstd = sb("x_rstd", [P, NT])
        silu_c = sb("silu_c", [P, KD])
        h_full = junk[:, :].rearrange("p (a n) -> p a n", n=HALF)
        ang, mag, turns = spare[:, 0:2, :], spare[:, 2:4, :], spare[:, 4, :]
        pos_i = spare[:, 5, :].bitcast(I32)
        p_mod = pb("p_mod", [P, HALF])
        p_gate = pb("p_gate", [P, 2, HALF])
        p_x = pb("p_x", [P, 4, HALF])
        block = ctx.enter_context(nc.Block())

        @block.sync
        def _(sp):
            sp.dma_start(t["cols"][:, :], a["cols"]).then_inc(ins_loaded, 16)
            sp.dma_start(t["consts"][:, :], a["consts"]).then_inc(ins_loaded, 16)
            sp.dma_start(t["ident"][:, :], a["ident"]).then_inc(ins_loaded, 16)
            sp.dma_start(causal_add[:, :], a["causal_add"]).then_inc(ins_loaded, 16)
            sp.dma_start(t["causal_kq"][:, :], a["causal_kq"]).then_inc(ins_loaded, 16)
            sp.dma_start(pos_i, a["positions"].partition_broadcast(P)).then_inc(pos_loaded, 16)
            for n in range(6):
                if n >= 2:
                    sp.wait_ge(ada_step, KD * (n - 1))
                sp.dma_start(ada[:, n % 2, :, :], a["w_ada"][n]).then_inc(ada_loaded[n % 2], 16)
                if n in (0, 1):
                    sp.dma_start(x_tok[:, 4 * n:4 * n + 4, :],
                                 a["x"][4 * n:4 * n + 4].rearrange("t p d -> p t d")).then_inc(x_loaded[n], 16)
            sp.dma_start(t["gate"][:, :], a["b_gate"].partition_broadcast(P)).then_inc(rows_loaded, 16)
            sp.dma_start(t["g_final"][:, :], a["g_final"].partition_broadcast(P)).then_inc(rows_loaded, 16)

        @block.gpsimd
        def _(pool):
            nc.gpsimd.memset(t["ones"][:, :], 1.0).then_inc(const_ready, 1)

        @block.scalar
        def _(act):
            act.wait_ge(ins_loaded, 80)
            nc.scalar.activation(t["ident_r"][:, :], t["ident"][:, :], ACT.Copy).then_inc(consts_split, 1)
            nc.scalar.activation(t["causal_r"][:, :], causal_add[:, :], ACT.Copy).then_inc(consts_split, 1)
            nc.scalar.activation(silu_c[:, :], t["cols"][:, COL_C:COL_C + KD], ACT.Silu).then_inc(silu_c_ready, 1)
            for n in range(NT):
                act.wait_ge(x_loaded[n // 4], 16)
                if n:
                    act.wait_ge(squared, n)
                nc.scalar.activation(junk[:, :], x_tok[:, n, :], ACT.Square,
                                     accum_out=ss[:, n:n + 1]).then_inc(squared, 1)
            act.wait_ge(rms, 1)
            nc.scalar.activation(root[:, :], ss[:, :], ACT.Sqrt).then_inc(rooted, 1)
            for n, sin_out in enumerate((t["sin_ret"][:, 1, :], t["sin_mla"][:, :])):
                act.wait_ge(table, 7 * (n + 1))
                nc.scalar.activation(mag[:, n, :], ang[:, n, :], ACT.Abs).then_inc(magnitude, 1)
                nc.scalar.activation(sin_out, ang[:, n, :], ACT.Sin, scale=(
                    t["consts"][:, CC_SIGN:CC_SIGN + 1] if n else 1.0)).then_inc(sines, 1)
                act.wait_ge(magnitude, n + 1)
                nc.scalar.activation((t["cos_mla"] if n else t["cos_ret"])[:, :], mag[:, n, :], ACT.Sin, scale=-1.0,
                                     bias=t["consts"][:, CC_HALF_PI:CC_HALF_PI + 1]).then_inc(sines, 1)
            nc.scalar.activation(t["sin_ret"][:, 0, :], ang[:, 0, :], ACT.Sin, scale=-1.0).then_inc(sines, 1)
            act.wait_ge(mod_ready, 3)
            for m in range(2 * KD):
                half, k = divmod(m, KD)
                act.wait_ge(turned, m + 1)
                nc.scalar.activation(t["h_hi"][:, k, half * HALF:(half + 1) * HALF], p_x[:, m % 4, :], ACT.Identity,
                                     scale=mod[:, KD + k:KD + k + 1], bias=mod[:, k:k + 1]).then_inc(h_hi_ready, 1)

        @block.vector
        def _(dve):
            dve.wait_ge(ins_loaded, 80)
            dve.wait_ge(pos_loaded, 16)
            steps = [0]

            def chained(ins):
                steps[0] += 1
                ins.then_inc(table, 1)
                dve.wait_ge(table, steps[0])

            for n, col in enumerate((CC_FREQ_RET, CC_FREQ_MLA)):
                chained(nc.vector.tensor_scalar(ang[:, n, :], pos_i, t["consts"][:, col:col + 1], None,
                                                ALU.mult))
                chained(nc.vector.tensor_scalar(turns, ang[:, n, :], float(1 / (2 * np.pi)), ROUNDER,
                                                ALU.mult, ALU.add))
                chained(nc.vector.tensor_scalar(turns, turns, -ROUNDER, None, ALU.add))
                for part in (TURN_1, TURN_2, TURN_3):
                    chained(nc.vector.scalar_tensor_tensor(out=ang[:, n, :], in0=turns, scalar=-part,
                                                           in1=ang[:, n, :], op0=ALU.mult, op1=ALU.add))
                chained(nc.vector.tensor_scalar(ang[:, n, :], ang[:, n, :], PI_BELOW, -PI_BELOW, ALU.min, ALU.max))
            dve.wait_ge(silu_c_ready, 1)
            for n in range(6):
                dve.wait_ge(ada_loaded[n % 2], 16 * (n // 2 + 1))
                cut = slice(n * HALF, (n + 1) * HALF)
                for k in range(KD):
                    if k == 0:
                        ins = nc.vector.tensor_scalar(acc[:, cut], ada[:, n % 2, k, :], silu_c[:, 0:1], None, ALU.mult)
                    else:
                        ins = nc.vector.scalar_tensor_tensor(out=acc[:, cut], in0=ada[:, n % 2, k, :],
                                                             scalar=silu_c[:, k:k + 1], in1=acc[:, cut],
                                                             op0=ALU.mult, op1=ALU.add)
                    ins.then_inc(ada_step, 1)
                    dve.wait_ge(ada_step, n * KD + k + 1)
                if n == 0:
                    dve.wait_ge(squared, NT)
                    nc.vector.tensor_scalar(ss[:, :], ss[:, :], 1.0 / D, EPS, ALU.mult, ALU.add).then_inc(rms, 1)
                    dve.wait_ge(rooted, 1)
                    nc.vector.reciprocal(rstd[:, :], root[:, :]).then_inc(rms, 1)
                    dve.wait_ge(rms, 2)
                    for j in range(NT):
                        nc.vector.tensor_scalar(x_tok[:, j, :], x_tok[:, j, :], rstd[:, j:j + 1], None,
                                                ALU.mult).then_inc(normed, 1)
                if n == 3:
                    dve.wait_ge(mod_summed, 1)
                    nc.vector.tensor_tensor(mod[:, :], p_mod[:, 0:16], t["cols"][:, COL_BADA:COL_BADA + 16],
                                            ALU.add).then_inc(mod_ready, 1)
                    dve.wait_ge(mod_ready, 1)
                    nc.vector.tensor_scalar(mod[:, KD:], mod[:, KD:], 1.0, None, ALU.add).then_inc(mod_ready, 1)
                    dve.wait_ge(mod_ready, 2)
                    nc.vector.tensor_tensor(mod[:, KD:], mod[:, KD:], t["cols"][:, COL_GPRE:COL_GPRE + KD],
                                            ALU.mult).then_inc(mod_ready, 1)
                    dve.wait_ge(mod_ready, 3)
                    for m in range(2 * KD):
                        half, k = divmod(m, KD)
                        dve.wait_ge(turned, m + 1)
                        if m >= 2:
                            dve.wait_ge(h_lo_ready, m - 1)
                        dve.wait_ge(h_hi_ready, m + 1)
                        nc.vector.tensor_scalar(h_full[:, m % 2, :], p_x[:, m % 4, :], mod[:, KD + k:KD + k + 1],
                                                mod[:, k:k + 1], ALU.mult, ALU.add).then_inc(h_full_ready, 1)
                        dve.wait_ge(h_full_ready, m + 1)
                        cols = slice(half * HALF, (half + 1) * HALF)
                        nc.vector.tensor_tensor(t["h_lo"][:, k, cols], h_full[:, m % 2, :],
                                                t["h_hi"][:, k, cols].bitcast(F32), ALU.subtract).then_inc(h_lo_ready, 1)
            dve.wait_ge(rows_loaded, 32)
            dve.wait_ge(mod_summed, 2)
            nc.vector.tensor_tensor(t["gate"][:, :], t["gate"][:, :], p_gate[:, :, :].rearrange("p a n -> p (a n)"),
                                    ALU.add).then_inc(mod_ready, 1)

        @block.tensor
        def _(pe):
            pe.wait_ge(normed, NT)
            pe.wait_ge(const_ready, 1)

            def turn(m):
                half, k = divmod(m, KD)
                if m >= 4:
                    pe.wait_ge(h_lo_ready, m - 3)
                for j in range(4):
                    last = nc.tensor.transpose(p_x[:, m % 4, j * P:(j + 1) * P],
                                               x_tok[:, 4 * half + j, k * P:(k + 1) * P], t["ident"][:, :])
                last.then_inc(turned, 1)

            for m in range(4):
                turn(m)
            pe.wait_ge(ada_step, 4 * KD)
            for n in range(16):
                last = nc.tensor.matmul(p_mod[:, n:n + 1], acc[:, n * P:(n + 1) * P], t["ones"][:, 0:1],
                                        start=True, stop=True)
            last.then_inc(mod_summed, 1)
            for m in range(4, 2 * KD):
                turn(m)
            pe.wait_ge(ada_step, 6 * KD)
            for half in range(2):
                last = nc.tensor.matmul(p_gate[:, half, :], t["ones"][:, :],
                                        acc[:, 2 * D + half * HALF:2 * D + (half + 1) * HALF], start=True, stop=True)
            last.then_inc(mod_summed, 1)


def normalise_latents(nc, sem, t, latent, cq_hi, cq_lo, ckv_hi, ckv_lo):
    squared = sem("latent_squared")
    summed = sem("latent_summed")
    rooted = sem("latent_rooted")
    inverted = sem("latent_inverted")
    scaled = sem("latent_scaled")
    hi_ready = sem("latent_hi_ready")
    lo_ready = sem("latent_lo_ready")
    swapped = sem("k_pe_swapped")
    roped = sem("k_pe_roped")
    with ExitStack() as ctx:
        sb = lambda n, shape, dt=F32: ctx.enter_context(nc.sbuf_tensor(n, shape, dt))
        square = sb("latent_square", [P, KQ + KKV, S])
        root = sb("latent_root", [P, 2, S])
        swap = sb("k_pe_swap", [P, S])
        rope = sb("k_pe_rope", [P, S])
        sums = ctx.enter_context(nc.psum_tensor("latent_sums", [P, 2, 2, HALF], F32))
        block = ctx.enter_context(nc.Block())
        tiles = [(0, n) for n in range(KQ)] + [(1, n) for n in range(KKV)]
        K_PE = KQ + KKV

        @block.sync
        def _(sp):
            for q in range(4):
                sp.dma_start(swap[32 * q:32 * q + 32, :],
                             latent[32 * (q ^ 1):32 * (q ^ 1) + 32, K_PE, :]).then_inc(swapped, 16)

        @block.scalar
        def _(act):
            for n in range(KQ + KKV):
                nc.scalar.activation(square[:, n, :], latent[:, n, :], ACT.Square).then_inc(squared, 1)
            for b, rank in enumerate((Q_RANK, KV_RANK)):
                act.wait_ge(summed, b + 1)
                nc.scalar.activation(root[:, b, :], sums[:, b, :, :].rearrange("p a n -> p (a n)"), ACT.Sqrt,
                                     scale=1.0 / rank, bias=t["consts"][:, CC_EPS:CC_EPS + 1]).then_inc(rooted, 1)
            for i, (b, n) in enumerate(tiles):
                act.wait_ge(scaled, i + 1)
                gain = t["cols"][:, COL_GQ + i:COL_GQ + i + 1]
                hi = ckv_hi if b else cq_hi
                nc.scalar.activation(hi[:, n, :], latent[:, i, :], ACT.Copy, scale=gain).then_inc(hi_ready, 1)
            act.wait_ge(roped, 3)
            nc.scalar.activation(t["k_rope_hi"][:, :], rope[:, :], ACT.Copy).then_inc(hi_ready, 1)

        @block.tensor
        def _(pe):
            for b, (first, last) in enumerate(((0, KQ), (KQ, KQ + KKV))):
                pe.wait_ge(squared, last)
                for half in range(2):
                    for n in range(first, last):
                        ins = nc.tensor.matmul(sums[:, b, half, :], t["ones"][:, :],
                                               square[:, n, half * HALF:(half + 1) * HALF],
                                               start=(n == first), stop=(n == last - 1))
                ins.then_inc(summed, 1)

        @block.vector
        def _(dve):
            dve.wait_ge(swapped, 64)
            nc.vector.tensor_tensor(rope[:, :], latent[:, K_PE, :], t["cos_mla"][:, :], ALU.mult).then_inc(roped, 1)
            nc.vector.tensor_tensor(swap[:, :], swap[:, :], t["sin_mla"][:, :], ALU.mult).then_inc(roped, 1)
            dve.wait_ge(roped, 2)
            nc.vector.tensor_tensor(rope[:, :], rope[:, :], swap[:, :], ALU.add).then_inc(roped, 1)
            for b in range(2):
                dve.wait_ge(rooted, b + 1)
                nc.vector.reciprocal(root[:, b, :], root[:, b, :]).then_inc(inverted, 1)
            dve.wait_ge(inverted, 2)
            for i, (b, n) in enumerate(tiles):
                nc.vector.tensor_tensor(latent[:, i, :], latent[:, i, :], root[:, b, :], ALU.mult).then_inc(scaled, 1)
            for i, (b, n) in enumerate(tiles):
                dve.wait_ge(hi_ready, i + 1)
                gain = t["cols"][:, COL_GQ + i:COL_GQ + i + 1]
                hi, lo = (ckv_hi, ckv_lo) if b else (cq_hi, cq_lo)
                nc.vector.scalar_tensor_tensor(out=lo[:, n, :], in0=latent[:, i, :], scalar=gain,
                                               in1=hi[:, n, :].bitcast(F32), op0=ALU.mult,
                                               op1=ALU.subtract).then_inc(lo_ready, 1)
            dve.wait_ge(hi_ready, len(tiles) + 1)
            nc.vector.tensor_tensor(t["k_rope_lo"][:, :], rope[:, :], t["k_rope_hi"][:, :].bitcast(F32),
                                    ALU.subtract).then_inc(lo_ready, 1)


def attention(nc, sem, a, t, q_t, q_rope_t, k_t, v_tok, act_t, y_t):
    loaded = sem("head_loaded")
    gate_loaded = [sem("gate_even_loaded"), sem("gate_odd_loaded")]
    roped = sem("q_rope_step")
    hi_ready = sem("head_hi_ready")
    lo_ready = sem("head_lo_ready")
    score_done = sem("score_done")
    max_done = sem("max_done")
    neg_done = sem("neg_max_done")
    exp_done = sem("exp_done")
    recip_done = sem("recip_done")
    prob_done = sem("prob_done")
    turned = sem("prob_turned")
    pt_hi_ready = sem("pt_hi_ready")
    pt_lo_ready = sem("pt_lo_ready")
    pv_done = sem("pv_done")
    y_done = sem("y_done")
    stored = [sem("y_even_stored"), sem("y_odd_stored")]
    LOADS = 9
    CHUNKS = [1, 1, 1, 1, 2, 2, 2, 2]
    BEFORE = [sum(CHUNKS[:i]) for i in range(NT + 1)]
    PAIRS = NT // 2
    with ExitStack() as ctx:
        sb = lambda n, shape, dt=F32: ctx.enter_context(nc.sbuf_tensor(n, shape, dt))
        pb = lambda n, shape: ctx.enter_context(nc.psum_tensor(n, shape, F32))
        q_raw, k_raw = sb("q_raw", [P, S]), sb("k_raw", [P, S])
        v_raw = sb("v_raw", [P, NT, V_MLA])
        r_raw, r_swap, r_sum = sb("r_raw", [P, S]), sb("r_swap", [P, S]), sb("r_sum", [P, S])
        gate = sb("head_gate", [P, 2, S])
        q_hi, q_lo = sb("q_hi", [P, 2, S], F32R), sb("q_lo", [P, 2, S], F32R)
        k_hi, k_lo = sb("k_hi", [P, 2, S], F32R), sb("k_lo", [P, 2, S], F32R)
        v_hi, v_lo = sb("v_hi", [P, 2, NT, V_MLA], F32R), sb("v_lo", [P, 2, NT, V_MLA], F32R)
        q_rope = sb("q_rope", [P, 2, S], F32R)
        prob = sb("prob", [P, 4, S])
        pt_hi, pt_lo = sb("pt_hi", [P, 2, NT, 256], F32R), sb("pt_lo", [P, 2, NT, 256], F32R)
        y = sb("y_head", [P, 2, S])
        row_max, neg_max = sb("row_max", [P, 4]), sb("neg_max", [P, 4])
        row_sum, recip = sb("row_sum", [P, 4]), sb("recip", [P, 4])
        p_s = pb("p_scores", [P, 2, S])
        p_t = pb("p_turned", [P, 2, HALF])
        p_y = pb("p_y", [P, 2, HALF])
        block = ctx.enter_context(nc.Block())

        ROUNDS = H_MLA // 2

        @block.sync
        def _(sp):
            with sp.Fori(0, ROUNDS) as it:
                for s in range(2):
                    h = it * 2 + s

                    def head(ap, rows=slice(None)):
                        return one(ap, h).rearrange("a p n -> p (a n)")[rows]

                    sp.wait_ge(lo_ready, it * 8 + 4 * (s + 1))
                    sp.dma_start(q_raw[:, :], head(q_t)).then_inc(loaded, 16)
                    sp.dma_start(k_raw[:, :], head(k_t)).then_inc(loaded, 16)
                    sp.dma_start(v_raw[:, :, :], one(v_tok, h).rearrange("a p t n -> p (a t) n")).then_inc(loaded, 16)
                    for rep in range(2):
                        sp.dma_start(r_raw[64 * rep:64 * rep + 64, :], head(q_rope_t)).then_inc(loaded, 16)
                        for part in range(2):
                            row, src = 64 * rep + 32 * part, 32 * (1 - part)
                            sp.dma_start(r_swap[row:row + 32, :], head(q_rope_t, slice(src, src + 32)))\
                                .then_inc(loaded, 16)
                    sp.wait_ge(y_done, it * 8 + 4 * (s + 1))
                    sp.dma_start(gate[:, s, :], head(act_t)).then_inc(gate_loaded[s], 16)

        @block.gpsimd
        def _(pool):
            def rotate(it, s):
                pool.wait_ge(loaded, it * (2 * 16 * LOADS) + 16 * LOADS * (s + 1))
                nc.gpsimd.tensor_tensor(r_raw[:, :], r_raw[:, :], t["cos_mla"][:, :], ALU.mult).then_inc(roped, 1)
                nc.gpsimd.tensor_tensor(r_swap[:, :], r_swap[:, :], t["sin_mla"][:, :], ALU.mult).then_inc(roped, 1)
                pool.wait_ge(roped, it * 6 + (3 * s + 2))
                pool.wait_ge(lo_ready, it * 8 + 4 * (s + 1))
                nc.gpsimd.tensor_tensor(r_sum[:, :], r_raw[:, :], r_swap[:, :], ALU.add).then_inc(roped, 1)

            with pool.Fori(0, ROUNDS) as it:
                for s in range(2):
                    rotate(it, s)

        def prepare_hi(act, it, s, part):
            if part == 0:
                act.wait_ge(loaded, it * (2 * 16 * LOADS) + 16 * LOADS * (s + 1))
                act.wait_ge(pv_done, it * 8 + 4 * (s + 1))
            src, out = [(q_raw[:, :], q_hi[:, s, :]), (k_raw[:, :], k_hi[:, s, :]),
                        (r_sum[:, :], q_rope[:, s, :]), (v_raw[:, :, :], v_hi[:, s, :, :])][part]
            if part == 2:
                act.wait_ge(roped, it * 6 + 3 * (s + 1))
            nc.scalar.activation(out, src, ACT.Copy).then_inc(hi_ready, 1)

        def prepare_lo(dve, it, s, part):
            dve.wait_ge(hi_ready, it * 8 + (4 * s + part + 1))
            low = slice(64, 128)
            src, hi, out = [
                (q_raw[:, :], q_hi[:, s, :], q_lo[:, s, :]), (k_raw[:, :], k_hi[:, s, :], k_lo[:, s, :]),
                (r_sum[low, :], q_rope[low, s, :], q_rope[low, s, :]),
                (v_raw[:, :, :], v_hi[:, s, :, :], v_lo[:, s, :, :])][part]
            nc.vector.tensor_tensor(out, src, hi.bitcast(F32), ALU.subtract).then_inc(lo_ready, 1)

        STEPS = 2 * NT
        CH = 2 * BEFORE[NT]
        RP = 2 * PAIRS

        def chunks(m):
            i = m % NT
            return [(BEFORE[i] + (m // NT) * BEFORE[NT] + c, 4 * c, min(4, i + 1 - 4 * c)) for c in range(CHUNKS[i])]

        @block.scalar
        def _(act):
            for part in range(4):
                prepare_hi(act, 0, 0, part)
            for free in stored:
                act.sem_inc(free, 16)

            def store(it, s):
                act.wait_ge(y_done, it * RP + (RP + PAIRS * (s + 1)))
                act.dma_start(one(y_t, it * 2 + s).rearrange("a p n -> p (a n)"), y[:, s, :])\
                    .then_inc(stored[s], 16)

            def step(it, m, old, last):
                if old(m - 3) and m - 3 < STEPS:
                    r, b = lag(it, m - 3, STEPS)
                    pair = b // 2
                    off = (b % 2) * P
                    for c, j, count in chunks(b):
                        act.wait_ge(turned, r * CH + (c + 1))
                        if old(m - 3 - 4):
                            act.wait_ge(pv_done, r * RP + (RP + pair - 1))
                        nc.scalar.activation(pt_hi[:, pair % 2, j:j + count, off:off + P],
                                             p_t[:, c % 2, 0:count * P].rearrange("p (j n) -> p j n", n=P),
                                             ACT.Copy).then_inc(pt_hi_ready, 1)
                if m < STEPS:
                    width = (m % NT + 1) * P
                    slot = m % 4
                    act.wait_ge(neg_done, it * STEPS + (m + 1))
                    if old(m - 4):
                        r, b = lag(it, m - 4, STEPS)
                        act.wait_ge(turned, r * CH + (chunks(b)[-1][0] + 1))
                    nc.scalar.activation(prob[:, slot, 0:width], p_s[:, m % 2, 0:width], ACT.Exp,
                                         bias=neg_max[:, slot:slot + 1], scale=SCALE,
                                         accum_out=row_sum[:, slot:slot + 1]).then_inc(exp_done, 1)
                if 4 <= m % NT and m < STEPS and not (last and m >= NT):
                    prepare_hi(act, it + m // NT, 1 - m // NT, m % NT - 4)
                if m == 14:
                    store(it, 0)
                if m == 6 and old(-1):
                    store(it - 1, 1)

            pipelined(act, step, ROUNDS, STEPS, 5)
            store(ROUNDS - 1, 1)
            for free in stored:
                act.wait_ge(free, 16 + 8 * H_MLA)

        @block.vector
        def _(dve):
            dve.sem_inc(lo_ready, 4)
            dve.sem_inc(y_done, 2 * PAIRS)
            for part in range(4):
                prepare_lo(dve, 0, 0, part)

            def step(it, m, old, last):
                if m < STEPS:
                    cell = slice(m % 4, m % 4 + 1)
                    dve.wait_ge(score_done, it * STEPS + (m + 1))
                    nc.vector.reduce_max(row_max[:, cell], p_s[:, m % 2, 0:(m % NT + 1) * P], AX.X)\
                        .then_inc(max_done, 1)
                    dve.wait_ge(max_done, it * STEPS + (m + 1))
                    nc.vector.tensor_scalar(neg_max[:, cell], row_max[:, cell], -SCALE, None, ALU.mult)\
                        .then_inc(neg_done, 1)
                if old(m - 1) and m - 1 < STEPS:
                    r, b = lag(it, m - 1, STEPS)
                    cell = slice(b % 4, b % 4 + 1)
                    width = (b % NT + 1) * P
                    dve.wait_ge(exp_done, r * STEPS + (b + 1))
                    nc.vector.reciprocal(recip[:, cell], row_sum[:, cell]).then_inc(recip_done, 1)
                    dve.wait_ge(recip_done, r * STEPS + (b + 1))
                    nc.vector.tensor_scalar(prob[:, b % 4, 0:width], prob[:, b % 4, 0:width], recip[:, cell],
                                            None, ALU.mult).then_inc(prob_done, 1)
                if old(m - 3) and m - 3 < STEPS:
                    r, b = lag(it, m - 3, STEPS)
                    pair = b // 2
                    off = (b % 2) * P
                    for c, j, count in chunks(b):
                        dve.wait_ge(pt_hi_ready, r * CH + (c + 1))
                        nc.vector.tensor_tensor(pt_lo[:, pair % 2, j:j + count, off:off + P],
                                                p_t[:, c % 2, 0:count * P].rearrange("p (j n) -> p j n", n=P),
                                                pt_hi[:, pair % 2, j:j + count, off:off + P].bitcast(F32),
                                                ALU.subtract).then_inc(pt_lo_ready, 1)
                if m % 2 == 0 and old(m - 6):
                    r, pair = lag(it, (m - 6) // 2, RP)
                    s, p = divmod(pair, PAIRS)
                    dve.wait_ge(pv_done, r * RP + (RP + pair + 1))
                    if p == 0:
                        dve.wait_ge(stored[s], r * 16 + 16)
                        dve.wait_ge(gate_loaded[s], r * 16 + 16)
                    cut = slice(256 * p, 256 * p + 256)
                    nc.vector.tensor_tensor(y[:, s, cut], p_y[:, pair % 2, 0:256], gate[:, s, cut], ALU.mult)\
                        .then_inc(y_done, 1)
                if 4 <= m % NT and m < STEPS and not (last and m >= NT):
                    prepare_lo(dve, it + m // NT, 1 - m // NT, m % NT - 4)

            pipelined(dve, step, ROUNDS, STEPS, 5)

        @block.tensor
        def _(pe):
            pe.sem_inc(pv_done, 2 * PAIRS)

            def scores(it, m, old):
                s, i = divmod(m, NT)
                if i == 0:
                    pe.wait_ge(lo_ready, it * 8 + (4 + 4 * s + 3))
                if old(m - 2):
                    pe.wait_ge(exp_done, it * STEPS + (m - 1))
                q = slice(i * P, (i + 1) * P)
                for c in range(0, (i + 1) * P, HALF):
                    k = slice(c, min(c + HALF, (i + 1) * P))
                    out = p_s[:, m % 2, k]
                    diagonal = k.stop == (i + 1) * P
                    nc.tensor.matmul(out, q_hi[:, s, q], k_hi[:, s, k], start=True, stop=False)
                    nc.tensor.matmul(out, q_hi[:, s, q], k_lo[:, s, k], start=False, stop=False)
                    nc.tensor.matmul(out, q_lo[:, s, q], k_hi[:, s, k], start=False, stop=False)
                    nc.tensor.matmul(out, q_rope[:, s, q], t["k_rope_hi"][:, k], start=False, stop=False)
                    last = nc.tensor.matmul(out, q_rope[:, s, q], t["k_rope_lo"][:, k], start=False, stop=not diagonal)
                    if diagonal:
                        last = nc.tensor.matmul(p_s[:, m % 2, q], t["ident_r"][:, :], t["causal_r"][:, :],
                                                start=False, stop=True)
                last.then_inc(score_done, 1)

            def turn(it, m, old):
                pe.wait_ge(prob_done, it * STEPS + (m + 1))
                for c, j, count in chunks(m):
                    if c >= 2 or old(-1):
                        pe.wait_ge(pt_lo_ready, it * CH + (c - 1))
                    for b in range(count):
                        last = nc.tensor.transpose(p_t[:, c % 2, b * P:(b + 1) * P],
                                                   prob[:, m % 4, (j + b) * P:(j + b + 1) * P], t["ident"][:, :])
                    last.then_inc(turned, 1)

            def values(it, pair, old):
                s, p = divmod(pair, PAIRS)
                if p == 0:
                    pe.wait_ge(lo_ready, it * 8 + (4 + 4 * s + 4))
                pe.wait_ge(pt_lo_ready, it * CH + (chunks(2 * pair + 1)[-1][0] + 1))
                pe.wait_ge(y_done, it * RP + (RP + pair - 1))
                for j in range(2 * p + 2):
                    cols = slice(P if j == 2 * p + 1 else 0, 256)
                    out = p_y[:, pair % 2, cols]
                    nc.tensor.matmul(out, v_hi[:, s, j, :], pt_hi[:, pair % 2, j, cols], start=(j == 0), stop=False)
                    nc.tensor.matmul(out, v_hi[:, s, j, :], pt_lo[:, pair % 2, j, cols], start=False, stop=False)
                    last = nc.tensor.matmul(out, v_lo[:, s, j, :], pt_hi[:, pair % 2, j, cols], start=False,
                                            stop=(j == 2 * p + 1))
                last.then_inc(pv_done, 1)

            def step(it, m, old, last):
                if m < STEPS:
                    scores(it, m, old)
                if m % 2 == 1 and old(m - 5):
                    values(*lag(it, (m - 5) // 2, RP), old)
                if old(m - 2) and m - 2 < STEPS:
                    r, b = lag(it, m - 2, STEPS)
                    turn(r, b, (lambda x: False) if isinstance(r, int) and r == 0 else old)

            pipelined(pe, step, ROUNDS, STEPS, 5)


def retention(nc, sem, a, t, act_t, v_tok, y_t):
    loaded = [sem("chunk_loaded_%d" % m) for m in range(NT)]
    rotated = sem("chunk_rotated")
    added = sem("chunk_rope_added")
    decayed = sem("chunk_decayed")
    qk_hi_ready = sem("qk_hi_ready")
    qk_lo_ready = sem("qk_lo_ready")
    v_hi_ready = sem("v_hi_ready")
    v_lo_ready = sem("v_lo_ready")
    k_turned = sem("k_turned")
    k_hi_ready = sem("k_tok_hi_ready")
    k_lo_ready = sem("k_tok_lo_ready")
    inner_done = sem("inner_scores_done")
    masked = sem("inner_scores_masked")
    i_hi_ready = sem("inner_hi_ready")
    i_lo_ready = sem("inner_lo_ready")
    out_done = sem("out_done")
    state_done = sem("state_done")
    r_hi_ready = sem("state_hi_ready")
    r_lo_ready = sem("state_lo_ready")
    stats_done = sem("stats_done")
    rooted = sem("out_rooted")
    normed = sem("out_normed")
    out_turned = sem("out_turned")
    y_done = sem("chunk_y_done")
    stored = [sem("chunk_y_even_stored"), sem("chunk_y_odd_stored")]
    C = NT
    LOADED = 5 * 16
    with ExitStack() as ctx:
        sb = lambda n, shape, dt=F32: ctx.enter_context(nc.sbuf_tensor(n, shape, dt))
        pb = lambda n, shape: ctx.enter_context(nc.psum_tensor(n, shape, F32))
        x = sb("qk_raw", [P, C, 2, 2, P])
        decay = sb("decay", [P, C, 2, P])
        v_raw = sb("v_chunk", [P, C, RET_V])
        gate = sb("gate_chunk", [P, C, 4, P])
        rot = sb("rot", [P, 4, 2, 2, P])
        cross = sb("rot_cross", [P, 4, 2, 2, P])
        qk_hi, qk_lo = sb("qk_hi", [P, 4, 2, 2, P], F32R), sb("qk_lo", [P, 4, 2, 2, P], F32R)
        v_hi, v_lo = sb("vr_hi", [P, 4, RET_V], F32R), sb("vr_lo", [P, 4, RET_V], F32R)
        k_hi, k_lo = sb("k_tok_hi", [P, 4, RET_QK], F32R), sb("k_tok_lo", [P, 4, RET_QK], F32R)
        inner = sb("inner", [P, 2, P])
        i_hi, i_lo = sb("inner_hi", [P, 4, P], F32R), sb("inner_lo", [P, 4, P], F32R)
        r_hi, r_lo = sb("state_hi", [P, 2, RET_V], F32R), sb("state_lo", [P, 2, RET_V], F32R)
        out_n = sb("out_n", [P, 2, RET_V])
        y = sb("y_chunk", [P, 2, 4, P])
        stats, mean_var = sb("stats", [P, 2, 6]), sb("mean_var", [P, 2, 2])
        root, rstd, shift = sb("root_r", [P, 2]), sb("rstd_r", [P, 2]), sb("shift_r", [P, 2])
        carrier = sb("carrier", [P, 1])
        p_k = pb("p_k_tok", [P, HALF])
        p_i = pb("p_inner", [P, HALF])
        p_o = pb("p_out", [P, 2, HALF])
        p_r = pb("p_state", [P, 2, HALF])
        p_y = pb("p_y_turned", [P, 2, HALF])
        block = ctx.enter_context(nc.Block())

        def two_tiles(tile, h, m):
            return act_t[bass.ds(h * 2 + tile, 2)].rearrange("a p n -> p a n")[:, :, m * P:(m + 1) * P]

        def four_tiles(ap, tile, h, m):
            return ap[bass.ds(h * 4 + tile, 4)].rearrange("a p n -> p a n")[:, :, m * P:(m + 1) * P]

        @block.sync
        def _(sp):
            def load(h, m):
                sp.dma_start(x[:, m, 0, :, :], two_tiles(Q_RET, h, m)).then_inc(loaded[m], 16)
                sp.dma_start(x[:, m, 1, :, :], two_tiles(K_RET, h, m)).then_inc(loaded[m], 16)
                sp.dma_start(decay[:, m, :, :], one(a["decay"], h)[:, :, m * P:(m + 1) * P]
                             .rearrange("a b n -> (a b) n").partition_broadcast(P)).then_inc(loaded[m], 16)
                sp.dma_start(v_raw[:, m, :], one(v_tok, h).rearrange("a p t n -> p (a t) n")[:, m, :])\
                    .then_inc(loaded[m], 16)
                sp.dma_start(gate[:, m, :, :], four_tiles(act_t, GATE_RET, h, m)).then_inc(loaded[m], 16)

            def body(h, is_last):
                for m in range(C):
                    sp.wait_ge(y_done, h * C + (m + 1))
                    sp.dma_start(four_tiles(y_t, 0, h, m), y[:, m % 2, :, :]).then_inc(stored[m % 2], 16)
                    if not is_last:
                        load(h + 1, m)

            for free in stored:
                sp.sem_inc(free, 16)
            for m in range(C):
                load(0, m)
            with sp.Fori(0, H_RET - 1) as h:
                body(h, False)
            body(H_RET - 1, True)
            for free in stored:
                sp.wait_ge(free, 16 + 8 * H_RET * C)

        @block.gpsimd
        def _(pool):
            def step(h, m, old, last):
                s = m % 4
                tok = slice(m * P, (m + 1) * P)
                pool.wait_ge(loaded[m], h * LOADED + LOADED)
                if old(m - 4):
                    pool.wait_ge(k_turned, h * C + (m - 3))
                nc.gpsimd.tensor_tensor(
                    rot[:, s, :, :, :].rearrange("p a b n -> p (a b) n"),
                    x[:, m, :, :, :].rearrange("p a b n -> p (a b) n"),
                    t["cos_ret"][:, tok].unsqueeze(1).broadcast_to([P, 4, P]), ALU.mult).then_inc(rotated, 1)
                for b in range(2):
                    nc.gpsimd.tensor_tensor(
                        cross[:, s, :, b, :], x[:, m, :, 1 - b, :],
                        t["sin_ret"][:, b, tok].unsqueeze(1).broadcast_to([P, 2, P]), ALU.mult).then_inc(rotated, 1)
                pool.wait_ge(v_hi_ready, h * C + (m + 1))
                nc.gpsimd.tensor_tensor(v_lo[:, s, :], v_raw[:, m, :], v_hi[:, s, :].bitcast(F32),
                                        ALU.subtract).then_inc(v_lo_ready, 1)

            pipelined(pool, step, H_RET, C, 0)

        @block.scalar
        def _(act):
            def step(h, m, old, last):
                if old(m - 4) and m - 4 < C:
                    g, b = lag(h, m - 4, C)
                    s = b % 2
                    cell = slice(s, s + 1)
                    if b < C - 1:
                        act.wait_ge(state_done, g * (C - 1) + (b + 1))
                        for half in range(2):
                            nc.scalar.activation(r_hi[:, half, :], p_r[:, half, :], ACT.Copy).then_inc(r_hi_ready, 1)
                    act.wait_ge(stats_done, g * (4 * C) + (4 * b + 2))
                    nc.scalar.activation(root[:, cell], mean_var[:, s, 1:2], ACT.Sqrt,
                                         bias=t["consts"][:, CC_EPS:CC_EPS + 1]).then_inc(rooted, 1)
                    act.wait_ge(stats_done, g * (4 * C) + (4 * b + 4))
                    nc.scalar.activation(out_n[:, s, :], p_o[:, s, :], ACT.Identity, scale=rstd[:, cell],
                                         bias=shift[:, cell]).then_inc(normed, 1)
                if old(m - 2) and m - 2 < C:
                    g, b = lag(h, m - 2, C)
                    act.wait_ge(k_turned, g * C + (b + 1))
                    nc.scalar.activation(k_hi[:, b % 4, :], p_k[:, 0:RET_QK], ACT.Copy).then_inc(k_hi_ready, 1)
                    act.wait_ge(masked, g * C + (b + 1))
                    nc.scalar.activation(i_hi[:, b % 4, :], inner[:, b % 2, :], ACT.Copy).then_inc(i_hi_ready, 1)
                if m < C:
                    act.wait_ge(loaded[m], h * LOADED + LOADED)
                    nc.scalar.activation(v_hi[:, m % 4, :], v_raw[:, m, :], ACT.Copy).then_inc(v_hi_ready, 1)
                    act.wait_ge(decayed, h * C + (m + 1))
                    nc.scalar.activation(qk_hi[:, m % 4, :, :, :], rot[:, m % 4, :, :, :], ACT.Copy)\
                        .then_inc(qk_hi_ready, 1)

            pipelined(act, step, H_RET, C, 4)

        @block.vector
        def _(dve):
            def step(h, m, old, last):
                if old(m - 4) and m - 4 < C:
                    g, b = lag(h, m - 4, C)
                    s = b % 2
                    cell = slice(s, s + 1)
                    dve.wait_ge(out_done, g * C + (b + 1))
                    nc.vector.bn_stats(stats[:, s, :], p_o[:, s, :]).then_inc(stats_done, 1)
                    dve.wait_ge(stats_done, g * (4 * C) + (4 * b + 1))
                    nc.vector.memset(carrier[:, :], 0.0)
                    nc.vector.bn_aggr(mean_var[:, s, :], stats[:, s, :]).then_inc(stats_done, 1)
                    if b < C - 1:
                        for half in range(2):
                            dve.wait_ge(r_hi_ready, g * (2 * (C - 1)) + (2 * b + half + 1))
                            nc.vector.tensor_tensor(r_lo[:, half, :], p_r[:, half, :], r_hi[:, half, :].bitcast(F32),
                                                    ALU.subtract).then_inc(r_lo_ready, 1)
                    dve.wait_ge(rooted, g * C + (b + 1))
                    nc.vector.reciprocal(rstd[:, cell], root[:, cell]).then_inc(stats_done, 1)
                    dve.wait_ge(stats_done, g * (4 * C) + (4 * b + 3))
                    nc.vector.tensor_scalar(shift[:, cell], mean_var[:, s, 0:1], -1.0, rstd[:, cell],
                                            ALU.mult, ALU.mult).then_inc(stats_done, 1)
                if old(m - 2) and m - 2 < C:
                    g, b = lag(h, m - 2, C)
                    dve.wait_ge(inner_done, g * C + (b + 1))
                    nc.vector.tensor_tensor(inner[:, b % 2, :], p_i[:, 0:P], t["causal_kq"][:, :], ALU.mult)\
                        .then_inc(masked, 1)
                    dve.wait_ge(k_hi_ready, g * C + (b + 1))
                    nc.vector.tensor_tensor(k_lo[:, b % 4, :], p_k[:, 0:RET_QK], k_hi[:, b % 4, :].bitcast(F32),
                                            ALU.subtract).then_inc(k_lo_ready, 1)
                if old(m - 3) and m - 3 < C:
                    g, b = lag(h, m - 3, C)
                    dve.wait_ge(i_hi_ready, g * C + (b + 1))
                    nc.vector.tensor_tensor(i_lo[:, b % 4, :], inner[:, b % 2, :], i_hi[:, b % 4, :].bitcast(F32),
                                            ALU.subtract).then_inc(i_lo_ready, 1)
                if m < C:
                    s = m % 4
                    dve.wait_ge(rotated, h * (3 * C) + 3 * (m + 1))
                    nc.vector.tensor_tensor(rot[:, s, :, :, :], rot[:, s, :, :, :], cross[:, s, :, :, :], ALU.add)\
                        .then_inc(added, 1)
                    dve.wait_ge(added, h * C + (m + 1))
                    nc.vector.tensor_tensor(rot[:, s, :, :, :], rot[:, s, :, :, :],
                                            decay[:, m, :, :].unsqueeze(2).broadcast_to([P, 2, 2, P]),
                                            ALU.mult).then_inc(decayed, 1)
                if old(m - 5) and m - 5 < C:
                    g, b = lag(h, m - 5, C)
                    dve.wait_ge(out_turned, g * C + (b + 1))
                    dve.wait_ge(loaded[b], g * LOADED + LOADED)
                    dve.wait_ge(stored[b % 2], g * (8 * C) + 16 * (b // 2 + 1))
                    nc.vector.tensor_tensor(y[:, b % 2, :, :], p_y[:, b % 2, :].rearrange("p (a n) -> p a n", n=P),
                                            gate[:, b, :, :], ALU.mult).then_inc(y_done, 1)
                if old(m - 1) and m - 1 < C:
                    g, b = lag(h, m - 1, C)
                    dve.wait_ge(qk_hi_ready, g * C + (b + 1))
                    nc.vector.tensor_tensor(qk_lo[:, b % 4, :, :, :], rot[:, b % 4, :, :, :],
                                            qk_hi[:, b % 4, :, :, :].bitcast(F32), ALU.subtract).then_inc(qk_lo_ready, 1)

            pipelined(dve, step, H_RET, C, 5)

        @block.tensor
        def _(pe):
            def outputs(h, m, old):
                s = m % 4
                pe.wait_ge(v_lo_ready, h * C + (m + 1))
                pe.wait_ge(i_lo_ready, h * C + (m + 1))
                if old:
                    pe.wait_ge(normed, h * C + (m - 1))
                out = p_o[:, m % 2, :]
                nc.tensor.matmul(out, i_hi[:, s, :], v_hi[:, s, :], start=True, stop=False)
                nc.tensor.matmul(out, i_hi[:, s, :], v_lo[:, s, :], start=False, stop=False)
                last = nc.tensor.matmul(out, i_lo[:, s, :], v_hi[:, s, :], start=False, stop=(m == 0))
                if m:
                    for b in range(2):
                        pe.wait_ge(r_lo_ready, h * (2 * (C - 1)) + (2 * (m - 1) + b + 1))
                        nc.tensor.matmul(out, qk_hi[:, s, 0, b, :], r_hi[:, b, :], start=False, stop=False)
                        nc.tensor.matmul(out, qk_lo[:, s, 0, b, :], r_hi[:, b, :], start=False, stop=False)
                        last = nc.tensor.matmul(out, qk_hi[:, s, 0, b, :], r_lo[:, b, :], start=False, stop=(b == 1))
                last.then_inc(out_done, 1)
                if m == C - 1:
                    return
                pe.wait_ge(k_lo_ready, h * C + (m + 1))
                for b in range(2):
                    cut = slice(b * P, (b + 1) * P)
                    out = p_r[:, b, :]
                    nc.tensor.matmul(out, k_hi[:, s, cut], v_hi[:, s, :], start=(m == 0), stop=False,
                                     skip_group_check=True)
                    nc.tensor.matmul(out, k_hi[:, s, cut], v_lo[:, s, :], start=False, stop=False,
                                     skip_group_check=True)
                    last = nc.tensor.matmul(out, k_lo[:, s, cut], v_hi[:, s, :], start=False, stop=True,
                                            skip_group_check=True)
                last.then_inc(state_done, 1)

            def inner_scores(h, m, old):
                s = m % 4
                pe.wait_ge(qk_lo_ready, h * C + (m + 1))
                if old:
                    pe.wait_ge(k_lo_ready, h * C + m)
                for b in range(2):
                    last = nc.tensor.transpose(p_k[:, b * P:(b + 1) * P], rot[:, s, 1, b, :], t["ident"][:, :])
                last.then_inc(k_turned, 1)
                if old:
                    pe.wait_ge(masked, h * C + m)
                for b in range(2):
                    out = p_i[:, 0:P]
                    nc.tensor.matmul(out, qk_hi[:, s, 1, b, :], qk_hi[:, s, 0, b, :], start=(b == 0), stop=False)
                    nc.tensor.matmul(out, qk_hi[:, s, 1, b, :], qk_lo[:, s, 0, b, :], start=False, stop=False)
                    last = nc.tensor.matmul(out, qk_lo[:, s, 1, b, :], qk_hi[:, s, 0, b, :], start=False,
                                            stop=(b == 1))
                last.then_inc(inner_done, 1)

            def step(h, m, old, last):
                if old(m - 4) and m - 4 < C:
                    outputs(*lag(h, m - 4, C), old(m - 6))
                if old(m - 2) and m - 2 < C:
                    inner_scores(*lag(h, m - 2, C), old(m - 3))
                if old(m - 5) and m - 5 < C:
                    g, b = lag(h, m - 5, C)
                    pe.wait_ge(normed, g * C + (b + 1))
                    if old(m - 7):
                        pe.wait_ge(y_done, g * C + (b - 1))
                    for j in range(4):
                        ins = nc.tensor.transpose(p_y[:, b % 2, j * P:(j + 1) * P],
                                                  out_n[:, b % 2, j * P:(j + 1) * P], t["ident"][:, :])
                    ins.then_inc(out_turned, 1)

            pipelined(pe, step, H_RET, C, 5)


def merge(nc, sem, a, t, weights, y_mla, y_ret, act_t, merged):
    y_loaded = [sem("y_even_loaded"), sem("y_odd_loaded")]
    y_hi_ready = sem("y_hi_ready")
    y_lo_ready = sem("y_lo_ready")
    loaded = sem("proj_w_loaded")
    hi_ready = sem("proj_w_hi_ready")
    lo_ready = sem("proj_w_lo_ready")
    summed = sem("proj_summed")
    gate_loaded = [sem("merge_gate_even_loaded"), sem("merge_gate_odd_loaded")]
    step = sem("merge_step")
    psum_free = sem("proj_psum_free")
    SETS, RING, PAIRS = 3, 12, KD // 2
    with ExitStack() as ctx:
        sb = lambda n, shape, dt=F32: ctx.enter_context(nc.sbuf_tensor(n, shape, dt))
        y_raw = sb("y_raw", [P, 2, S])
        y_hi, y_lo = sb("y_hi", [P, RING, S], F32R), sb("y_lo", [P, RING, S], F32R)
        raw = sb("proj_raw", [P, KD, 2 * P])
        w_hi, w_lo = sb("proj_hi", [P, KD, 2 * P], F32R), sb("proj_lo", [P, KD, 2 * P], F32R)
        gate = sb("merge_gate", [P, 2, S])
        part = sb("merge_part", [P, 2, S])
        psum = ctx.enter_context(nc.psum_tensor("p_proj", [P, 4, S], F32))
        block = ctx.enter_context(nc.Block())

        def gain(i):
            return t["cols"][:, COL_GRET + i:COL_GRET + i + 1] if i < 2 * KD else None

        @block.gpsimd
        def _(pool):
            for i in range(SETS * KD):
                if i >= 2:
                    pool.wait_ge(y_lo_ready, i - 1)
                src = y_ret[i] if i < 2 * KD else y_mla[i - 2 * KD]
                pool.dma_start(y_raw[:, i % 2, :], src).then_inc(y_loaded[i % 2], 16)

        @block.sync
        def _(sp):
            sp.dma_start(raw[:, :, :], weights[0]).then_inc(loaded, 16)
            for z in range(SETS):
                def body(g, is_last):
                    if z:
                        for j in range(2):
                            sp.wait_ge(psum_free, g * 2 + (z * KD + j + 1))
                            sp.dma_start(gate[:, j, :], one(act_t, g * 2 + (j + (MERGE_RET if z == 1 else MERGE_MLA)))
                                         .rearrange("a p n -> p (a n)")).then_inc(gate_loaded[j], 16)
                    if not is_last or z < SETS - 1:
                        sp.wait_ge(lo_ready, g * 2 + (2 * PAIRS * z + 2))
                        sp.dma_start(raw[:, :, :], one(weights, g + (z * PAIRS + 1))
                                     .rearrange("a p k n -> p (a k) n")).then_inc(loaded, 16)

                with sp.Fori(0, PAIRS - 1) as g:
                    body(g, False)
                body(PAIRS - 1, True)

        @block.scalar
        def _(act):
            def split_y(i):
                act.wait_ge(y_loaded[i % 2], 16 * (i // 2 + 1))
                scale = gain(i)
                nc.scalar.activation(y_hi[:, i % RING, :], y_raw[:, i % 2, :], ACT.Copy,
                                     scale=1.0 if scale is None else scale).then_inc(y_hi_ready, 1)

            def split_w(z, g, j, first=False):
                if not first:
                    act.wait_ge(summed, g * 2 + (z * KD + j + 1))
                    if j == 0:
                        act.wait_ge(loaded, g * 16 + 16 * (z * PAIRS + 2))
                cut = slice(j * P, (j + 1) * P)
                nc.scalar.activation(w_hi[:, :, cut], raw[:, :, cut], ACT.Copy).then_inc(hi_ready, 1)

            act.wait_ge(loaded, 16)
            split_w(0, 0, 0, first=True)
            for k in range(KD):
                split_y(k)
            split_w(0, 0, 1, first=True)
            for z in range(SETS):
                with act.Fori(0, PAIRS - 1) as g:
                    for j in range(2):
                        split_w(z, g, j)
                if z < SETS - 1:
                    for k in range(4):
                        split_y((z + 1) * KD + k)
                    for j in range(2):
                        split_w(z, PAIRS - 1, j)
                    for k in range(4, KD):
                        split_y((z + 1) * KD + k)

        @block.vector
        def _(dve):
            def low_y(i):
                dve.wait_ge(y_hi_ready, i + 1)
                slot = i % RING
                if gain(i) is None:
                    ins = nc.vector.tensor_tensor(y_lo[:, slot, :], y_raw[:, i % 2, :],
                                                  y_hi[:, slot, :].bitcast(F32), ALU.subtract)
                else:
                    ins = nc.vector.scalar_tensor_tensor(out=y_lo[:, slot, :], in0=y_raw[:, i % 2, :], scalar=gain(i),
                                                         in1=y_hi[:, slot, :].bitcast(F32), op0=ALU.mult,
                                                         op1=ALU.subtract)
                ins.then_inc(y_lo_ready, 1)

            def low_w(z, g, j, ahead=1):
                dve.wait_ge(hi_ready, g * 2 + (2 * PAIRS * z + 2 * ahead + j + 1))
                cut = slice(j * P, (j + 1) * P)
                nc.vector.tensor_tensor(w_lo[:, :, cut], raw[:, :, cut], w_hi[:, :, cut].bitcast(F32),
                                        ALU.subtract).then_inc(lo_ready, 1)

            def evacuate(z, g, j):
                out = merged[:, bass.ds(g * 2 + j, 1), :].rearrange("p a n -> p (a n)")
                dve.wait_ge(summed, g * 2 + (z * KD + j + 1))
                if z == 0:
                    nc.vector.tensor_copy(out, psum[:, j, :]).then_inc(psum_free, 1)
                    return
                dve.wait_ge(gate_loaded[j], g * 16 + 16 * ((z - 1) * PAIRS + 1))
                if z == 1:
                    nc.vector.tensor_tensor(part[:, j, :], psum[:, j, :], out, ALU.add).then_inc(step, 1)
                    dve.wait_ge(step, g * 2 + ((z - 1) * KD + j + 1))
                    nc.vector.tensor_tensor(out, part[:, j, :], gate[:, j, :], ALU.mult).then_inc(psum_free, 1)
                else:
                    nc.vector.tensor_tensor(part[:, j, :], psum[:, j, :], gate[:, j, :], ALU.mult).then_inc(step, 1)
                    dve.wait_ge(step, g * 2 + ((z - 1) * KD + j + 1))
                    nc.vector.tensor_tensor(out, part[:, j, :], out, ALU.add).then_inc(psum_free, 1)

            dve.sem_inc(psum_free, 2)
            low_w(0, 0, 0, ahead=0)
            for k in range(KD):
                low_y(k)
            low_w(0, 0, 1, ahead=0)
            for z in range(SETS):
                with dve.Fori(0, PAIRS - 1) as g:
                    for j in range(2):
                        evacuate(z, g, j)
                        low_w(z, g, j)
                if z < SETS - 1:
                    for k in range(4):
                        low_y((z + 1) * KD + k)
                for j in range(2):
                    evacuate(z, PAIRS - 1, j)
                    if z < SETS - 1:
                        low_w(z, PAIRS - 1, j)
                if z < SETS - 1:
                    for k in range(4, KD):
                        low_y((z + 1) * KD + k)

        @block.tensor
        def _(pe):
            def tile(z, g, j, first=False):
                cut = slice(j * P, (j + 1) * P)
                pe.wait_ge(lo_ready, g * 2 + (2 * PAIRS * z + j + 1))
                pe.wait_ge(psum_free, g * 2 + (z * KD + j + 1))
                for half in range(2):
                    out = psum[:, j, half * HALF:(half + 1) * HALF]
                    tok = slice(half * HALF, (half + 1) * HALF)
                    for k in range(KD):
                        slot = (z * KD + k) % RING
                        if first and half == 0:
                            pe.wait_ge(y_lo_ready, z * KD + k + 1)
                        nc.tensor.matmul(out, w_hi[:, k, cut], y_hi[:, slot, tok], start=(k == 0), stop=False)
                        nc.tensor.matmul(out, w_hi[:, k, cut], y_lo[:, slot, tok], start=False, stop=False)
                        last = nc.tensor.matmul(out, w_lo[:, k, cut], y_hi[:, slot, tok], start=False,
                                                stop=(k == KD - 1))
                last.then_inc(summed, 1)

            for z in range(SETS):
                for j in range(2):
                    tile(z, 0, j, first=(j == 0))
                with pe.Fori(1, PAIRS) as g:
                    for j in range(2):
                        tile(z, g, j)


def output(nc, sem, a, t, w_out, merged, out):
    w_loaded = [sem("out_w_even_loaded"), sem("out_w_odd_loaded")]
    x_loaded = [sem("residual_even_loaded"), sem("residual_odd_loaded")]
    m_hi_ready = sem("merged_hi_ready")
    m_lo_ready = sem("merged_lo_ready")
    w_hi_ready = sem("out_w_hi_ready")
    w_lo_ready = sem("out_w_lo_ready")
    summed = sem("out_summed")
    gated = sem("out_gated")
    added = sem("out_added")
    squared = sem("out_squared")
    meaned = sem("out_meaned")
    rooted = sem("out_root_ready")
    inverted = sem("out_inverted")
    finished = sem("out_finished")
    stored = [sem("out_even_stored"), sem("out_odd_stored")]
    with ExitStack() as ctx:
        sb = lambda n, shape, dt=F32: ctx.enter_context(nc.sbuf_tensor(n, shape, dt))
        m_hi, m_lo = sb("m_hi", [P, KD, S], F32R), sb("m_lo", [P, KD, S], F32R)
        w_raw = sb("out_raw", [P, 2, D])
        w_hi, w_lo = sb("out_hi", [P, KD, D], F32R), sb("out_lo", [P, KD, D], F32R)
        x = sb("residual", [P, 2, D])
        y = sb("out_y", [P, 2, D])
        ss, root, rstd = sb("out_ss", [P, 2]), sb("out_root", [P, 2]), sb("out_rstd", [P, 2])
        psum = ctx.enter_context(nc.psum_tensor("p_final", [P, 4, D], F32))
        block = ctx.enter_context(nc.Block())

        @block.sync
        def _(sp):
            for k in range(KD):
                if k >= 2:
                    sp.wait_ge(w_lo_ready, k - 1)
                sp.dma_start(w_raw[:, k % 2, :], w_out[k]).then_inc(w_loaded[k % 2], 16)
            for n in range(NT):
                if n >= 2:
                    sp.wait_ge(stored[n % 2], 16 * (n // 2))
                sp.dma_start(x[:, n % 2, :], a["x"][n]).then_inc(x_loaded[n % 2], 16)

        @block.gpsimd
        def _(pool):
            for n in range(NT):
                pool.wait_ge(finished, n + 1)
                pool.dma_start(out[n * P:(n + 1) * P, :], x[:, n % 2, :]).then_inc(stored[n % 2], 16)
            for done in stored:
                pool.wait_ge(done, 8 * NT)

        @block.scalar
        def _(act):
            for k in range(KD):
                nc.scalar.activation(m_hi[:, k, :], merged[:, k, :], ACT.Copy).then_inc(m_hi_ready, 1)
                act.wait_ge(w_loaded[k % 2], 16 * (k // 2 + 1))
                nc.scalar.activation(w_hi[:, k, :], w_raw[:, k % 2, :], ACT.Copy).then_inc(w_hi_ready, 1)
            for n in range(NT):
                s = n % 2
                act.wait_ge(added, n + 1)
                nc.scalar.activation(psum[:, n % 4, :], y[:, s, :], ACT.Square, accum_out=ss[:, s:s + 1])\
                    .then_inc(squared, 1)
                act.wait_ge(meaned, n + 1)
                nc.scalar.activation(root[:, s:s + 1], ss[:, s:s + 1], ACT.Sqrt).then_inc(rooted, 1)

        @block.vector
        def _(dve):
            for k in range(KD):
                dve.wait_ge(m_hi_ready, k + 1)
                nc.vector.tensor_tensor(m_lo[:, k, :], merged[:, k, :], m_hi[:, k, :].bitcast(F32),
                                        ALU.subtract).then_inc(m_lo_ready, 1)
                dve.wait_ge(w_hi_ready, k + 1)
                nc.vector.tensor_tensor(w_lo[:, k, :], w_raw[:, k % 2, :], w_hi[:, k, :].bitcast(F32),
                                        ALU.subtract).then_inc(w_lo_ready, 1)
            for n in range(NT):
                s = n % 2
                dve.wait_ge(summed, n + 1)
                nc.vector.tensor_tensor(y[:, s, :], psum[:, n % 4, :], t["gate"][:, :], ALU.mult).then_inc(gated, 1)
                dve.wait_ge(gated, n + 1)
                dve.wait_ge(x_loaded[s], 16 * (n // 2 + 1))
                nc.vector.tensor_tensor(y[:, s, :], y[:, s, :], x[:, s, :], ALU.add).then_inc(added, 1)
                dve.wait_ge(squared, n + 1)
                nc.vector.tensor_scalar(ss[:, s:s + 1], ss[:, s:s + 1], 1.0 / D, EPS, ALU.mult, ALU.add)\
                    .then_inc(meaned, 1)
                dve.wait_ge(rooted, n + 1)
                nc.vector.reciprocal(rstd[:, s:s + 1], root[:, s:s + 1]).then_inc(inverted, 1)
                dve.wait_ge(inverted, n + 1)
                nc.vector.scalar_tensor_tensor(out=x[:, s, :], in0=y[:, s, :], scalar=rstd[:, s:s + 1],
                                               in1=t["g_final"][:, :], op0=ALU.mult, op1=ALU.mult).then_inc(finished, 1)

        @block.tensor
        def _(pe):
            for n in range(NT):
                tok = slice(n * P, (n + 1) * P)
                if n >= 4:
                    pe.wait_ge(rooted, n - 3)
                for half in range(2):
                    cut = slice(half * HALF, (half + 1) * HALF)
                    for k in range(KD):
                        if n == 0 and half == 0:
                            pe.wait_ge(m_lo_ready, k + 1)
                            pe.wait_ge(w_lo_ready, k + 1)
                        res = psum[:, n % 4, cut]
                        nc.tensor.matmul(res, m_hi[:, k, tok], w_hi[:, k, cut], start=(k == 0), stop=False)
                        nc.tensor.matmul(res, m_hi[:, k, tok], w_lo[:, k, cut], start=False, stop=False)
                        last = nc.tensor.matmul(res, m_lo[:, k, tok], w_hi[:, k, cut], start=False, stop=(k == KD - 1))
                last.then_inc(summed, 1)


def build(nc, a, out):
    with ExitStack() as ctx:
        def sem(name):
            return ctx.enter_context(nc.semaphore(name))

        def sb(name, shape, dt=F32, where=ctx):
            return where.enter_context(nc.sbuf_tensor(name, shape, dt))

        def scratch(name, shape):
            return nc.dram_tensor(name, shape, F32, kind="Internal").ap()

        products = ProductSemaphores(sem)
        act_t = scratch("act_t", (ACT_TILES, P, S))
        v_ret = scratch("v_ret", (H_RET, P, NT, RET_V))
        q_t = scratch("q_t", (12, P, S))
        k_t = scratch("k_t", (H_MLA, P, S))
        v_mla = scratch("v_mla", (H_MLA, P, NT, V_MLA))
        y_mla = scratch("y_mla", (H_MLA, P, S))
        y_ret = scratch("y_ret", (H_RET * 4, P, S))

        t = {
            "cols": sb("cols", [P, N_COLS]), "consts": sb("consts", [P, 8]), "ones": sb("ones", [P, P]),
            "ident": sb("ident", [P, P]), "ident_r": sb("ident_r", [P, P], F32R),
            "causal_r": sb("causal_r", [P, P], F32R), "causal_kq": sb("causal_kq", [P, P]),
            "gate": sb("gate", [P, D]), "g_final": sb("g_final", [P, D]),
        }
        with ExitStack() as tables:
            t["cos_ret"] = sb("cos_ret", [P, S], where=tables)
            t["sin_ret"] = sb("sin_ret", [P, 2, S], where=tables)
            t["cos_mla"] = sb("cos_mla", [P, S], where=tables)
            t["sin_mla"] = sb("sin_mla", [P, S], where=tables)
            t["k_rope_hi"] = sb("k_rope_hi", [P, S], F32R, where=tables)
            t["k_rope_lo"] = sb("k_rope_lo", [P, S], F32R, where=tables)
            with ExitStack() as latents:
                latent = sb("latent", [P, 6, S], where=latents)
                with ExitStack() as hidden:
                    t["h_hi"] = sb("h_hi", [P, KD, S], F32R, where=hidden)
                    t["h_lo"] = sb("h_lo", [P, KD, S], F32R, where=hidden)
                    condition(nc, sem, a, t, latent)
                    with ExitStack() as w:
                        raw = sb("w_raw", [P, KD, HALF], where=w)
                        w_hi, w_lo = sb("w_hi", [P, KD, HALF], F32R, w), sb("w_lo", [P, KD, HALF], F32R, w)
                        stage = sb("stage", [P, 2, S], where=w)
                        psum = w.enter_context(nc.psum_tensor("p_tiles", [P, 4, S], F32))
                        common = (t["h_hi"], t["h_lo"], raw, w_hi, w_lo, psum)
                        transposed_product(nc, products, a["w_latent"], *common, [(2, ACT.Copy)], keep=latent)
                        transposed_product(nc, products, a["w_act"], *common,
                                           [(2, ACT.Silu), (4, ACT.Copy), (4, ACT.Silu), (4, ACT.Sigmoid)],
                                           stage=stage, dst=act_t)
                        token_product(nc, products, a["w_v"], *common, stage,
                                      lambda e, g, tile, src: e.dma_start(
                                          one(v_ret, g).rearrange("a p t n -> p (a t) n")[:, tile, :], src))
                with ExitStack() as up:
                    cq_hi, cq_lo = sb("cq_hi", [P, KQ, S], F32R, up), sb("cq_lo", [P, KQ, S], F32R, up)
                    ckv_hi, ckv_lo = sb("ckv_hi", [P, KKV, S], F32R, up), sb("ckv_lo", [P, KKV, S], F32R, up)
                    normalise_latents(nc, sem, t, latent, cq_hi, cq_lo, ckv_hi, ckv_lo)
                    raw = sb("up_raw", [P, KQ, HALF], where=up)
                    w_hi, w_lo = sb("up_hi", [P, KQ, HALF], F32R, up), sb("up_lo", [P, KQ, HALF], F32R, up)
                    stage = sb("up_stage", [P, 2, S], where=up)
                    psum = up.enter_context(nc.psum_tensor("p_up", [P, 4, S], F32))
                    transposed_product(nc, products, a["w_q_up"], cq_hi, cq_lo, raw, w_hi, w_lo, psum,
                                       [(3, ACT.Copy)], stage=stage, dst=q_t)
                    transposed_product(nc, products, a["w_k_up"], ckv_hi, ckv_lo, raw, w_hi, w_lo, psum,
                                       [(2, ACT.Copy)], stage=stage, dst=k_t)
                    token_product(nc, products, a["w_v_up"], ckv_hi, ckv_lo, raw, w_hi, w_lo, psum, stage,
                                  lambda e, g, tile, src: e.dma_start(
                                      v_mla[bass.ds(g * 4, 4)].rearrange("h p t n -> p h t n")[:, :, tile, :],
                                      src.rearrange("p (h n) -> p h n", h=4)))
            q_rope_t = q_t[8:12].rearrange("a (b p) n -> (a b) p n", b=2)
            attention(nc, sem, a, t, q_t, q_rope_t, k_t, v_mla, act_t, y_mla)
            retention(nc, sem, a, t, act_t, v_ret, y_ret)
        merged = sb("merged", [P, KD, S])
        merge(nc, sem, a, t, a["w_proj"], y_mla, y_ret, act_t, merged)
        output(nc, sem, a, t, a["w_out"], merged, out)


def shape_constants():
    consts = np.zeros((P, 8), np.float32)
    f = np.arange(P)
    consts[:, CC_FREQ_RET] = 10000.0 ** (-(2.0 * f) / RET_QK)
    consts[:, CC_FREQ_MLA] = 10000.0 ** (-(2.0 * (f % 32)) / ROPE)
    consts[:, CC_SIGN] = np.where(f % 64 < 32, -1.0, 1.0)
    consts[:, CC_HALF_PI] = np.pi / 2
    consts[:, CC_EPS] = EPS
    log_gamma = np.log1p(-np.exp2(-5.0 - np.arange(H_RET)))[:, None]
    token = np.arange(S)[None, :] + 1.0
    decay = np.stack([np.exp(log_gamma * token), np.exp(-log_gamma * token) * RET_QK ** -0.5], axis=1)
    later = f[None, :] > f[:, None]
    return {
        "consts": consts, "decay": decay.astype(np.float32), "ident": np.eye(P, dtype=np.float32),
        "causal_add": np.where(later, MASKED, 0.0).astype(np.float32),
        "causal_kq": (f[:, None] <= f[None, :]).astype(np.float32),
    }


def kernel(**inputs):
    import concourse.bacc as bacc
    from concourse.bass_utils import run_bass_kernel_spmd

    def groups(w, cols):
        k, n = w.shape
        return np.ascontiguousarray(w.reshape(k // P, P, n // cols, cols).transpose(2, 1, 0, 3))

    def columns(v):
        return v.reshape(-1, P).T

    w_in = inputs["w_in"][0]
    w_q = inputs["w_q_up"][0].reshape(Q_RANK, H_MLA, NOPE + ROPE)
    w_kv = inputs["w_kv_up"][0].reshape(KV_RANK, H_MLA, NOPE + V_MLA)
    b_ada = inputs["b_ada"][0]
    w_ret = inputs["w_proj_ret"][0]
    k_pe = w_in[:, 640:704]
    arrays = {
        "x": inputs["x"][0].reshape(NT, P, D),
        "positions": inputs["positions"][0],
        "cols": np.ascontiguousarray(np.concatenate([
            columns(inputs["c"][0]), columns(b_ada[:2 * D]), columns(inputs["g_pre"][0]), columns(inputs["g_q"][0]),
            columns(inputs["g_kv"][0]), columns(inputs["g_ret"][0])], axis=1)),
        "b_gate": b_ada[2 * D:],
        "g_final": inputs["g_final"],
        "w_ada": groups(inputs["w_ada"][0], HALF),
        "w_latent": groups(np.concatenate([w_in[:, :640], k_pe, k_pe], axis=1), 3 * P),
        "w_act": groups(np.concatenate([w_in[:, 704:3776], w_in[:, 5824:]], axis=1), HALF),
        "w_v": groups(w_in[:, 3776:5824], HALF),
        "w_q_up": groups(np.concatenate([w_q[:, :, :NOPE].reshape(Q_RANK, -1), w_q[:, :, NOPE:].reshape(Q_RANK, -1)],
                                        axis=1), HALF),
        "w_k_up": groups(w_kv[:, :, :NOPE].reshape(KV_RANK, -1), HALF),
        "w_v_up": groups(w_kv[:, :, NOPE:].reshape(KV_RANK, -1), HALF),
        "w_proj": np.concatenate([groups(w_ret[:D], 2 * P), groups(w_ret[D:], 2 * P),
                                  groups(inputs["w_proj_mla"][0], 2 * P)]),
        "w_out": inputs["w_out"][0].reshape(KD, P, D),
    }
    nc = bacc.Bacc("TRN2", target_bir_lowering=False, num_devices=1)
    aps = {}
    for name, value in arrays.items():
        value = arrays[name] = np.ascontiguousarray(value)
        aps[name] = nc.dram_tensor("in_" + name, value.shape, mybir.dt.from_np(value.dtype), kind="ExternalInput").ap()
    for name, value in shape_constants().items():
        made = nc.inline_tensor(value, name="const_" + name)
        aps[name] = made.ap() if not isinstance(made, bass.AP) else made
    out = nc.dram_tensor("out", (S, D), F32, kind="ExternalOutput").ap()
    build(nc, aps, out)
    result = run_bass_kernel_spmd(nc, [{"in_" + k: v for k, v in arrays.items()}], core_ids=[0])
    return result.results[0]["out"].reshape(1, S, D)
```

```python
from contextlib import ExitStack

import numpy as np
import concourse.bass as bass
from concourse import mybir

F32 = mybir.dt.float32
F32R = mybir.dt.float32r
I32 = mybir.dt.int32
ALU = mybir.AluOpType
ACT = mybir.ActivationFunctionType
AX = mybir.AxisListType

P = 128
S = 1024
D = 1024
KD = D // P
NT = S // P
HALF = 512
EPS = 1e-6
Q_RANK, KV_RANK, ROPE = 384, 256, 64
KQ, KKV = Q_RANK // P, KV_RANK // P
H_MLA, NOPE, V_MLA = 8, 128, 128
SCALE = float(NOPE + ROPE) ** -0.5
H_RET, RET_QK, RET_V = 4, 256, 512
GATE_MLA, Q_RET, K_RET, GATE_RET, MERGE_MLA, MERGE_RET = 0, 8, 16, 24, 40, 48
ACT_TILES = 56
MASKED = -1e30
TURN_1 = 6.28125
TURN_2 = float(np.float32(2 * np.pi - TURN_1))
TURN_3 = float(2 * np.pi - TURN_1 - TURN_2)
ROUNDER = 12582912.0
PI_BELOW = 3.1415925
COL_C, COL_BADA, COL_GPRE, COL_GQ, COL_GKV, COL_GRET = 0, 8, 24, 32, 35, 37
N_COLS = 53
CC_FREQ_RET, CC_FREQ_MLA, CC_SIGN, CC_HALF_PI, CC_EPS = 0, 1, 2, 3, 4


def one(ap, i):
    return ap[bass.ds(i, 1)]


def pipelined(engine, step, rounds, size, drain):
    def body(it, first, last):
        for m in range(size):
            step(it, m, lambda b: b >= 0 or not first, last)

    body(0, True, False)
    with engine.Fori(1, rounds - 1) as it:
        body(it, False, False)
    body(rounds - 1, False, True)
    for m in range(size, size + drain):
        step(rounds - 1, m, lambda b: b < size, True)


def lag(it, m, size):
    return (it, m) if m >= 0 else (it - 1, m + size)


class ProductSemaphores:

    def __init__(self, sem):
        self.loaded = sem("product_w_loaded")
        self.hi_ready = sem("product_w_hi_ready")
        self.lo_ready = sem("product_w_lo_ready")
        self.slot_free = sem("product_w_slot_free")
        self.summed = sem("product_tile_summed")
        self.psum_free = sem("product_psum_free")
        self.stage_free = [sem("product_stage_even_free"), sem("product_stage_odd_free")]
        self.base = dict.fromkeys(("loaded", "hi", "lo", "slot", "summed", "psum", "stage"), 0)


class Product:

    def __init__(self, nc, sems, weights, x_hi, x_lo, raw, w_hi, w_lo, psum):
        self.nc, self.sems, self.weights = nc, sems, weights
        self.x_hi, self.x_lo, self.raw, self.w_hi, self.w_lo, self.psum = x_hi, x_lo, raw, w_hi, w_lo, psum
        self.groups, _, self.k_tiles, self.cols = weights.shape
        self.base = dict(sems.base)

    def past(self, parts, tiles, staged):
        counts = dict(loaded=16 * self.groups, hi=parts, lo=parts, summed=tiles, psum=tiles,
                      stage=8 * tiles if staged else 0)
        for key, count in counts.items():
            self.sems.base[key] += count
        self.end = dict(self.sems.base)

    def load(self, sp, g):
        sp.dma_start(self.raw[:, 0:self.k_tiles, 0:self.cols],
                     one(self.weights, g).rearrange("a p k n -> p (a k) n")).then_inc(self.sems.loaded, 16)

    def sync(self, sp, follow=None, led=False):
        if not led:
            self.load(sp, 0)
        parts = self.parts
        with sp.Fori(0, self.groups - 1) as g:
            sp.wait_ge(self.sems.lo_ready, g * parts + (parts + self.base["lo"]))
            self.load(sp, g + 1)
            self.stores(sp, g)
        if follow:
            sp.wait_ge(self.sems.lo_ready, self.end["lo"])
            follow.load(sp, 0)
        self.stores(sp, self.groups - 1)

    def wait_stored(self, sp):
        for free in self.sems.stage_free:
            sp.wait_ge(free, 16 + self.end["stage"])


class TransposedProduct(Product):

    def __init__(self, *common, segments, stage=None, dst=None, keep=None):
        super().__init__(*common)
        self.segments, self.stage, self.dst, self.keep = segments, stage, dst, keep
        self.parts = self.cols // P
        tiles = self.groups * self.parts
        self.past(tiles, tiles, dst is not None)

    def stores(self, sp, g):
        if self.dst is None:
            return
        for j in range(self.parts):
            sp.wait_ge(self.sems.psum_free, g * self.parts + (2 + j + 1 + self.base["psum"]))
            sp.dma_start(one(self.dst, g * self.parts + j).rearrange("a p n -> p (a n)"),
                         self.stage[:, j % 2, :]).then_inc(self.sems.stage_free[j % 2], 16)

    def split(self, act, g, j):
        if j == 0:
            act.wait_ge(self.sems.loaded, g * 16 + 16 + self.base["loaded"])
        cut = (slice(None), slice(0, self.k_tiles), slice(j * P, (j + 1) * P))
        self.nc.scalar.activation(self.w_hi[cut], self.raw[cut], ACT.Copy).then_inc(self.sems.hi_ready, 1)

    def take_over(self, act, j, last):
        for tile in range(j, self.parts if last else j + 1):
            self.split(act, 0, tile)

    def evacuate(self, act, g, j, func):
        per = self.parts
        act.wait_ge(self.sems.summed, g * per + (j + 1 + self.base["summed"]))
        if self.keep is None:
            act.wait_ge(self.sems.stage_free[j % 2], g * (8 * per) + (16 * (j // 2 + 1) + self.base["stage"]))
            out = self.stage[:, j % 2, :]
        else:
            out = self.keep[:, bass.ds(g * per + j, 1), :].rearrange("p a n -> p (a n)")
        self.nc.scalar.activation(out, self.psum[:, j % 2, :], func).then_inc(self.sems.psum_free, 1)

    def scalar(self, act, follow=None, led=False):
        if not led:
            self.take_over(act, 0, True)
        first = 0
        for count, func in self.segments:
            last = first + count
            looped = min(last, self.groups - 1)
            if looped > first:
                with act.Fori(first, looped) as g:
                    for j in range(self.parts):
                        self.evacuate(act, g, j, func)
                        self.split(act, g + 1, j)
            first = last
        for j in range(self.parts):
            self.evacuate(act, self.groups - 1, j, func)
            if follow:
                follow.take_over(act, j, j == self.parts - 1)

    def vector(self, dve, first=0, last=None):
        with dve.Fori(first, self.groups if last is None else last) as g:
            for j in range(self.parts):
                cut = (slice(None), slice(0, self.k_tiles), slice(j * P, (j + 1) * P))
                dve.wait_ge(self.sems.hi_ready, g * self.parts + (j + 1 + self.base["hi"]))
                self.nc.vector.tensor_tensor(self.w_lo[cut], self.raw[cut], self.w_hi[cut].bitcast(F32),
                                             ALU.subtract).then_inc(self.sems.lo_ready, 1)

    def tensor(self, pe):
        nc, w_hi, w_lo, x_hi, x_lo = self.nc, self.w_hi, self.w_lo, self.x_hi, self.x_lo
        with pe.Fori(0, self.groups) as g:
            for j in range(self.parts):
                cut = slice(j * P, (j + 1) * P)
                pe.wait_ge(self.sems.lo_ready, g * self.parts + (j + 1 + self.base["lo"]))
                pe.wait_ge(self.sems.psum_free, g * self.parts + (j + 1 + self.base["psum"]))
                for half in range(2):
                    tok = slice(half * HALF, (half + 1) * HALF)
                    out = self.psum[:, j % 2, tok]
                    for k in range(self.k_tiles):
                        nc.tensor.matmul(out, w_hi[:, k, cut], x_hi[:, k, tok], start=(k == 0), stop=False)
                        nc.tensor.matmul(out, w_hi[:, k, cut], x_lo[:, k, tok], start=False, stop=False)
                        last = nc.tensor.matmul(out, w_lo[:, k, cut], x_hi[:, k, tok],
                                                start=False, stop=(k == self.k_tiles - 1))
                last.then_inc(self.sems.summed, 1)


class TokenProduct(Product):

    def __init__(self, *common, stage, store):
        super().__init__(*common)
        self.stage, self.store = stage, store
        self.parts = self.k_tiles
        self.sems.base["slot"] += self.groups * (self.k_tiles - 1)
        self.past(self.groups * self.k_tiles, self.groups * NT, True)

    def stores(self, sp, g):
        for t in range(NT):
            sp.wait_ge(self.sems.psum_free, g * NT + (2 + t + 1 + self.base["psum"]))
            self.store(sp, g, t, self.stage[:, t % 2, 0:HALF]).then_inc(self.sems.stage_free[t % 2], 16)

    def split(self, act, g, k, first=False):
        if k == 0:
            act.wait_ge(self.sems.loaded, g * 16 + 16 + self.base["loaded"])
        if not first and k < self.k_tiles - 1:
            act.wait_ge(self.sems.slot_free, (g - 1) * (self.k_tiles - 1) + (k + 1 + self.base["slot"]))
        elif not first:
            act.wait_ge(self.sems.summed, g * NT + self.base["summed"])
        self.nc.scalar.activation(self.w_hi[:, k, :], self.raw[:, k, :], ACT.Copy).then_inc(self.sems.hi_ready, 1)

    def take_over(self, act, j, last):
        if last:
            for k in range(self.k_tiles):
                self.split(act, 0, k, first=True)

    def evacuate(self, act, g, t):
        act.wait_ge(self.sems.summed, g * NT + (t + 1 + self.base["summed"]))
        act.wait_ge(self.sems.stage_free[t % 2], g * (8 * NT) + (16 * (t // 2 + 1) + self.base["stage"]))
        self.nc.scalar.activation(self.stage[:, t % 2, 0:HALF], self.psum[:, t % 2, 0:HALF], ACT.Copy)\
            .then_inc(self.sems.psum_free, 1)

    def scalar(self, act, led=False):
        if not led:
            self.take_over(act, 0, True)
        with act.Fori(0, self.groups - 1) as g:
            for t in range(NT - 1):
                self.evacuate(act, g, t)
            for k in range(self.k_tiles):
                self.split(act, g + 1, k)
            self.evacuate(act, g, NT - 1)
        for t in range(NT):
            self.evacuate(act, self.groups - 1, t)

    def vector(self, dve, first=0, last=None):
        with dve.Fori(first, self.groups if last is None else last) as g:
            for k in range(self.k_tiles):
                dve.wait_ge(self.sems.hi_ready, g * self.k_tiles + (k + 1 + self.base["hi"]))
                self.nc.vector.tensor_tensor(self.w_lo[:, k, :], self.raw[:, k, :], self.w_hi[:, k, :].bitcast(F32),
                                             ALU.subtract).then_inc(self.sems.lo_ready, 1)

    def tensor(self, pe):
        nc, w_hi, w_lo, x_hi, x_lo = self.nc, self.w_hi, self.w_lo, self.x_hi, self.x_lo
        with pe.Fori(0, self.groups) as g:
            for t in range(NT):
                tok = slice(t * P, (t + 1) * P)
                out = self.psum[:, t % 2, 0:HALF]
                pe.wait_ge(self.sems.psum_free, g * NT + (t + 1 + self.base["psum"]))
                for k in range(self.k_tiles):
                    if t == 0:
                        pe.wait_ge(self.sems.lo_ready, g * self.k_tiles + (k + 1 + self.base["lo"]))
                    nc.tensor.matmul(out, x_hi[:, k, tok], w_hi[:, k, :], start=(k == 0), stop=False)
                    nc.tensor.matmul(out, x_lo[:, k, tok], w_hi[:, k, :], start=False, stop=False)
                    last = nc.tensor.matmul(out, x_hi[:, k, tok], w_lo[:, k, :],
                                            start=False, stop=(k == self.k_tiles - 1))
                    if t == NT - 1 and k < self.k_tiles - 1:
                        last.then_inc(self.sems.slot_free, 1)
                last.then_inc(self.sems.summed, 1)


def condition(nc, sem, products, a, t, spare, raw):
    ins_loaded = sem("vectors_loaded")
    x_loaded = [sem("x_first_loaded"), sem("x_second_loaded")]
    rows_loaded = sem("rows_loaded")
    pos_loaded = sem("positions_loaded")
    ada_loaded = [sem("ada_even_loaded"), sem("ada_odd_loaded")]
    silu_c_ready = sem("silu_c_ready")
    ada_step = sem("ada_step")
    gate_step = sem("ada_gate_step")
    mod_summed = sem("mod_summed")
    mod_ready = sem("mod_ready")
    squared = sem("x_squared")
    rms = sem("x_rms")
    rooted = sem("x_rooted")
    normed = sem("x_normed")
    turned = sem("x_turned")
    h_hi_ready = sem("h_hi_ready")
    h_full_ready = sem("h_full_ready")
    h_lo_ready = sem("h_lo_ready")
    table = sem("table_step")
    sines = sem("sines_ready")
    magnitude = sem("angle_magnitude")
    const_ready = sem("const_ready")
    consts_split = sem("consts_split")
    with ExitStack() as ctx:
        sb = lambda n, shape, dt=F32: ctx.enter_context(nc.sbuf_tensor(n, shape, dt))
        pb = lambda n, shape: ctx.enter_context(nc.psum_tensor(n, shape, F32))
        x_tok = sb("x_tok", [P, NT, D])
        causal_add = sb("causal_add", [P, P])
        ada = [raw, sb("ada_odd", [P, KD, HALF])]
        acc = sb("ada_sum", [P, 2 * D])
        junk = sb("junk", [P, D])
        mod = sb("mod", [P, 16])
        ss = sb("x_sumsq", [P, NT])
        root = sb("x_root", [P, NT])
        rstd = sb("x_rstd", [P, NT])
        silu_c = sb("silu_c", [P, KD])
        silu_rows = sb("silu_rows", [P, KD, P])
        h_full = junk[:, :].rearrange("p (a n) -> p a n", n=HALF)
        ang, mag, turns = spare[:, 0:2, :], spare[:, 2:4, :], spare[:, 4, :]
        pos_i = spare[:, 5, :].bitcast(I32)
        p_mod = pb("p_mod", [P, HALF])
        p_gate = pb("p_gate", [P, 2, HALF])
        p_x = pb("p_x", [P, 4, HALF])
        block = ctx.enter_context(nc.Block())

        @block.sync
        def _(sp):
            sp.dma_start(t["cols"][:, :], a["cols"]).then_inc(ins_loaded, 16)
            sp.dma_start(t["consts"][:, :], a["consts"]).then_inc(ins_loaded, 16)
            sp.dma_start(t["ident"][:, :], a["ident"]).then_inc(ins_loaded, 16)
            sp.dma_start(causal_add[:, :], a["causal_add"]).then_inc(ins_loaded, 16)
            sp.dma_start(t["causal_kq"][:, :], a["causal_kq"]).then_inc(ins_loaded, 16)
            sp.dma_start(pos_i, a["positions"].partition_broadcast(P)).then_inc(pos_loaded, 16)
            for n in range(2):
                sp.dma_start(x_tok[:, 4 * n:4 * n + 4, :],
                             a["x"][4 * n:4 * n + 4].rearrange("t p d -> p t d")).then_inc(x_loaded[n], 16)
            for n in range(6):
                if n >= 2:
                    sp.wait_ge(ada_step, KD * (n - 1))
                sp.dma_start(ada[n % 2][:, :, :], a["w_ada"][n]).then_inc(ada_loaded[n % 2], 16)
            sp.dma_start(t["gate"][:, :], a["b_gate"].partition_broadcast(P)).then_inc(rows_loaded, 16)
            sp.dma_start(t["g_final"][:, :], a["g_final"].partition_broadcast(P)).then_inc(rows_loaded, 16)
            sp.wait_ge(gate_step, 1)
            sp.dma_start(raw[:, :, 0:2 * P], a["w_latent"][0]).then_inc(products.loaded, 16)

        @block.gpsimd
        def _(pool):
            nc.gpsimd.memset(t["ones"][:, :], 1.0).then_inc(const_ready, 1)

        @block.scalar
        def _(act):
            act.wait_ge(ins_loaded, 80)
            nc.scalar.activation(t["ident_r"][:, :], t["ident"][:, :], ACT.Copy).then_inc(consts_split, 1)
            nc.scalar.activation(t["causal_r"][:, :], causal_add[:, :], ACT.Copy).then_inc(consts_split, 1)
            nc.scalar.activation(silu_c[:, :], t["cols"][:, COL_C:COL_C + KD], ACT.Silu).then_inc(silu_c_ready, 1)
            for n in range(NT):
                act.wait_ge(x_loaded[n // 4], 16)
                if n:
                    act.wait_ge(squared, n)
                nc.scalar.activation(junk[:, :], x_tok[:, n, :], ACT.Square,
                                     accum_out=ss[:, n:n + 1]).then_inc(squared, 1)
            act.wait_ge(rms, 1)
            nc.scalar.activation(root[:, :], ss[:, :], ACT.Sqrt).then_inc(rooted, 1)
            for n, sin_out in enumerate((t["sin_ret"][:, 1, :], t["sin_mla"][:, :])):
                act.wait_ge(table, 7 * (n + 1))
                nc.scalar.activation(mag[:, n, :], ang[:, n, :], ACT.Abs).then_inc(magnitude, 1)
                nc.scalar.activation(sin_out, ang[:, n, :], ACT.Sin, scale=(
                    t["consts"][:, CC_SIGN:CC_SIGN + 1] if n else 1.0)).then_inc(sines, 1)
                act.wait_ge(magnitude, n + 1)
                nc.scalar.activation((t["cos_mla"] if n else t["cos_ret"])[:, :], mag[:, n, :], ACT.Sin, scale=-1.0,
                                     bias=t["consts"][:, CC_HALF_PI:CC_HALF_PI + 1]).then_inc(sines, 1)
            nc.scalar.activation(t["sin_ret"][:, 0, :], ang[:, 0, :], ACT.Sin, scale=-1.0).then_inc(sines, 1)
            act.wait_ge(mod_ready, 3)
            for m in range(2 * KD):
                half, k = divmod(m, KD)
                act.wait_ge(turned, m + 1)
                nc.scalar.activation(t["h_hi"][:, k, half * HALF:(half + 1) * HALF], p_x[:, m % 4, :], ACT.Identity,
                                     scale=mod[:, KD + k:KD + k + 1], bias=mod[:, k:k + 1]).then_inc(h_hi_ready, 1)

        @block.vector
        def _(dve):
            dve.wait_ge(ins_loaded, 80)
            dve.wait_ge(pos_loaded, 16)
            steps = [0]

            def chained(ins):
                steps[0] += 1
                ins.then_inc(table, 1)
                dve.wait_ge(table, steps[0])

            for n, col in enumerate((CC_FREQ_RET, CC_FREQ_MLA)):
                chained(nc.vector.tensor_scalar(ang[:, n, :], pos_i, t["consts"][:, col:col + 1], None,
                                                ALU.mult))
                chained(nc.vector.tensor_scalar(turns, ang[:, n, :], float(1 / (2 * np.pi)), ROUNDER,
                                                ALU.mult, ALU.add))
                chained(nc.vector.tensor_scalar(turns, turns, -ROUNDER, None, ALU.add))
                for part in (TURN_1, TURN_2, TURN_3):
                    chained(nc.vector.scalar_tensor_tensor(out=ang[:, n, :], in0=turns, scalar=-part,
                                                           in1=ang[:, n, :], op0=ALU.mult, op1=ALU.add))
                chained(nc.vector.tensor_scalar(ang[:, n, :], ang[:, n, :], PI_BELOW, -PI_BELOW, ALU.min, ALU.max))
            dve.wait_ge(silu_c_ready, 1)
            for k in range(KD):
                nc.vector.tensor_scalar(silu_rows[:, k, :], t["ident"][:, :], 0.0, silu_c[:, k:k + 1],
                                        ALU.mult, ALU.add).then_inc(silu_c_ready, 1)
            for n in range(4):
                dve.wait_ge(ada_loaded[n % 2], 16 * (n // 2 + 1))
                cut = slice(n * HALF, (n + 1) * HALF)
                for k in range(KD):
                    if k == 0:
                        ins = nc.vector.tensor_scalar(acc[:, cut], ada[n % 2][:, k, :], silu_c[:, 0:1], None, ALU.mult)
                    else:
                        ins = nc.vector.scalar_tensor_tensor(out=acc[:, cut], in0=ada[n % 2][:, k, :],
                                                             scalar=silu_c[:, k:k + 1], in1=acc[:, cut],
                                                             op0=ALU.mult, op1=ALU.add)
                    ins.then_inc(ada_step, 1)
                    dve.wait_ge(ada_step, n * KD + k + 1)
                if n == 0:
                    dve.wait_ge(squared, NT)
                    nc.vector.tensor_scalar(ss[:, :], ss[:, :], 1.0 / D, EPS, ALU.mult, ALU.add).then_inc(rms, 1)
                    dve.wait_ge(rooted, 1)
                    nc.vector.reciprocal(rstd[:, :], root[:, :]).then_inc(rms, 1)
                    dve.wait_ge(rms, 2)
                    for j in range(NT):
                        nc.vector.tensor_scalar(x_tok[:, j, :], x_tok[:, j, :], rstd[:, j:j + 1], None,
                                                ALU.mult).then_inc(normed, 1)
                if n == 3:
                    dve.wait_ge(mod_summed, 1)
                    nc.vector.tensor_tensor(mod[:, :], p_mod[:, 0:16], t["cols"][:, COL_BADA:COL_BADA + 16],
                                            ALU.add).then_inc(mod_ready, 1)
                    dve.wait_ge(mod_ready, 1)
                    nc.vector.tensor_scalar(mod[:, KD:], mod[:, KD:], 1.0, None, ALU.add).then_inc(mod_ready, 1)
                    dve.wait_ge(mod_ready, 2)
                    nc.vector.tensor_tensor(mod[:, KD:], mod[:, KD:], t["cols"][:, COL_GPRE:COL_GPRE + KD],
                                            ALU.mult).then_inc(mod_ready, 1)
                    dve.wait_ge(mod_ready, 3)
                    for m in range(2 * KD):
                        half, k = divmod(m, KD)
                        dve.wait_ge(turned, m + 1)
                        if m >= 2:
                            dve.wait_ge(h_lo_ready, m - 1)
                        dve.wait_ge(h_hi_ready, m + 1)
                        nc.vector.tensor_scalar(h_full[:, m % 2, :], p_x[:, m % 4, :], mod[:, KD + k:KD + k + 1],
                                                mod[:, k:k + 1], ALU.mult, ALU.add).then_inc(h_full_ready, 1)
                        dve.wait_ge(h_full_ready, m + 1)
                        cols = slice(half * HALF, (half + 1) * HALF)
                        nc.vector.tensor_tensor(t["h_lo"][:, k, cols], h_full[:, m % 2, :],
                                                t["h_hi"][:, k, cols].bitcast(F32), ALU.subtract).then_inc(h_lo_ready, 1)
            dve.wait_ge(rows_loaded, 32)
            dve.wait_ge(gate_step, 2)
            nc.vector.tensor_tensor(t["gate"][:, :], t["gate"][:, :], p_gate[:, :, :].rearrange("p a n -> p (a n)"),
                                    ALU.add).then_inc(mod_ready, 1)

        @block.tensor
        def _(pe):
            pe.wait_ge(normed, NT)
            pe.wait_ge(const_ready, 1)

            def turn(m):
                half, k = divmod(m, KD)
                if m >= 4:
                    pe.wait_ge(h_lo_ready, m - 3)
                for j in range(4):
                    last = nc.tensor.transpose(p_x[:, m % 4, j * P:(j + 1) * P],
                                               x_tok[:, 4 * half + j, k * P:(k + 1) * P], t["ident"][:, :])
                last.then_inc(turned, 1)

            for m in range(4):
                turn(m)
            for n in range(16):
                if n % 4 == 0:
                    pe.wait_ge(ada_step, (n // 4 + 1) * KD)
                last = nc.tensor.matmul(p_mod[:, n:n + 1], acc[:, n * P:(n + 1) * P], t["ones"][:, 0:1],
                                        start=True, stop=True)
            last.then_inc(mod_summed, 1)
            for m in range(4, 2 * KD):
                turn(m)
            pe.wait_ge(silu_c_ready, 1 + KD)
            for n in range(2):
                pe.wait_ge(ada_loaded[n], 48)
                for k in range(KD):
                    last = nc.tensor.matmul(p_gate[:, n, :], silu_rows[:, k, :], ada[n][:, k, :],
                                            start=(k == 0), stop=(k == KD - 1))
                last.then_inc(gate_step, 1)


def project(nc, sem, products, a, t, latent, raw, act_t, v_ret):
    squared = sem("latent_squared")
    added = sem("latent_squares_added")
    summed = sem("latent_summed")
    rooted = sem("latent_rooted")
    inverted = sem("latent_inverted")
    swapped = sem("k_pe_swapped")
    roped = sem("k_pe_roped")
    K_PE = KQ + KKV
    with ExitStack() as ctx:
        w_hi = ctx.enter_context(nc.sbuf_tensor("w_hi", [P, KD, HALF], F32R))
        w_lo = ctx.enter_context(nc.sbuf_tensor("w_lo", [P, KD, HALF], F32R))
        stage = ctx.enter_context(nc.sbuf_tensor("stage", [P, 2, S], F32))
        swap = ctx.enter_context(nc.sbuf_tensor("k_pe_swap", [P, S], F32))
        total = ctx.enter_context(nc.sbuf_tensor("latent_total", [P, 2, S], F32))
        square = ctx.enter_context(nc.sbuf_tensor("latent_square", [P, 2, S], F32))
        psum = ctx.enter_context(nc.psum_tensor("p_tiles", [P, 2, S], F32))
        sums = ctx.enter_context(nc.psum_tensor("latent_sums", [P, 2, 2, HALF], F32))
        block = ctx.enter_context(nc.Block())
        common = (t["h_hi"], t["h_lo"], raw, w_hi, w_lo, psum)
        down = TransposedProduct(nc, products, a["w_latent"], *common, segments=[(3, ACT.Copy)], keep=latent)
        gates = TransposedProduct(nc, products, a["w_act"], *common, stage=stage, dst=act_t,
                                  segments=[(2, ACT.Silu), (4, ACT.Copy), (4, ACT.Silu), (4, ACT.Sigmoid)])
        values = TokenProduct(nc, products, a["w_v"], *common, stage=stage, store=lambda e, g, tile, src: e.dma_start(
            one(v_ret, g).rearrange("a p t n -> p (a t) n")[:, tile, :], src))
        k_pe = latent[:, K_PE, :]
        k_swap = swap[:, :]
        places = [total[:, 0, :], square[:, 0, :], square[:, 1, :], total[:, 1, :], square[:, 0, :]]

        @block.sync
        def _(sp):
            for free in products.stage_free:
                sp.sem_inc(free, 16)
            down.sync(sp, follow=gates, led=True)
            sp.wait_ge(products.psum_free, 2 + down.end["psum"])
            for q in range(4):
                sp.dma_start(k_swap[32 * q:32 * q + 32, :],
                             latent[32 * (q ^ 1):32 * (q ^ 1) + 32, K_PE, :]).then_inc(swapped, 16)
            gates.sync(sp, follow=values, led=True)
            values.sync(sp, led=True)
            values.wait_stored(sp)

        @block.scalar
        def _(act):
            act.sem_inc(products.psum_free, 2)
            down.scalar(act, follow=gates)
            for n in range(KQ + KKV):
                if n == 4:
                    act.wait_ge(added, 1)
                nc.scalar.activation(places[n], latent[:, n, :], ACT.Square).then_inc(squared, 1)
            act.wait_ge(roped, 3)
            nc.scalar.activation(t["k_rope_hi"][:, :], k_pe, ACT.Copy).then_inc(roped, 1)
            gates.scalar(act, follow=values, led=True)
            for b, rank in enumerate((Q_RANK, KV_RANK)):
                act.wait_ge(summed, b + 1)
                nc.scalar.activation(total[:, b, :], sums[:, b, :, :].rearrange("p a n -> p (a n)"), ACT.Sqrt,
                                     scale=1.0 / rank, bias=t["consts"][:, CC_EPS:CC_EPS + 1]).then_inc(rooted, 1)
            values.scalar(act, led=True)

        @block.vector
        def _(dve):
            down.vector(dve)
            gates.vector(dve, last=1)
            for n, (b, i) in enumerate(((0, 1), (0, 2), (1, 4))):
                dve.wait_ge(squared, i + 1)
                if n == 1:
                    dve.wait_ge(added, 1)
                nc.vector.tensor_tensor(total[:, b, :], total[:, b, :], places[i], ALU.add).then_inc(added, 1)
            dve.wait_ge(swapped, 64)
            nc.vector.tensor_tensor(k_pe, k_pe, t["cos_mla"][:, :], ALU.mult).then_inc(roped, 1)
            nc.vector.tensor_tensor(k_swap, k_swap, t["sin_mla"][:, :], ALU.mult).then_inc(roped, 1)
            dve.wait_ge(roped, 2)
            nc.vector.tensor_tensor(k_pe, k_pe, k_swap, ALU.add).then_inc(roped, 1)
            dve.wait_ge(roped, 4)
            nc.vector.tensor_tensor(t["k_rope_lo"][:, :], k_pe, t["k_rope_hi"][:, :].bitcast(F32),
                                    ALU.subtract).then_inc(roped, 1)
            gates.vector(dve, first=1)
            values.vector(dve, last=1)
            for b in range(2):
                dve.wait_ge(rooted, b + 1)
                nc.vector.reciprocal(total[:, b, :], total[:, b, :]).then_inc(inverted, 1)
            dve.wait_ge(inverted, 2)
            for i in range(KQ + KKV):
                nc.vector.tensor_tensor(latent[:, i, :], latent[:, i, :], total[:, int(i >= KQ), :], ALU.mult)\
                    .then_inc(inverted, 1)
            values.vector(dve, first=1)

        @block.tensor
        def _(pe):
            down.tensor(pe)
            gates.tensor(pe)
            pe.wait_ge(added, 3)
            for b in range(2):
                for half in range(2):
                    ins = nc.tensor.matmul(sums[:, b, half, :], t["ones"][:, :],
                                           total[:, b, half * HALF:(half + 1) * HALF], start=True, stop=True)
                ins.then_inc(summed, 1)
            values.tensor(pe)


class HeadInputs:
    LOADS = 9

    def __init__(self, nc, sem, sb, t, q_t, q_rope_t, k_t, v_tok):
        self.nc, self.t = nc, t
        self.q_t, self.q_rope_t, self.k_t, self.v_tok = q_t, q_rope_t, k_t, v_tok
        self.loaded = sem("head_loaded")
        self.roped = sem("q_rope_step")
        self.q_raw, self.k_raw = sb("q_raw", [P, S]), sb("k_raw", [P, S])
        self.v_raw = sb("v_raw", [P, NT, V_MLA])
        self.r_raw, self.r_swap, self.r_sum = sb("r_raw", [P, S]), sb("r_swap", [P, S]), sb("r_sum", [P, S])

    def load_qk(self, sp, h):
        def head(ap, rows=slice(None)):
            return one(ap, h).rearrange("a p n -> p (a n)")[rows]

        for rep in range(2):
            sp.dma_start(self.r_raw[64 * rep:64 * rep + 64, :], head(self.q_rope_t)).then_inc(self.loaded, 16)
            for part in range(2):
                row, src = 64 * rep + 32 * part, 32 * (1 - part)
                sp.dma_start(self.r_swap[row:row + 32, :], head(self.q_rope_t, slice(src, src + 32)))\
                    .then_inc(self.loaded, 16)
        sp.dma_start(self.q_raw[:, :], head(self.q_t)).then_inc(self.loaded, 16)
        sp.dma_start(self.k_raw[:, :], head(self.k_t)).then_inc(self.loaded, 16)

    def load_v(self, sp, h):
        sp.dma_start(self.v_raw[:, :, :], one(self.v_tok, h).rearrange("a p t n -> p (a t) n")).then_inc(self.loaded, 16)

    def rotate_products(self):
        nc, t = self.nc, self.t
        nc.gpsimd.tensor_tensor(self.r_raw[:, :], self.r_raw[:, :], t["cos_mla"][:, :], ALU.mult).then_inc(self.roped, 1)
        nc.gpsimd.tensor_tensor(self.r_swap[:, :], self.r_swap[:, :], t["sin_mla"][:, :], ALU.mult)\
            .then_inc(self.roped, 1)

    def rotate_sum(self):
        self.nc.gpsimd.tensor_tensor(self.r_sum[:, :], self.r_raw[:, :], self.r_swap[:, :], ALU.add)\
            .then_inc(self.roped, 1)


def project_latents(nc, sem, products, a, t, latent, q_t, k_t, v_mla, head_in):
    hi_ready = sem("latent_hi_ready")
    lo_ready = sem("latent_lo_ready")
    with ExitStack() as ctx:
        sb = lambda n, shape, dt=F32: ctx.enter_context(nc.sbuf_tensor(n, shape, dt))
        c_hi, c_lo = sb("c_hi", [P, KQ + KKV, S], F32R), sb("c_lo", [P, KQ + KKV, S], F32R)
        raw = sb("up_raw", [P, KQ, HALF])
        w_hi, w_lo = sb("up_hi", [P, KQ, HALF], F32R), sb("up_lo", [P, KQ, HALF], F32R)
        stage = sb("up_stage", [P, 2, S])
        psum = ctx.enter_context(nc.psum_tensor("p_up", [P, 2, S], F32))
        block = ctx.enter_context(nc.Block())
        weights = (raw, w_hi, w_lo, psum)
        c_q, c_kv = (c_hi[:, 0:KQ, :], c_lo[:, 0:KQ, :]), (c_hi[:, KQ:, :], c_lo[:, KQ:, :])
        q_up = TransposedProduct(nc, products, a["w_q_up"], *c_q, *weights, segments=[(3, ACT.Copy)],
                                 stage=stage, dst=q_t)
        k_up = TransposedProduct(nc, products, a["w_k_up"], *c_kv, *weights, segments=[(2, ACT.Copy)],
                                 stage=stage, dst=k_t)
        v_up = TokenProduct(nc, products, a["w_v_up"], *c_kv, *weights, stage=stage,
                            store=lambda e, g, tile, src: e.dma_start(
                                v_mla[bass.ds(g * 4, 4)].rearrange("h p t n -> p h t n")[:, :, tile, :],
                                src.rearrange("p (h n) -> p h n", h=4)))

        @block.sync
        def _(sp):
            q_up.sync(sp, follow=k_up)
            k_up.sync(sp, follow=v_up, led=True)
            k_up.wait_stored(sp)
            head_in.load_qk(sp, 0)
            v_up.sync(sp, led=True)
            v_up.wait_stored(sp)
            head_in.load_v(sp, 0)

        @block.gpsimd
        def _(pool):
            pool.wait_ge(head_in.loaded, 16 * (head_in.LOADS - 1))
            head_in.rotate_products()
            pool.wait_ge(head_in.roped, 2)
            head_in.rotate_sum()

        @block.scalar
        def _(act):
            def high(tiles):
                for i in tiles:
                    nc.scalar.activation(c_hi[:, i, :], latent[:, i, :], ACT.Copy,
                                         scale=t["cols"][:, COL_GQ + i:COL_GQ + i + 1]).then_inc(hi_ready, 1)

            high(range(KQ))
            q_up.take_over(act, 0, True)
            high(range(KQ, KQ + KKV))
            q_up.scalar(act, follow=k_up, led=True)
            k_up.scalar(act, follow=v_up, led=True)
            v_up.scalar(act, led=True)

        @block.vector
        def _(dve):
            def low(tiles):
                for i in tiles:
                    dve.wait_ge(hi_ready, i + 1)
                    nc.vector.scalar_tensor_tensor(out=c_lo[:, i, :], in0=latent[:, i, :],
                                                   scalar=t["cols"][:, COL_GQ + i:COL_GQ + i + 1],
                                                   in1=c_hi[:, i, :].bitcast(F32), op0=ALU.mult,
                                                   op1=ALU.subtract).then_inc(lo_ready, 1)

            low(range(KQ))
            q_up.vector(dve, last=1)
            low(range(KQ, KQ + KKV))
            q_up.vector(dve, first=1)
            k_up.vector(dve)
            v_up.vector(dve)

        @block.tensor
        def _(pe):
            pe.wait_ge(lo_ready, KQ)
            q_up.tensor(pe)
            pe.wait_ge(lo_ready, KQ + KKV)
            k_up.tensor(pe)
            v_up.tensor(pe)


def attention(nc, sem, a, t, head_in, act_t, y_t):
    loaded, roped, LOADS = head_in.loaded, head_in.roped, head_in.LOADS
    gate_loaded = [sem("gate_even_loaded"), sem("gate_odd_loaded")]
    hi_ready = sem("head_hi_ready")
    lo_ready = sem("head_lo_ready")
    score_done = sem("score_done")
    max_done = sem("max_done")
    neg_done = sem("neg_max_done")
    exp_done = sem("exp_done")
    recip_done = sem("recip_done")
    prob_done = sem("prob_done")
    turned = sem("prob_turned")
    pt_hi_ready = sem("pt_hi_ready")
    pt_lo_ready = sem("pt_lo_ready")
    pv_done = sem("pv_done")
    y_done = sem("y_done")
    stored = [sem("y_even_stored"), sem("y_odd_stored")]
    CHUNKS = [1, 1, 1, 1, 2, 2, 2, 2]
    BEFORE = [sum(CHUNKS[:i]) for i in range(NT + 1)]
    PAIRS = NT // 2
    with ExitStack() as ctx:
        sb = lambda n, shape, dt=F32: ctx.enter_context(nc.sbuf_tensor(n, shape, dt))
        pb = lambda n, shape: ctx.enter_context(nc.psum_tensor(n, shape, F32))
        q_raw, k_raw, v_raw, r_sum = head_in.q_raw, head_in.k_raw, head_in.v_raw, head_in.r_sum
        gate = sb("head_gate", [P, 2, S])
        q_hi, q_lo = sb("q_hi", [P, 2, S], F32R), sb("q_lo", [P, 2, S], F32R)
        k_hi, k_lo = sb("k_hi", [P, 2, S], F32R), sb("k_lo", [P, 2, S], F32R)
        v_hi, v_lo = sb("v_hi", [P, 2, NT, V_MLA], F32R), sb("v_lo", [P, 2, NT, V_MLA], F32R)
        q_rope = sb("q_rope", [P, 2, S], F32R)
        prob = sb("prob", [P, 4, S])
        pt_hi, pt_lo = sb("pt_hi", [P, 2, NT, 256], F32R), sb("pt_lo", [P, 2, NT, 256], F32R)
        y = sb("y_head", [P, 2, S])
        row_max, neg_max = sb("row_max", [P, 4]), sb("neg_max", [P, 4])
        row_sum, recip = sb("row_sum", [P, 4]), sb("recip", [P, 4])
        p_s = pb("p_scores", [P, 2, S])
        p_t = pb("p_turned", [P, 2, HALF])
        p_y = pb("p_y", [P, 2, HALF])
        block = ctx.enter_context(nc.Block())

        ROUNDS = H_MLA // 2

        @block.sync
        def _(sp):
            def load(it, s):
                sp.wait_ge(lo_ready, it * 8 + 4 * (s + 1))
                head_in.load_qk(sp, it * 2 + s)
                head_in.load_v(sp, it * 2 + s)

            def load_gate(it, s):
                sp.wait_ge(y_done, it * 8 + 4 * (s + 1))
                sp.dma_start(gate[:, s, :], one(act_t, it * 2 + s).rearrange("a p n -> p (a n)"))\
                    .then_inc(gate_loaded[s], 16)

            load_gate(0, 0)
            load(0, 1)
            load_gate(0, 1)
            with sp.Fori(1, ROUNDS) as it:
                for s in range(2):
                    load(it, s)
                    load_gate(it, s)

        @block.gpsimd
        def _(pool):
            def rotate(it, s):
                pool.wait_ge(loaded, it * (2 * 16 * LOADS) + 16 * LOADS * (s + 1))
                head_in.rotate_products()
                pool.wait_ge(roped, it * 6 + (3 * s + 2))
                pool.wait_ge(lo_ready, it * 8 + 4 * (s + 1))
                head_in.rotate_sum()

            rotate(0, 1)
            with pool.Fori(1, ROUNDS) as it:
                for s in range(2):
                    rotate(it, s)

        def prepare_hi(act, it, s, part):
            if part == 0:
                act.wait_ge(loaded, it * (2 * 16 * LOADS) + 16 * LOADS * (s + 1))
                act.wait_ge(pv_done, it * 8 + 4 * (s + 1))
            src, out = [(q_raw[:, :], q_hi[:, s, :]), (k_raw[:, :], k_hi[:, s, :]),
                        (r_sum[:, :], q_rope[:, s, :]), (v_raw[:, :, :], v_hi[:, s, :, :])][part]
            if part == 2:
                act.wait_ge(roped, it * 6 + 3 * (s + 1))
            nc.scalar.activation(out, src, ACT.Copy).then_inc(hi_ready, 1)

        def prepare_lo(dve, it, s, part):
            dve.wait_ge(hi_ready, it * 8 + (4 * s + part + 1))
            low = slice(64, 128)
            src, hi, out = [
                (q_raw[:, :], q_hi[:, s, :], q_lo[:, s, :]), (k_raw[:, :], k_hi[:, s, :], k_lo[:, s, :]),
                (r_sum[low, :], q_rope[low, s, :], q_rope[low, s, :]),
                (v_raw[:, :, :], v_hi[:, s, :, :], v_lo[:, s, :, :])][part]
            nc.vector.tensor_tensor(out, src, hi.bitcast(F32), ALU.subtract).then_inc(lo_ready, 1)

        STEPS = 2 * NT
        CH = 2 * BEFORE[NT]
        RP = 2 * PAIRS

        def chunks(m):
            i = m % NT
            return [(BEFORE[i] + (m // NT) * BEFORE[NT] + c, 4 * c, min(4, i + 1 - 4 * c)) for c in range(CHUNKS[i])]

        @block.scalar
        def _(act):
            for part in range(4):
                prepare_hi(act, 0, 0, part)
            for free in stored:
                act.sem_inc(free, 16)

            def store(it, s):
                act.wait_ge(y_done, it * RP + (RP + PAIRS * (s + 1)))
                act.dma_start(one(y_t, it * 2 + s).rearrange("a p n -> p (a n)"), y[:, s, :])\
                    .then_inc(stored[s], 16)

            def step(it, m, old, last):
                if old(m - 3) and m - 3 < STEPS:
                    r, b = lag(it, m - 3, STEPS)
                    pair = b // 2
                    off = (b % 2) * P
                    for c, j, count in chunks(b):
                        act.wait_ge(turned, r * CH + (c + 1))
                        if old(m - 3 - 4):
                            act.wait_ge(pv_done, r * RP + (RP + pair - 1))
                        nc.scalar.activation(pt_hi[:, pair % 2, j:j + count, off:off + P],
                                             p_t[:, c % 2, 0:count * P].rearrange("p (j n) -> p j n", n=P),
                                             ACT.Copy).then_inc(pt_hi_ready, 1)
                if m < STEPS:
                    width = (m % NT + 1) * P
                    slot = m % 4
                    act.wait_ge(neg_done, it * STEPS + (m + 1))
                    if old(m - 4):
                        r, b = lag(it, m - 4, STEPS)
                        act.wait_ge(turned, r * CH + (chunks(b)[-1][0] + 1))
                    nc.scalar.activation(prob[:, slot, 0:width], p_s[:, m % 2, 0:width], ACT.Exp,
                                         bias=neg_max[:, slot:slot + 1], scale=SCALE,
                                         accum_out=row_sum[:, slot:slot + 1]).then_inc(exp_done, 1)
                if 4 <= m % NT and m < STEPS and not (last and m >= NT):
                    prepare_hi(act, it + m // NT, 1 - m // NT, m % NT - 4)
                if m == 14:
                    store(it, 0)
                if m == 6 and old(-1):
                    store(it - 1, 1)

            pipelined(act, step, ROUNDS, STEPS, 5)
            store(ROUNDS - 1, 1)
            for free in stored:
                act.wait_ge(free, 16 + 8 * H_MLA)

        @block.vector
        def _(dve):
            dve.sem_inc(lo_ready, 4)
            dve.sem_inc(y_done, 2 * PAIRS)
            for part in range(4):
                prepare_lo(dve, 0, 0, part)

            def step(it, m, old, last):
                if old(m - 3) and m - 3 < STEPS:
                    r, b = lag(it, m - 3, STEPS)
                    pair = b // 2
                    off = (b % 2) * P
                    for c, j, count in chunks(b):
                        dve.wait_ge(pt_hi_ready, r * CH + (c + 1))
                        nc.vector.tensor_tensor(pt_lo[:, pair % 2, j:j + count, off:off + P],
                                                p_t[:, c % 2, 0:count * P].rearrange("p (j n) -> p j n", n=P),
                                                pt_hi[:, pair % 2, j:j + count, off:off + P].bitcast(F32),
                                                ALU.subtract).then_inc(pt_lo_ready, 1)
                if m < STEPS:
                    cell = slice(m % 4, m % 4 + 1)
                    dve.wait_ge(score_done, it * STEPS + (m + 1))
                    nc.vector.reduce_max(row_max[:, cell], p_s[:, m % 2, 0:(m % NT + 1) * P], AX.X)\
                        .then_inc(max_done, 1)
                    dve.wait_ge(max_done, it * STEPS + (m + 1))
                    nc.vector.tensor_scalar(neg_max[:, cell], row_max[:, cell], -SCALE, None, ALU.mult)\
                        .then_inc(neg_done, 1)
                if old(m - 1) and m - 1 < STEPS:
                    r, b = lag(it, m - 1, STEPS)
                    cell = slice(b % 4, b % 4 + 1)
                    width = (b % NT + 1) * P
                    dve.wait_ge(exp_done, r * STEPS + (b + 1))
                    nc.vector.reciprocal(recip[:, cell], row_sum[:, cell]).then_inc(recip_done, 1)
                    dve.wait_ge(recip_done, r * STEPS + (b + 1))
                    nc.vector.tensor_scalar(prob[:, b % 4, 0:width], prob[:, b % 4, 0:width], recip[:, cell],
                                            None, ALU.mult).then_inc(prob_done, 1)
                if m % 2 == 0 and old(m - 6):
                    r, pair = lag(it, (m - 6) // 2, RP)
                    s, p = divmod(pair, PAIRS)
                    dve.wait_ge(pv_done, r * RP + (RP + pair + 1))
                    if p == 0:
                        dve.wait_ge(stored[s], r * 16 + 16)
                        dve.wait_ge(gate_loaded[s], r * 16 + 16)
                    cut = slice(256 * p, 256 * p + 256)
                    nc.vector.tensor_tensor(y[:, s, cut], p_y[:, pair % 2, 0:256], gate[:, s, cut], ALU.mult)\
                        .then_inc(y_done, 1)
                if 4 <= m % NT and m < STEPS and not (last and m >= NT):
                    prepare_lo(dve, it + m // NT, 1 - m // NT, m % NT - 4)

            pipelined(dve, step, ROUNDS, STEPS, 5)

        @block.tensor
        def _(pe):
            pe.sem_inc(pv_done, 2 * PAIRS)

            def scores(it, m, old):
                s, i = divmod(m, NT)
                if i == 0:
                    pe.wait_ge(lo_ready, it * 8 + (4 + 4 * s + 3))
                if old(m - 2):
                    pe.wait_ge(exp_done, it * STEPS + (m - 1))
                q = slice(i * P, (i + 1) * P)
                for c in range(0, (i + 1) * P, HALF):
                    k = slice(c, min(c + HALF, (i + 1) * P))
                    out = p_s[:, m % 2, k]
                    diagonal = k.stop == (i + 1) * P
                    nc.tensor.matmul(out, q_hi[:, s, q], k_hi[:, s, k], start=True, stop=False)
                    nc.tensor.matmul(out, q_hi[:, s, q], k_lo[:, s, k], start=False, stop=False)
                    nc.tensor.matmul(out, q_lo[:, s, q], k_hi[:, s, k], start=False, stop=False)
                    nc.tensor.matmul(out, q_rope[:, s, q], t["k_rope_hi"][:, k], start=False, stop=False)
                    last = nc.tensor.matmul(out, q_rope[:, s, q], t["k_rope_lo"][:, k], start=False, stop=not diagonal)
                    if diagonal:
                        last = nc.tensor.matmul(p_s[:, m % 2, q], t["ident_r"][:, :], t["causal_r"][:, :],
                                                start=False, stop=True)
                last.then_inc(score_done, 1)

            def turn(it, m, old):
                pe.wait_ge(prob_done, it * STEPS + (m + 1))
                for c, j, count in chunks(m):
                    if c >= 2 or old(-1):
                        pe.wait_ge(pt_lo_ready, it * CH + (c - 1))
                    for b in range(count):
                        last = nc.tensor.transpose(p_t[:, c % 2, b * P:(b + 1) * P],
                                                   prob[:, m % 4, (j + b) * P:(j + b + 1) * P], t["ident"][:, :])
                    last.then_inc(turned, 1)

            def values(it, pair, old):
                s, p = divmod(pair, PAIRS)
                if p == 0:
                    pe.wait_ge(lo_ready, it * 8 + (4 + 4 * s + 4))
                pe.wait_ge(pt_lo_ready, it * CH + (chunks(2 * pair + 1)[-1][0] + 1))
                pe.wait_ge(y_done, it * RP + (RP + pair - 1))
                for j in range(2 * p + 2):
                    cols = slice(P if j == 2 * p + 1 else 0, 256)
                    out = p_y[:, pair % 2, cols]
                    nc.tensor.matmul(out, v_hi[:, s, j, :], pt_hi[:, pair % 2, j, cols], start=(j == 0), stop=False)
                    nc.tensor.matmul(out, v_hi[:, s, j, :], pt_lo[:, pair % 2, j, cols], start=False, stop=False)
                    last = nc.tensor.matmul(out, v_lo[:, s, j, :], pt_hi[:, pair % 2, j, cols], start=False,
                                            stop=(j == 2 * p + 1))
                last.then_inc(pv_done, 1)

            def step(it, m, old, last):
                if m < STEPS:
                    scores(it, m, old)
                if m % 2 == 1 and old(m - 5):
                    values(*lag(it, (m - 5) // 2, RP), old)
                if old(m - 2) and m - 2 < STEPS:
                    r, b = lag(it, m - 2, STEPS)
                    turn(r, b, (lambda x: False) if isinstance(r, int) and r == 0 else old)

            pipelined(pe, step, ROUNDS, STEPS, 5)


def retention(nc, sem, a, t, act_t, v_tok, y_t):
    loaded = [sem("chunk_loaded_%d" % m) for m in range(NT)]
    rotated = sem("chunk_rotated")
    added = sem("chunk_rope_added")
    decayed = sem("chunk_decayed")
    qk_hi_ready = sem("qk_hi_ready")
    qk_lo_ready = sem("qk_lo_ready")
    v_hi_ready = sem("v_hi_ready")
    v_lo_ready = sem("v_lo_ready")
    k_turned = sem("k_turned")
    k_hi_ready = sem("k_tok_hi_ready")
    k_lo_ready = sem("k_tok_lo_ready")
    inner_done = sem("inner_scores_done")
    masked = sem("inner_scores_masked")
    i_hi_ready = sem("inner_hi_ready")
    i_lo_ready = sem("inner_lo_ready")
    out_done = sem("out_done")
    state_done = sem("state_done")
    r_hi_ready = sem("state_hi_ready")
    r_lo_ready = sem("state_lo_ready")
    stats_done = sem("stats_done")
    rooted = sem("out_rooted")
    normed = sem("out_normed")
    out_turned = sem("out_turned")
    y_done = sem("chunk_y_done")
    stored = [sem("chunk_y_even_stored"), sem("chunk_y_odd_stored")]
    C = NT
    LOADED = 5 * 16
    with ExitStack() as ctx:
        sb = lambda n, shape, dt=F32: ctx.enter_context(nc.sbuf_tensor(n, shape, dt))
        pb = lambda n, shape: ctx.enter_context(nc.psum_tensor(n, shape, F32))
        x = sb("qk_raw", [P, C, 2, 2, P])
        decay = sb("decay", [P, C, 2, P])
        v_raw = sb("v_chunk", [P, C, RET_V])
        gate = sb("gate_chunk", [P, C, 4, P])
        rot = sb("rot", [P, 4, 2, 2, P])
        cross = sb("rot_cross", [P, 4, 2, 2, P])
        qk_hi, qk_lo = sb("qk_hi", [P, 4, 2, 2, P], F32R), sb("qk_lo", [P, 4, 2, 2, P], F32R)
        v_hi, v_lo = sb("vr_hi", [P, 4, RET_V], F32R), sb("vr_lo", [P, 4, RET_V], F32R)
        k_hi, k_lo = sb("k_tok_hi", [P, 4, RET_QK], F32R), sb("k_tok_lo", [P, 4, RET_QK], F32R)
        inner = sb("inner", [P, 2, P])
        i_hi, i_lo = sb("inner_hi", [P, 4, P], F32R), sb("inner_lo", [P, 4, P], F32R)
        r_hi, r_lo = sb("state_hi", [P, 2, RET_V], F32R), sb("state_lo", [P, 2, RET_V], F32R)
        out_n = sb("out_n", [P, 2, RET_V])
        y = sb("y_chunk", [P, 2, 4, P])
        stats, mean_var = sb("stats", [P, 2, 6]), sb("mean_var", [P, 2, 2])
        root, rstd, shift = sb("root_r", [P, 2]), sb("rstd_r", [P, 2]), sb("shift_r", [P, 2])
        carrier = sb("carrier", [P, 1])
        p_k = pb("p_k_tok", [P, HALF])
        p_i = pb("p_inner", [P, HALF])
        p_o = pb("p_out", [P, 2, HALF])
        p_r = pb("p_state", [P, 2, HALF])
        p_y = pb("p_y_turned", [P, 2, HALF])
        block = ctx.enter_context(nc.Block())

        def two_tiles(tile, h, m):
            return act_t[bass.ds(h * 2 + tile, 2)].rearrange("a p n -> p a n")[:, :, m * P:(m + 1) * P]

        def four_tiles(ap, tile, h, m):
            return ap[bass.ds(h * 4 + tile, 4)].rearrange("a p n -> p a n")[:, :, m * P:(m + 1) * P]

        @block.sync
        def _(sp):
            def load(h, m):
                sp.dma_start(x[:, m, 0, :, :], two_tiles(Q_RET, h, m)).then_inc(loaded[m], 16)
                sp.dma_start(x[:, m, 1, :, :], two_tiles(K_RET, h, m)).then_inc(loaded[m], 16)
                sp.dma_start(decay[:, m, :, :], one(a["decay"], h)[:, :, m * P:(m + 1) * P]
                             .rearrange("a b n -> (a b) n").partition_broadcast(P)).then_inc(loaded[m], 16)
                sp.dma_start(v_raw[:, m, :], one(v_tok, h).rearrange("a p t n -> p (a t) n")[:, m, :])\
                    .then_inc(loaded[m], 16)
                sp.dma_start(gate[:, m, :, :], four_tiles(act_t, GATE_RET, h, m)).then_inc(loaded[m], 16)

            def body(h, is_last):
                for m in range(C):
                    sp.wait_ge(y_done, h * C + (m + 1))
                    sp.dma_start(four_tiles(y_t, 0, h, m), y[:, m % 2, :, :]).then_inc(stored[m % 2], 16)
                    if not is_last:
                        load(h + 1, m)

            for free in stored:
                sp.sem_inc(free, 16)
            for m in range(C):
                load(0, m)
            with sp.Fori(0, H_RET - 1) as h:
                body(h, False)
            body(H_RET - 1, True)
            for free in stored:
                sp.wait_ge(free, 16 + 8 * H_RET * C)

        @block.gpsimd
        def _(pool):
            def step(h, m, old, last):
                if m < C:
                    s = m % 4
                    tok = slice(m * P, (m + 1) * P)
                    pool.wait_ge(loaded[m], h * LOADED + LOADED)
                    if old(m - 4):
                        pool.wait_ge(k_turned, h * C + (m - 3))
                    nc.gpsimd.tensor_tensor(
                        rot[:, s, :, :, :].rearrange("p a b n -> p (a b) n"),
                        x[:, m, :, :, :].rearrange("p a b n -> p (a b) n"),
                        t["cos_ret"][:, tok].unsqueeze(1).broadcast_to([P, 4, P]), ALU.mult).then_inc(rotated, 1)
                    for b in range(2):
                        nc.gpsimd.tensor_tensor(
                            cross[:, s, :, b, :], x[:, m, :, 1 - b, :],
                            t["sin_ret"][:, b, tok].unsqueeze(1).broadcast_to([P, 2, P]), ALU.mult)\
                            .then_inc(rotated, 1)
                if old(m - 2) and m - 2 < C:
                    g, b = lag(h, m - 2, C)
                    pool.wait_ge(v_hi_ready, g * C + (b + 1))
                    nc.gpsimd.tensor_tensor(v_lo[:, b % 4, :], v_raw[:, b, :], v_hi[:, b % 4, :].bitcast(F32),
                                            ALU.subtract).then_inc(v_lo_ready, 1)

            pipelined(pool, step, H_RET, C, 2)

        @block.scalar
        def _(act):
            def step(h, m, old, last):
                if old(m - 4) and m - 4 < C:
                    g, b = lag(h, m - 4, C)
                    s = b % 2
                    cell = slice(s, s + 1)
                    if b < C - 1:
                        act.wait_ge(state_done, g * (C - 1) + (b + 1))
                        for half in range(2):
                            nc.scalar.activation(r_hi[:, half, :], p_r[:, half, :], ACT.Copy).then_inc(r_hi_ready, 1)
                    act.wait_ge(stats_done, g * (4 * C) + (4 * b + 2))
                    nc.scalar.activation(root[:, cell], mean_var[:, s, 1:2], ACT.Sqrt,
                                         bias=t["consts"][:, CC_EPS:CC_EPS + 1]).then_inc(rooted, 1)
                    act.wait_ge(stats_done, g * (4 * C) + (4 * b + 4))
                    nc.scalar.activation(out_n[:, s, :], p_o[:, s, :], ACT.Identity, scale=rstd[:, cell],
                                         bias=shift[:, cell]).then_inc(normed, 1)
                if old(m - 2) and m - 2 < C:
                    g, b = lag(h, m - 2, C)
                    act.wait_ge(k_turned, g * C + (b + 1))
                    nc.scalar.activation(k_hi[:, b % 4, :], p_k[:, 0:RET_QK], ACT.Copy).then_inc(k_hi_ready, 1)
                    act.wait_ge(masked, g * C + (b + 1))
                    nc.scalar.activation(i_hi[:, b % 4, :], inner[:, b % 2, :], ACT.Copy).then_inc(i_hi_ready, 1)
                if m < C:
                    act.wait_ge(loaded[m], h * LOADED + LOADED)
                    nc.scalar.activation(v_hi[:, m % 4, :], v_raw[:, m, :], ACT.Copy).then_inc(v_hi_ready, 1)
                    act.wait_ge(decayed, h * C + (m + 1))
                    nc.scalar.activation(qk_hi[:, m % 4, :, :, :], rot[:, m % 4, :, :, :], ACT.Copy)\
                        .then_inc(qk_hi_ready, 1)

            pipelined(act, step, H_RET, C, 4)

        @block.vector
        def _(dve):
            def step(h, m, old, last):
                if old(m - 3) and m - 3 < C:
                    g, b = lag(h, m - 3, C)
                    dve.wait_ge(i_hi_ready, g * C + (b + 1))
                    nc.vector.tensor_tensor(i_lo[:, b % 4, :], inner[:, b % 2, :], i_hi[:, b % 4, :].bitcast(F32),
                                            ALU.subtract).then_inc(i_lo_ready, 1)
                if old(m - 1) and m - 1 < C:
                    g, b = lag(h, m - 1, C)
                    dve.wait_ge(qk_hi_ready, g * C + (b + 1))
                    nc.vector.tensor_tensor(qk_lo[:, b % 4, :, :, :], rot[:, b % 4, :, :, :],
                                            qk_hi[:, b % 4, :, :, :].bitcast(F32), ALU.subtract).then_inc(qk_lo_ready, 1)
                if old(m - 6) and m - 6 < C:
                    g, b = lag(h, m - 6, C)
                    dve.wait_ge(out_turned, g * C + (b + 1))
                    dve.wait_ge(loaded[b], g * LOADED + LOADED)
                    dve.wait_ge(stored[b % 2], g * (8 * C) + 16 * (b // 2 + 1))
                    nc.vector.tensor_tensor(y[:, b % 2, :, :], p_y[:, b % 2, :].rearrange("p (a n) -> p a n", n=P),
                                            gate[:, b, :, :], ALU.mult).then_inc(y_done, 1)
                if m < C:
                    s = m % 4
                    dve.wait_ge(rotated, h * (3 * C) + 3 * (m + 1))
                    nc.vector.tensor_tensor(rot[:, s, :, :, :], rot[:, s, :, :, :], cross[:, s, :, :, :], ALU.add)\
                        .then_inc(added, 1)
                    dve.wait_ge(added, h * C + (m + 1))
                    nc.vector.tensor_tensor(rot[:, s, :, :, :], rot[:, s, :, :, :],
                                            decay[:, m, :, :].unsqueeze(2).broadcast_to([P, 2, 2, P]),
                                            ALU.mult).then_inc(decayed, 1)
                if old(m - 4) and m - 4 < C:
                    g, b = lag(h, m - 4, C)
                    s = b % 2
                    cell = slice(s, s + 1)
                    dve.wait_ge(out_done, g * C + (b + 1))
                    nc.vector.bn_stats(stats[:, s, :], p_o[:, s, :]).then_inc(stats_done, 1)
                    dve.wait_ge(stats_done, g * (4 * C) + (4 * b + 1))
                    nc.vector.memset(carrier[:, :], 0.0)
                    nc.vector.bn_aggr(mean_var[:, s, :], stats[:, s, :]).then_inc(stats_done, 1)
                    if b < C - 1:
                        for half in range(2):
                            dve.wait_ge(r_hi_ready, g * (2 * (C - 1)) + (2 * b + half + 1))
                            nc.vector.tensor_tensor(r_lo[:, half, :], p_r[:, half, :], r_hi[:, half, :].bitcast(F32),
                                                    ALU.subtract).then_inc(r_lo_ready, 1)
                    dve.wait_ge(rooted, g * C + (b + 1))
                    nc.vector.reciprocal(rstd[:, cell], root[:, cell]).then_inc(stats_done, 1)
                    dve.wait_ge(stats_done, g * (4 * C) + (4 * b + 3))
                    nc.vector.tensor_scalar(shift[:, cell], mean_var[:, s, 0:1], -1.0, rstd[:, cell],
                                            ALU.mult, ALU.mult).then_inc(stats_done, 1)
                if old(m - 2) and m - 2 < C:
                    g, b = lag(h, m - 2, C)
                    dve.wait_ge(inner_done, g * C + (b + 1))
                    nc.vector.tensor_tensor(inner[:, b % 2, :], p_i[:, 0:P], t["causal_kq"][:, :], ALU.mult)\
                        .then_inc(masked, 1)
                    dve.wait_ge(k_hi_ready, g * C + (b + 1))
                    nc.vector.tensor_tensor(k_lo[:, b % 4, :], p_k[:, 0:RET_QK], k_hi[:, b % 4, :].bitcast(F32),
                                            ALU.subtract).then_inc(k_lo_ready, 1)

            pipelined(dve, step, H_RET, C, 6)

        @block.tensor
        def _(pe):
            def outputs(h, m, old):
                s = m % 4
                pe.wait_ge(v_lo_ready, h * C + (m + 1))
                pe.wait_ge(i_lo_ready, h * C + (m + 1))
                if old:
                    pe.wait_ge(normed, h * C + (m - 1))
                out = p_o[:, m % 2, :]
                nc.tensor.matmul(out, i_hi[:, s, :], v_hi[:, s, :], start=True, stop=False)
                nc.tensor.matmul(out, i_hi[:, s, :], v_lo[:, s, :], start=False, stop=False)
                last = nc.tensor.matmul(out, i_lo[:, s, :], v_hi[:, s, :], start=False, stop=(m == 0))
                if m:
                    for b in range(2):
                        pe.wait_ge(r_lo_ready, h * (2 * (C - 1)) + (2 * (m - 1) + b + 1))
                        nc.tensor.matmul(out, qk_hi[:, s, 0, b, :], r_hi[:, b, :], start=False, stop=False)
                        nc.tensor.matmul(out, qk_lo[:, s, 0, b, :], r_hi[:, b, :], start=False, stop=False)
                        last = nc.tensor.matmul(out, qk_hi[:, s, 0, b, :], r_lo[:, b, :], start=False, stop=(b == 1))
                last.then_inc(out_done, 1)
                if m == C - 1:
                    return
                pe.wait_ge(k_lo_ready, h * C + (m + 1))
                for b in range(2):
                    cut = slice(b * P, (b + 1) * P)
                    out = p_r[:, b, :]
                    nc.tensor.matmul(out, k_hi[:, s, cut], v_hi[:, s, :], start=(m == 0), stop=False,
                                     skip_group_check=True)
                    nc.tensor.matmul(out, k_hi[:, s, cut], v_lo[:, s, :], start=False, stop=False,
                                     skip_group_check=True)
                    last = nc.tensor.matmul(out, k_lo[:, s, cut], v_hi[:, s, :], start=False, stop=True,
                                            skip_group_check=True)
                last.then_inc(state_done, 1)

            def inner_scores(h, m, old):
                s = m % 4
                pe.wait_ge(qk_lo_ready, h * C + (m + 1))
                if old:
                    pe.wait_ge(k_lo_ready, h * C + m)
                for b in range(2):
                    last = nc.tensor.transpose(p_k[:, b * P:(b + 1) * P], rot[:, s, 1, b, :], t["ident"][:, :])
                last.then_inc(k_turned, 1)
                if old:
                    pe.wait_ge(masked, h * C + m)
                for b in range(2):
                    out = p_i[:, 0:P]
                    nc.tensor.matmul(out, qk_hi[:, s, 1, b, :], qk_hi[:, s, 0, b, :], start=(b == 0), stop=False)
                    nc.tensor.matmul(out, qk_hi[:, s, 1, b, :], qk_lo[:, s, 0, b, :], start=False, stop=False)
                    last = nc.tensor.matmul(out, qk_lo[:, s, 1, b, :], qk_hi[:, s, 0, b, :], start=False,
                                            stop=(b == 1))
                last.then_inc(inner_done, 1)

            def step(h, m, old, last):
                if old(m - 4) and m - 4 < C:
                    outputs(*lag(h, m - 4, C), old(m - 6))
                if old(m - 2) and m - 2 < C:
                    inner_scores(*lag(h, m - 2, C), old(m - 3))
                if old(m - 5) and m - 5 < C:
                    g, b = lag(h, m - 5, C)
                    pe.wait_ge(normed, g * C + (b + 1))
                    if old(m - 7):
                        pe.wait_ge(y_done, g * C + (b - 1))
                    for j in range(4):
                        ins = nc.tensor.transpose(p_y[:, b % 2, j * P:(j + 1) * P],
                                                  out_n[:, b % 2, j * P:(j + 1) * P], t["ident"][:, :])
                    ins.then_inc(out_turned, 1)

            pipelined(pe, step, H_RET, C, 5)


def merge(nc, sem, a, t, weights, y_mla, y_ret, act_t, merged):
    y_loaded = [sem("y_tile_loaded_%d" % i) for i in range(4)]
    y_hi_ready = sem("y_hi_ready")
    y_lo_ready = sem("y_lo_ready")
    loaded = sem("proj_w_loaded")
    hi_ready = sem("proj_w_hi_ready")
    lo_ready = sem("proj_w_lo_ready")
    summed = sem("proj_summed")
    gate_loaded = [sem("merge_gate_even_loaded"), sem("merge_gate_odd_loaded")]
    step = sem("merge_step")
    psum_free = sem("proj_psum_free")
    SETS, RING, PAIRS = 3, 14, KD // 2
    AHEAD = RING - KD
    with ExitStack() as ctx:
        sb = lambda n, shape, dt=F32: ctx.enter_context(nc.sbuf_tensor(n, shape, dt))
        y_raw = sb("y_raw", [P, 4, S])
        y_hi, y_lo = sb("y_hi", [P, RING, S], F32R), sb("y_lo", [P, RING, S], F32R)
        raw = sb("proj_raw", [P, KD, 2 * P])
        w_hi, w_lo = sb("proj_hi", [P, KD, 2 * P], F32R), sb("proj_lo", [P, KD, 2 * P], F32R)
        gate = sb("merge_gate", [P, 2, S])
        psum = ctx.enter_context(nc.psum_tensor("p_proj", [P, 4, S], F32))
        block = ctx.enter_context(nc.Block())

        def gain(i):
            return t["cols"][:, COL_GRET + i:COL_GRET + i + 1] if i < 2 * KD else None

        @block.gpsimd
        def _(pool):
            for i in range(SETS * KD):
                if i >= 4:
                    pool.wait_ge(y_lo_ready, i - 3)
                src = y_ret[i] if i < 2 * KD else y_mla[i - 2 * KD]
                pool.dma_start(y_raw[:, i % 4, :], src).then_inc(y_loaded[i % 4], 16)

        @block.sync
        def _(sp):
            sp.dma_start(raw[:, :, :], weights[0]).then_inc(loaded, 16)
            for z in range(SETS):
                def body(g, is_last):
                    if z:
                        for j in range(2):
                            sp.wait_ge(psum_free, g * 2 + (z * KD + j + 1))
                            sp.dma_start(gate[:, j, :], one(act_t, g * 2 + (j + (MERGE_RET if z == 1 else MERGE_MLA)))
                                         .rearrange("a p n -> p (a n)")).then_inc(gate_loaded[j], 16)
                    if not is_last or z < SETS - 1:
                        sp.wait_ge(lo_ready, g * 2 + (2 * PAIRS * z + 2))
                        sp.dma_start(raw[:, :, :], one(weights, g + (z * PAIRS + 1))
                                     .rearrange("a p k n -> p (a k) n")).then_inc(loaded, 16)

                with sp.Fori(0, PAIRS - 1) as g:
                    body(g, False)
                body(PAIRS - 1, True)

        @block.scalar
        def _(act):
            def split_y(i):
                act.wait_ge(y_loaded[i % 4], 16 * (i // 4 + 1))
                scale = gain(i)
                nc.scalar.activation(y_hi[:, i % RING, :], y_raw[:, i % 4, :], ACT.Copy,
                                     scale=1.0 if scale is None else scale).then_inc(y_hi_ready, 1)

            def split_w(z, g, j, first=False):
                if not first:
                    act.wait_ge(summed, g * 2 + (z * KD + j + 1))
                    if j == 0:
                        act.wait_ge(loaded, g * 16 + 16 * (z * PAIRS + 2))
                cut = slice(j * P, (j + 1) * P)
                nc.scalar.activation(w_hi[:, :, cut], raw[:, :, cut], ACT.Copy).then_inc(hi_ready, 1)

            act.wait_ge(loaded, 16)
            for j in range(2):
                split_w(0, 0, j, first=True)
            for k in range(KD):
                split_y(k)
            for z in range(SETS):
                with act.Fori(0, PAIRS - 1) as g:
                    for j in range(2):
                        split_w(z, g, j)
                if z < SETS - 1:
                    for k in range(AHEAD):
                        split_y((z + 1) * KD + k)
                    for j in range(2):
                        split_w(z, PAIRS - 1, j)
                    for k in range(AHEAD, KD):
                        split_y((z + 1) * KD + k)

        @block.vector
        def _(dve):
            def low_y(i):
                dve.wait_ge(y_hi_ready, i + 1)
                slot = i % RING
                if gain(i) is None:
                    ins = nc.vector.tensor_tensor(y_lo[:, slot, :], y_raw[:, i % 4, :],
                                                  y_hi[:, slot, :].bitcast(F32), ALU.subtract)
                else:
                    ins = nc.vector.scalar_tensor_tensor(out=y_lo[:, slot, :], in0=y_raw[:, i % 4, :], scalar=gain(i),
                                                         in1=y_hi[:, slot, :].bitcast(F32), op0=ALU.mult,
                                                         op1=ALU.subtract)
                ins.then_inc(y_lo_ready, 1)

            def low_w(z, g, j, ahead=1):
                dve.wait_ge(hi_ready, g * 2 + (2 * PAIRS * z + 2 * ahead + j + 1))
                cut = slice(j * P, (j + 1) * P)
                nc.vector.tensor_tensor(w_lo[:, :, cut], raw[:, :, cut], w_hi[:, :, cut].bitcast(F32),
                                        ALU.subtract).then_inc(lo_ready, 1)

            def evacuate(z, g, j):
                out = merged[:, bass.ds(g * 2 + j, 1), :].rearrange("p a n -> p (a n)")
                dve.wait_ge(summed, g * 2 + (z * KD + j + 1))
                tile = psum[:, z % 2 * 2 + j, :]
                if z == 0:
                    nc.vector.tensor_copy(out, tile).then_inc(psum_free, 1)
                    return
                dve.wait_ge(gate_loaded[j], g * 16 + 16 * ((z - 1) * PAIRS + 1))
                if z == 1:
                    nc.vector.tensor_tensor(out, tile, out, ALU.add).then_inc(step, 1)
                    dve.wait_ge(step, g * 2 + ((z - 1) * KD + j + 1))
                    nc.vector.tensor_tensor(out, out, gate[:, j, :], ALU.mult).then_inc(psum_free, 1)
                else:
                    nc.vector.tensor_tensor(gate[:, j, :], tile, gate[:, j, :], ALU.mult).then_inc(step, 1)
                    dve.wait_ge(step, g * 2 + ((z - 1) * KD + j + 1))
                    nc.vector.tensor_tensor(out, gate[:, j, :], out, ALU.add).then_inc(psum_free, 1)

            dve.sem_inc(psum_free, 2)
            for j in range(2):
                low_w(0, 0, j, ahead=0)
            for k in range(KD):
                low_y(k)
            for z in range(SETS):
                with dve.Fori(0, PAIRS - 1) as g:
                    for j in range(2):
                        evacuate(z, g, j)
                        low_w(z, g, j)
                if z < SETS - 1:
                    for k in range(AHEAD):
                        low_y((z + 1) * KD + k)
                for j in range(2):
                    if z < SETS - 1:
                        low_w(z, PAIRS - 1, j)
                    evacuate(z, PAIRS - 1, j)
                if z < SETS - 1:
                    for k in range(AHEAD, KD):
                        low_y((z + 1) * KD + k)

        @block.tensor
        def _(pe):
            def products(z, j, k, half):
                cut = slice(j * P, (j + 1) * P)
                tok = slice(half * HALF, (half + 1) * HALF)
                out = psum[:, z % 2 * 2 + j, tok]
                slot = (z * KD + k) % RING
                nc.tensor.matmul(out, w_hi[:, k, cut], y_hi[:, slot, tok], start=(k == 0), stop=False)
                nc.tensor.matmul(out, w_hi[:, k, cut], y_lo[:, slot, tok], start=False, stop=False)
                return nc.tensor.matmul(out, w_lo[:, k, cut], y_hi[:, slot, tok], start=False, stop=(k == KD - 1))

            def first_tiles(z, tiles):
                for j in tiles:
                    pe.wait_ge(lo_ready, 2 * PAIRS * z + j + 1)
                if z:
                    pe.wait_ge(psum_free, 2 + (z - 1) * KD)
                for k in range(KD):
                    pe.wait_ge(y_lo_ready, z * KD + k + 1)
                    for j in tiles:
                        for half in range(2):
                            last = products(z, j, k, half)
                        if k == KD - 1:
                            last.then_inc(summed, 1)

            def tile(z, g, j):
                pe.wait_ge(lo_ready, g * 2 + (2 * PAIRS * z + j + 1))
                pe.wait_ge(psum_free, g * 2 + (z * KD + j + 1))
                for half in range(2):
                    for k in range(KD):
                        last = products(z, j, k, half)
                last.then_inc(summed, 1)

            for z in range(SETS):
                first_tiles(z, [0] if z else [0, 1])
                if z:
                    tile(z, 0, 1)
                with pe.Fori(1, PAIRS) as g:
                    for j in range(2):
                        tile(z, g, j)


def output(nc, sem, a, t, w_out, merged, out):
    w_loaded = [sem("out_w_even_loaded"), sem("out_w_odd_loaded")]
    x_loaded = [sem("residual_even_loaded"), sem("residual_odd_loaded")]
    m_hi_ready = sem("merged_hi_ready")
    m_lo_ready = sem("merged_lo_ready")
    w_hi_ready = sem("out_w_hi_ready")
    w_lo_ready = sem("out_w_lo_ready")
    summed = sem("out_summed")
    gated = sem("out_gated")
    added = sem("out_added")
    squared = sem("out_squared")
    meaned = sem("out_meaned")
    rooted = sem("out_root_ready")
    inverted = sem("out_inverted")
    finished = sem("out_finished")
    stored = [sem("out_even_stored"), sem("out_odd_stored")]
    with ExitStack() as ctx:
        sb = lambda n, shape, dt=F32: ctx.enter_context(nc.sbuf_tensor(n, shape, dt))
        m_hi, m_lo = sb("m_hi", [P, KD, S], F32R), sb("m_lo", [P, KD, S], F32R)
        w_raw = sb("out_raw", [P, 2, D])
        w_hi, w_lo = sb("out_hi", [P, KD, D], F32R), sb("out_lo", [P, KD, D], F32R)
        x = sb("residual", [P, 2, D])
        y = sb("out_y", [P, 2, D])
        ss, root, rstd = sb("out_ss", [P, 2]), sb("out_root", [P, 2]), sb("out_rstd", [P, 2])
        psum = ctx.enter_context(nc.psum_tensor("p_final", [P, 4, D], F32))
        block = ctx.enter_context(nc.Block())

        @block.sync
        def _(sp):
            for k in range(KD):
                if k >= 2:
                    sp.wait_ge(w_lo_ready, k - 1)
                sp.dma_start(w_raw[:, k % 2, :], w_out[k]).then_inc(w_loaded[k % 2], 16)
            for n in range(NT):
                if n >= 2:
                    sp.wait_ge(stored[n % 2], 16 * (n // 2))
                sp.dma_start(x[:, n % 2, :], a["x"][n]).then_inc(x_loaded[n % 2], 16)

        @block.gpsimd
        def _(pool):
            for n in range(NT):
                pool.wait_ge(finished, n + 1)
                pool.dma_start(out[n * P:(n + 1) * P, :], x[:, n % 2, :]).then_inc(stored[n % 2], 16)
            for done in stored:
                pool.wait_ge(done, 8 * NT)

        @block.scalar
        def _(act):
            for k in range(KD):
                nc.scalar.activation(m_hi[:, k, :], merged[:, k, :], ACT.Copy).then_inc(m_hi_ready, 1)
                act.wait_ge(w_loaded[k % 2], 16 * (k // 2 + 1))
                nc.scalar.activation(w_hi[:, k, :], w_raw[:, k % 2, :], ACT.Copy).then_inc(w_hi_ready, 1)
            for n in range(NT):
                s = n % 2
                act.wait_ge(added, n + 1)
                nc.scalar.activation(psum[:, n % 4, :], y[:, s, :], ACT.Square, accum_out=ss[:, s:s + 1])\
                    .then_inc(squared, 1)
                act.wait_ge(meaned, n + 1)
                nc.scalar.activation(root[:, s:s + 1], ss[:, s:s + 1], ACT.Sqrt).then_inc(rooted, 1)

        @block.vector
        def _(dve):
            for k in range(KD):
                dve.wait_ge(m_hi_ready, k + 1)
                nc.vector.tensor_tensor(m_lo[:, k, :], merged[:, k, :], m_hi[:, k, :].bitcast(F32),
                                        ALU.subtract).then_inc(m_lo_ready, 1)
                dve.wait_ge(w_hi_ready, k + 1)
                nc.vector.tensor_tensor(w_lo[:, k, :], w_raw[:, k % 2, :], w_hi[:, k, :].bitcast(F32),
                                        ALU.subtract).then_inc(w_lo_ready, 1)
            for n in range(NT):
                s = n % 2
                dve.wait_ge(summed, n + 1)
                nc.vector.tensor_tensor(y[:, s, :], psum[:, n % 4, :], t["gate"][:, :], ALU.mult).then_inc(gated, 1)
                dve.wait_ge(gated, n + 1)
                dve.wait_ge(x_loaded[s], 16 * (n // 2 + 1))
                nc.vector.tensor_tensor(y[:, s, :], y[:, s, :], x[:, s, :], ALU.add).then_inc(added, 1)
                dve.wait_ge(squared, n + 1)
                nc.vector.tensor_scalar(ss[:, s:s + 1], ss[:, s:s + 1], 1.0 / D, EPS, ALU.mult, ALU.add)\
                    .then_inc(meaned, 1)
                dve.wait_ge(rooted, n + 1)
                nc.vector.reciprocal(rstd[:, s:s + 1], root[:, s:s + 1]).then_inc(inverted, 1)
                dve.wait_ge(inverted, n + 1)
                nc.vector.scalar_tensor_tensor(out=x[:, s, :], in0=y[:, s, :], scalar=rstd[:, s:s + 1],
                                               in1=t["g_final"][:, :], op0=ALU.mult, op1=ALU.mult).then_inc(finished, 1)

        @block.tensor
        def _(pe):
            def products(n, k, half):
                tok = slice(n * P, (n + 1) * P)
                cut = slice(half * HALF, (half + 1) * HALF)
                res = psum[:, n % 4, cut]
                nc.tensor.matmul(res, m_hi[:, k, tok], w_hi[:, k, cut], start=(k == 0), stop=False)
                nc.tensor.matmul(res, m_hi[:, k, tok], w_lo[:, k, cut], start=False, stop=False)
                return nc.tensor.matmul(res, m_lo[:, k, tok], w_hi[:, k, cut], start=False, stop=(k == KD - 1))

            for k in range(KD):
                pe.wait_ge(m_lo_ready, k + 1)
                pe.wait_ge(w_lo_ready, k + 1)
                for n in range(2):
                    for half in range(2):
                        last = products(n, k, half)
                    if k == KD - 1:
                        last.then_inc(summed, 1)
            for n in range(2, NT):
                if n >= 4:
                    pe.wait_ge(rooted, n - 3)
                for half in range(2):
                    for k in range(KD):
                        last = products(n, k, half)
                last.then_inc(summed, 1)


def build(nc, a, out):
    with ExitStack() as ctx:
        def sem(name):
            return ctx.enter_context(nc.semaphore(name))

        def sb(name, shape, dt=F32, where=ctx):
            return where.enter_context(nc.sbuf_tensor(name, shape, dt))

        def scratch(name, shape):
            return nc.dram_tensor(name, shape, F32, kind="Internal").ap()

        products = ProductSemaphores(sem)
        act_t = scratch("act_t", (ACT_TILES, P, S))
        v_ret = scratch("v_ret", (H_RET, P, NT, RET_V))
        q_t = scratch("q_t", (12, P, S))
        k_t = scratch("k_t", (H_MLA, P, S))
        v_mla = scratch("v_mla", (H_MLA, P, NT, V_MLA))
        y_mla = scratch("y_mla", (H_MLA, P, S))
        y_ret = scratch("y_ret", (H_RET * 4, P, S))

        t = {
            "cols": sb("cols", [P, N_COLS]), "consts": sb("consts", [P, 8]), "ones": sb("ones", [P, P]),
            "ident": sb("ident", [P, P]), "ident_r": sb("ident_r", [P, P], F32R),
            "causal_r": sb("causal_r", [P, P], F32R), "causal_kq": sb("causal_kq", [P, P]),
            "gate": sb("gate", [P, D]), "g_final": sb("g_final", [P, D]),
        }
        with ExitStack() as tables:
            t["cos_ret"] = sb("cos_ret", [P, S], where=tables)
            t["sin_ret"] = sb("sin_ret", [P, 2, S], where=tables)
            t["cos_mla"] = sb("cos_mla", [P, S], where=tables)
            t["sin_mla"] = sb("sin_mla", [P, S], where=tables)
            t["k_rope_hi"] = sb("k_rope_hi", [P, S], F32R, where=tables)
            t["k_rope_lo"] = sb("k_rope_lo", [P, S], F32R, where=tables)
            q_rope_t = q_t[8:12].rearrange("a (b p) n -> (a b) p n", b=2)
            with ExitStack() as latents:
                latent = sb("latent", [P, 6, S], where=latents)
                with ExitStack() as hidden:
                    t["h_hi"] = sb("h_hi", [P, KD, S], F32R, where=hidden)
                    t["h_lo"] = sb("h_lo", [P, KD, S], F32R, where=hidden)
                    raw = sb("w_raw", [P, KD, HALF], where=hidden)
                    condition(nc, sem, products, a, t, latent, raw)
                    project(nc, sem, products, a, t, latent, raw, act_t, v_ret)
                heads = latents.enter_context(ExitStack())
                head_in = HeadInputs(nc, sem, lambda name, shape: sb(name, shape, where=heads), t,
                                     q_t, q_rope_t, k_t, v_mla)
                project_latents(nc, sem, products, a, t, latent, q_t, k_t, v_mla, head_in)
                attention(nc, sem, a, t, head_in, act_t, y_mla)
            retention(nc, sem, a, t, act_t, v_ret, y_ret)
        merged = sb("merged", [P, KD, S])
        merge(nc, sem, a, t, a["w_proj"], y_mla, y_ret, act_t, merged)
        output(nc, sem, a, t, a["w_out"], merged, out)


def shape_constants():
    consts = np.zeros((P, 8), np.float32)
    f = np.arange(P)
    consts[:, CC_FREQ_RET] = 10000.0 ** (-(2.0 * f) / RET_QK)
    consts[:, CC_FREQ_MLA] = 10000.0 ** (-(2.0 * (f % 32)) / ROPE)
    consts[:, CC_SIGN] = np.where(f % 64 < 32, -1.0, 1.0)
    consts[:, CC_HALF_PI] = np.pi / 2
    consts[:, CC_EPS] = EPS
    log_gamma = np.log1p(-np.exp2(-5.0 - np.arange(H_RET)))[:, None]
    token = np.arange(S)[None, :] + 1.0
    decay = np.stack([np.exp(log_gamma * token), np.exp(-log_gamma * token) * RET_QK ** -0.5], axis=1)
    later = f[None, :] > f[:, None]
    return {
        "consts": consts, "decay": decay.astype(np.float32), "ident": np.eye(P, dtype=np.float32),
        "causal_add": np.where(later, MASKED, 0.0).astype(np.float32),
        "causal_kq": (f[:, None] <= f[None, :]).astype(np.float32),
    }


def kernel(**inputs):
    import concourse.bacc as bacc
    from concourse.bass_utils import run_bass_kernel_spmd

    def groups(w, cols):
        k, n = w.shape
        return np.ascontiguousarray(w.reshape(k // P, P, n // cols, cols).transpose(2, 1, 0, 3))

    def columns(v):
        return v.reshape(-1, P).T

    w_in = inputs["w_in"][0]
    w_q = inputs["w_q_up"][0].reshape(Q_RANK, H_MLA, NOPE + ROPE)
    w_kv = inputs["w_kv_up"][0].reshape(KV_RANK, H_MLA, NOPE + V_MLA)
    b_ada = inputs["b_ada"][0]
    w_ret = inputs["w_proj_ret"][0]
    k_pe = w_in[:, 640:704]
    arrays = {
        "x": inputs["x"][0].reshape(NT, P, D),
        "positions": inputs["positions"][0],
        "cols": np.ascontiguousarray(np.concatenate([
            columns(inputs["c"][0]), columns(b_ada[:2 * D]), columns(inputs["g_pre"][0]), columns(inputs["g_q"][0]),
            columns(inputs["g_kv"][0]), columns(inputs["g_ret"][0])], axis=1)),
        "b_gate": b_ada[2 * D:],
        "g_final": inputs["g_final"],
        "w_ada": groups(inputs["w_ada"][0], HALF),
        "w_latent": groups(np.concatenate([w_in[:, :640], k_pe, k_pe], axis=1), 2 * P),
        "w_act": groups(np.concatenate([w_in[:, 704:3776], w_in[:, 5824:]], axis=1), HALF),
        "w_v": groups(w_in[:, 3776:5824], HALF),
        "w_q_up": groups(np.concatenate([w_q[:, :, :NOPE].reshape(Q_RANK, -1), w_q[:, :, NOPE:].reshape(Q_RANK, -1)],
                                        axis=1), HALF),
        "w_k_up": groups(w_kv[:, :, :NOPE].reshape(KV_RANK, -1), HALF),
        "w_v_up": groups(w_kv[:, :, NOPE:].reshape(KV_RANK, -1), HALF),
        "w_proj": np.concatenate([groups(w_ret[:D], 2 * P), groups(w_ret[D:], 2 * P),
                                  groups(inputs["w_proj_mla"][0], 2 * P)]),
        "w_out": inputs["w_out"][0].reshape(KD, P, D),
    }
    nc = bacc.Bacc("TRN2", target_bir_lowering=False, num_devices=1)
    aps = {}
    for name, value in arrays.items():
        value = arrays[name] = np.ascontiguousarray(value)
        aps[name] = nc.dram_tensor("in_" + name, value.shape, mybir.dt.from_np(value.dtype), kind="ExternalInput").ap()
    for name, value in shape_constants().items():
        made = nc.inline_tensor(value, name="const_" + name)
        aps[name] = made.ap() if not isinstance(made, bass.AP) else made
    out = nc.dram_tensor("out", (S, D), F32, kind="ExternalOutput").ap()
    build(nc, aps, out)
    result = run_bass_kernel_spmd(nc, [{"in_" + k: v for k, v in arrays.items()}], core_ids=[0])
    return result.results[0]["out"].reshape(1, S, D)
```
